# Optimizing a Trainium2 kernel written in Bass

```python
import jax, jax.numpy as jnp
from jax import lax
import numpy as np

D_MODEL = 1024
BATCH = 1
SEQ = 512
DEPTH = 2
DEC_BATCH = 8
DEC_SEQ = 16
PAST_LEN = 512

CHUNK = 64
QBLOCK = 128
N_A = DEPTH // 2
N_B = DEPTH - N_A
H_A = 4
DK_A = D_MODEL // 2 // H_A
DV_A = D_MODEL // H_A
KD_A = H_A * DK_A
VD_A = H_A * DV_A
GATE_RANK = 16
GATE_TAU = 16.0
IN_A = 2 * KD_A + 2 * VD_A + GATE_RANK
H_B = 8
NOPE = 128
ROPE = 64
V_B = D_MODEL // H_B
VD_B = H_B * V_B
Q_LORA = 384
KV_LORA = 256
IN_B = Q_LORA + VD_B
ROPE_BASE = 10000.0
EPS = 1e-6

kernel_name = "yoco_gla_mla_streaming_step"

def rmsnorm(x, g):
    xf = x.astype(jnp.float32)
    y = xf * lax.rsqrt(jnp.mean(xf * xf, axis=-1, keepdims=True) + EPS)
    return (y * g.astype(jnp.float32)).astype(x.dtype)

def rope(x, pos):
    half = ROPE // 2
    inv = jnp.power(ROPE_BASE, -jnp.arange(half, dtype=jnp.float32) / half)
    ang = pos.astype(jnp.float32)[:, None] * inv[None, :]
    shp = (1, pos.shape[0]) + (1,) * (x.ndim - 3) + (half,)
    cos = jnp.cos(ang).reshape(shp)
    sin = jnp.sin(ang).reshape(shp)
    xf = x.astype(jnp.float32)
    x1, x2 = xf[..., :half], xf[..., half:]
    return jnp.concatenate([x1 * cos - x2 * sin, x2 * cos + x1 * sin], axis=-1).astype(x.dtype)

def gla_chunk_step(S, blk):
    q, k, v, g = blk
    C = q.shape[2]
    b = jnp.cumsum(g, axis=2)
    b_last = b[:, :, -1:, :]
    qe = q * jnp.exp(b)
    scores = jnp.einsum('bhtk,bhsk->bhts', qe, k * jnp.exp(-b))
    causal = jnp.tril(jnp.ones((C, C), dtype=bool))
    scores = jnp.where(causal, scores, 0.0)
    o = jnp.einsum('bhts,bhsv->bhtv', scores, v) + jnp.einsum('bhtk,bhkv->bhtv', qe, S)
    S_new = jnp.exp(b_last[:, :, 0, :])[..., None] * S + jnp.einsum(
        'bhsk,bhsv->bhkv', k * jnp.exp(b_last - b), v)
    return S_new, o

def gla_core(q, k, v, g, S0):
    B, H, T, _ = q.shape
    c = min(CHUNK, T)
    n = T // c

    def split(a):
        return a.reshape(B, H, n, c, a.shape[-1]).transpose(2, 0, 1, 3, 4)

    S, o = lax.scan(gla_chunk_step, S0, (split(q), split(k), split(v), split(g)))
    o = o.transpose(1, 2, 0, 3, 4).reshape(B, H, T, v.shape[-1])
    return o, S

def gla_layer(x, S0, norm_pre, w_in, w_gate2, b_gate, head_norm, w_out, norm_post):
    B, T, _ = x.shape
    h = rmsnorm(x, norm_pre)
    proj = h @ w_in
    q, k, v, gate, glr = jnp.split(
        proj, [KD_A, 2 * KD_A, 2 * KD_A + VD_A, 2 * KD_A + 2 * VD_A], axis=-1)
    z = (glr @ w_gate2 + b_gate).astype(jnp.float32)
    g = jax.nn.log_sigmoid(z) / GATE_TAU

    def heads(a, d):
        return a.astype(jnp.float32).reshape(B, T, H_A, d).transpose(0, 2, 1, 3)

    o, S = gla_core(heads(q, DK_A) * (DK_A ** -0.5), heads(k, DK_A), heads(v, DV_A),
                    heads(g, DK_A), S0.astype(jnp.float32))
    o = rmsnorm(o.transpose(0, 2, 1, 3), head_norm.reshape(H_A, DV_A)).reshape(B, T, VD_A)
    o = o.astype(x.dtype) * jax.nn.silu(gate)
    return x + rmsnorm(o @ w_out, norm_post), S

def shared_kv(x, pos, kv_norm, kv_w_down, kv_latent_norm):
    h = rmsnorm(x, kv_norm)
    lat = h @ kv_w_down
    ckv = rmsnorm(lat[..., :KV_LORA], kv_latent_norm)
    krope = rope(lat[..., KV_LORA:], pos)
    return ckv, krope

def expand_kv(ckv, krope, w_uk, w_uv):
    B, S, _ = ckv.shape
    k_nope = (ckv @ w_uk).reshape(B, S, H_B, NOPE)
    k = jnp.concatenate(
        [k_nope, jnp.broadcast_to(krope[:, :, None, :], (B, S, H_B, ROPE)).astype(k_nope.dtype)], axis=-1)
    v = (ckv @ w_uv).reshape(B, S, H_B, V_B)
    return k, v

def mla_attend(q, k, v, q_offset):
    B, T, H, D = q.shape
    S = k.shape[1]
    blk = min(QBLOCK, T)
    n = T // blk
    scale = D ** -0.5
    k_chunk = jnp.arange(S) // CHUNK
    qb = q.reshape(B, n, blk, H, D).transpose(1, 0, 2, 3, 4)

    def one(args):
        qi, i = args
        q_chunk = (q_offset + i * blk + jnp.arange(blk)) // CHUNK
        s = jnp.einsum('bqhd,bshd->bhqs', qi, k).astype(jnp.float32) * scale
        s = jnp.where(k_chunk[None, :] <= q_chunk[:, None], s, -jnp.inf)
        p = jax.nn.softmax(s, axis=-1).astype(v.dtype)
        return jnp.einsum('bhqs,bshd->bqhd', p, v)

    o = lax.map(one, (qb, jnp.arange(n)))
    return o.transpose(1, 0, 2, 3, 4).reshape(B, T, H, v.shape[-1])

def mla_layer(x, k, v, pos, q_offset, norm_pre, w_in, q_norm, w_uq, w_out, norm_post):
    B, T, _ = x.shape
    h = rmsnorm(x, norm_pre)
    proj = h @ w_in
    q_lat, gate = proj[..., :Q_LORA], proj[..., Q_LORA:]
    q = (rmsnorm(q_lat, q_norm) @ w_uq).reshape(B, T, H_B, NOPE + ROPE)
    q = jnp.concatenate([q[..., :NOPE], rope(q[..., NOPE:], pos)], axis=-1)
    o = mla_attend(q, k, v, q_offset).reshape(B, T, VD_B) * jax.nn.silu(gate)
    return x + rmsnorm(o @ w_out, norm_post)

def trunk(x, gla_state0, cache_ckv, cache_krope, pos_offset,
          a_norm_pre, a_w_in, a_w_gate2, a_b_gate, a_head_norm, a_w_out, a_norm_post,
          kv_norm, kv_w_down, kv_latent_norm, kv_w_uk, kv_w_uv,
          b_norm_pre, b_w_in, b_q_norm, b_w_uq, b_w_out, b_norm_post):
    T = x.shape[1]
    pos = pos_offset + jnp.arange(T)
    states = []
    ckv_new = krope_new = k_sh = v_sh = None
    for layer in range(DEPTH):
        if layer == N_A:
            ckv_new, krope_new = shared_kv(x, pos, kv_norm, kv_w_down, kv_latent_norm)
            if cache_ckv is None:
                ckv_all, krope_all = ckv_new, krope_new
            else:
                ckv_all = jnp.concatenate([cache_ckv.astype(ckv_new.dtype), ckv_new], axis=1)
                krope_all = jnp.concatenate([cache_krope.astype(krope_new.dtype), krope_new], axis=1)
            k_sh, v_sh = expand_kv(ckv_all, krope_all, kv_w_uk, kv_w_uv)
        if layer < N_A:
            x, S = gla_layer(x, gla_state0[layer], a_norm_pre[layer], a_w_in[layer], a_w_gate2[layer],
                             a_b_gate[layer], a_head_norm[layer], a_w_out[layer], a_norm_post[layer])
            states.append(S)
        else:
            j = layer - N_A
            x = mla_layer(x, k_sh, v_sh, pos, pos_offset, b_norm_pre[j], b_w_in[j], b_q_norm[j],
                          b_w_uq[j], b_w_out[j], b_norm_post[j])
    return x, jnp.stack(states), ckv_new, krope_new

def setup_inputs(seed: int = 0) -> dict:
    key = jax.random.key(seed)
    ks = jax.random.split(key, 24)
    f32 = jnp.float32

    def w(k, shape, fan_in):
        return jax.random.normal(k, shape, f32) * (fan_in ** -0.5)

    def g(k, shape):
        return 1.0 + 0.05 * jax.random.normal(k, shape, f32)

    return {
        "x_prompt": jax.random.normal(ks[0], (BATCH, SEQ, D_MODEL), f32),
        "x_sample": jax.random.normal(ks[1], (DEC_BATCH, DEC_SEQ, D_MODEL), f32),
        "state_gla": jax.random.normal(ks[2], (N_A, DEC_BATCH, H_A, DK_A, DV_A), f32),
        "cache_ckv": jax.random.normal(ks[3], (DEC_BATCH, PAST_LEN, KV_LORA), f32),
        "cache_krope": jax.random.normal(ks[4], (DEC_BATCH, PAST_LEN, ROPE), f32),
        "a_norm_pre": g(ks[5], (N_A, D_MODEL)),
        "a_w_in": w(ks[6], (N_A, D_MODEL, IN_A), D_MODEL),
        "a_w_gate2": w(ks[7], (N_A, GATE_RANK, KD_A), GATE_RANK),
        "a_b_gate": 0.1 * jax.random.normal(ks[8], (N_A, KD_A), f32),
        "a_head_norm": g(ks[9], (N_A, VD_A)),
        "a_w_out": w(ks[10], (N_A, VD_A, D_MODEL), VD_A),
        "a_norm_post": g(ks[11], (N_A, D_MODEL)),
        "kv_norm": g(ks[12], (D_MODEL,)),
        "kv_w_down": w(ks[13], (D_MODEL, KV_LORA + ROPE), D_MODEL),
        "kv_latent_norm": g(ks[14], (KV_LORA,)),
        "kv_w_uk": w(ks[15], (KV_LORA, H_B * NOPE), KV_LORA),
        "kv_w_uv": w(ks[16], (KV_LORA, VD_B), KV_LORA),
        "b_norm_pre": g(ks[17], (N_B, D_MODEL)),
        "b_w_in": w(ks[18], (N_B, D_MODEL, IN_B), D_MODEL),
        "b_q_norm": g(ks[19], (N_B, Q_LORA)),
        "b_w_uq": w(ks[20], (N_B, Q_LORA, H_B * (NOPE + ROPE)), Q_LORA),
        "b_w_out": w(ks[21], (N_B, VD_B, D_MODEL), VD_B),
        "b_norm_post": g(ks[22], (N_B, D_MODEL)),
    }

def reference(x_prompt, x_sample, state_gla, cache_ckv, cache_krope,
              a_norm_pre, a_w_in, a_w_gate2, a_b_gate, a_head_norm, a_w_out, a_norm_post,
              kv_norm, kv_w_down, kv_latent_norm, kv_w_uk, kv_w_uv,
              b_norm_pre, b_w_in, b_q_norm, b_w_uq, b_w_out, b_norm_post):
    weights = (a_norm_pre, a_w_in, a_w_gate2, a_b_gate, a_head_norm, a_w_out, a_norm_post,
               kv_norm, kv_w_down, kv_latent_norm, kv_w_uk, kv_w_uv,
               b_norm_pre, b_w_in, b_q_norm, b_w_uq, b_w_out, b_norm_post)
    state0 = jnp.zeros((N_A, x_prompt.shape[0], H_A, DK_A, DV_A), jnp.float32)
    y_prompt, st_p, ckv_prompt, krope_prompt = trunk(x_prompt, state0, None, None, 0, *weights)
    past = cache_ckv.shape[1]
    y_sample, st_s, ckv_sample, krope_sample = trunk(x_sample, state_gla, cache_ckv, cache_krope,
                                                     past, *weights)
    state_gla_prompt = st_p.astype(x_prompt.dtype)
    state_gla_sample = st_s.astype(state_gla.dtype)
    return (y_prompt, y_sample, state_gla_prompt, state_gla_sample,
            ckv_prompt, krope_prompt, ckv_sample, krope_sample)


_drawn_inputs = setup_inputs


def setup_inputs(seed=0):
    import zlib

    import numpy as np

    out = dict(_drawn_inputs(seed))
    spreads = {}
    factors = {}
    for name, (base, spread) in spreads.items():
        noise = np.random.default_rng([zlib.crc32(name.encode()), seed]).standard_normal(out[name].shape)
        drawn = base * np.exp(spread * noise) if base else spread * noise
        out[name] = __import__('jax').numpy.asarray(drawn.astype(out[name].dtype))
    for name, factor in factors.items():
        out[name] = (out[name] * factor).astype(out[name].dtype)
    return out
```

```python
import concourse.bass as bass
from concourse import mybir
from contextlib import ExitStack

P = 128
D = 1024
KD = D // P
SEQ = 512
SB, SL = 8, 16
PAST = 512
NP = SEQ // P
NT = NP + 1
TOK = NT * P
HALF = TOK // 2
HA, DK, DV = 4, 128, 256
RANK = 16
HB, NOPE, ROPE, VB = 8, 128, 64, 128
RH = ROPE // 2
QL, KL = 384, 256
KQ, KC = QL // P, KL // P
EPS = 1e-6
NEG = -float(2 ** 120)
SCALE = (NOPE + ROPE) ** -0.5
PIECE = 1024
NSTAGE = 3
NBANK = 4

def columns(sizes):
    out, at = {}, 0
    for name, n in sizes:
        out[name] = (at, at + n)
        at += n
    return out, at


CONST, NCONST = columns((("ident", P), ("mask_p", P), ("mask_s", P), ("member", SB), ("cos", NT * RH), ("sin", NT * RH)))
CONST_R, NCONST_R = columns((("cum_p", P + 2), ("cum_s", P + 2), ("early", P), ("late", P), ("ones", P), ("others", 2 * P)))


def slabs():
    out = {"glr": [[("a_w_in", 0, KD, 2 * HA * DK + 2 * HA * DV, RANK, "a_norm_pre")]]}
    for h in range(HA):
        out["qk", h] = [[("a_w_in", 0, KD, h * DK, DK, "a_norm_pre")], [("a_w_in", 0, KD, (HA + h) * DK, DK, "a_norm_pre")]]
        for n, base in (("v", 2 * HA * DK), ("g", 2 * HA * DK + HA * DV)):
            out[n, h] = [[("a_w_in", k, k + 4, base + h * DV, DV, "a_norm_pre")] for k in (0, 4)]
    for s in range(4):
        out["wo", "A", s] = [[("a_w_out", k, k + 4, s * 256, 256, "a_head_norm")] for k in (0, 4)]
    out["kvc"] = [[("kv_w_down", k, k + 4, 0, KL, "kv_norm")] for k in (0, 4)]
    out["kvr"] = [[("kv_w_down", 0, KD, KL, ROPE, "kv_norm")]]
    out["ql0"] = [[("b_w_in", k, k + 4, 0, 256, "b_norm_pre")] for k in (0, 4)]
    out["ql1"] = [[("b_w_in", 0, KD, 256, 128, "b_norm_pre")]]
    for s in range(4):
        out["gb", s] = [[("b_w_in", k, k + 4, QL + s * 256, 256, "b_norm_pre")] for k in (0, 4)]
    out["uqr"] = [[("uq_rope", 0, KQ, h * ROPE, 4 * ROPE, "b_q_norm")] for h in (0, 4)]
    for h in range(HB):
        out["hd", h] = [[("b_w_uq", 0, KQ, h * (NOPE + ROPE), NOPE, "b_q_norm"),
                         ("kv_w_uk", 0, KC, h * NOPE, NOPE, None), ("kv_w_uv", 0, KC, h * VB, VB, None)]]
    out["uv"] = [[("kv_w_uv", k, k + 1, 0, HB * VB, None)] for k in range(KC)]
    for s in range(4):
        out["wo", "B", s] = [[("b_w_out", k, k + 4, s * 256, 256, None)] for k in (0, 4)]
    return out


SLABS = slabs()
SLAB_NO = {name: n for n, name in enumerate(SLABS)}
PIECES = [(name, j) for name, pieces in SLABS.items() for j in range(len(pieces))]
PIECE_NO = {p: n for n, p in enumerate(PIECES)}
SLAB_NAMES = list(SLABS)


def stage_counts():
    count, out = [0] * NSTAGE, []
    for n, (name, j) in enumerate(PIECES):
        for w, k0, k1, *_ in SLABS[name][j]:
            count[n % NSTAGE] += 16 * (k1 - k0 if w == "uq_rope" else 1)
        out.append(count[n % NSTAGE])
    return out


STAGE_COUNT = stage_counts()


def steps():
    out = []

    def load(name):
        out.extend(("piece", name, j) for j in range(len(SLABS[name])))

    out.append(("const",))
    load("glr")
    load(("qk", 0))
    for t in range(NT):
        out += [("xn", t), ("xT", "A", t)]
    out += [("glr",)]
    load(("v", 0))
    for t in range(NT):
        out += [("z", t)]
    out += [("ln",)]
    for t in range(NT):
        out += [("lg", t), ("c", t)]
    out += [("lds", 0)]
    for h in range(HA):
        nxt = ("qk", h + 1) if h + 1 < HA else ("wo", "A", 1)
        out += [("e", h), ("q", h), ("k", h), ("qlo", h), ("klo", h)]
        load(("g", h))
        out += [("v", h), ("kT", h), ("vs", h), ("sc", h)]
        load(nxt if h + 1 < HA else ("wo", "A", 0))
        out += [("gt", h), ("gts", h), ("sclo", h), ("U", h), ("Slo", h)]
        load(("v", h + 1) if h + 1 < HA else nxt)
        out += [("stp", h), ("os", h), ("o", h), ("Us", h, 0), ("Us", h, 1), ("sts", h)]
        if h + 1 < HA:
            out += [("lds", h + 1)]
    out += [("ldr",)]
    for ph in "AB":
        if ph == "B":
            heads(out, load)
        for t in range(NT):
            out += [("oT", ph, t)]
        for s in range(4):
            out += [("y", ph, s), ("ys", ph, s)]
            if s < 2:
                load(("wo", ph, s + 2))
            elif ph == "A":
                load("kvc" if s == 2 else "kvr")
        for t in range(NT):
            out += [("r", ph, t)]
            if ph == "A":
                out += [("rx", t), ("xT", "B", t)]
            else:
                out += [("oy", t)]
    return out


def heads(out, load):
    out += [("lc",), ("lcs",)]
    load("ql0")
    out += [("lr",)]
    load("ql1")
    out += [("cn",), ("och",)]
    out += [("qa",), ("qas",)]
    load(("gb", 0))
    out += [("qb",), ("qs",)]
    load(("gb", 1))
    out += [("cT", t) for t in range(NT)]
    out += [("qT", t) for t in range(NT)]
    for s in range(4):
        out += [("gb", s), ("gbs", s)]
        load([("gb", 2), ("gb", 3), "uqr", ("hd", 0)][s])
    for t in range(NT):
        out += [("qr", t)]
        if t:
            out += [("qrT", t - 1)]
    out += [("qrT", NT - 1)]
    load(("hd", 1))
    out += [("qn", 0), ("wt", 0), ("kh", 0), ("vh", 0), ("qabs", 0)]
    for h in range(HB):
        more = h + 1 < HB
        out += [("S", h, 0), ("S", h, 1)]
        if more:
            out += [("qn", h + 1), ("wt", h + 1)]
        out += [("T", h, 0)]
        if more:
            out += [("kh", h + 1)]
        out += [("O", h, 0), ("T", h, 1)]
        if more:
            out += [("qabs", h + 1)]
        out += [("O", h, 1)]
        if more:
            out += [("vh", h + 1)]
        if h + 2 < HB:
            load(("hd", h + 2))
    load("uv")
    out += [("ldc", 0), ("ldc", 1), ("ct", 0), ("cr", 0)]
    for b in range(SB):
        out += [("ss", b), ("cs", b)]
        if b + 2 < SB:
            out += [("ldc", b + 2)]
        if b + 1 < SB:
            out += [("ct", b + 1), ("cr", b + 1)]
        out += [("sn", b), ("st", b), ("sv", b)]
    load(("wo", "B", 0))
    out += [("so",)]
    load(("wo", "B", 1))


PARTS = {
    "const": ("act",), "piece": ("sp", "pool", "act", "dve"), "lds": ("sp",), "sts": ("sp",), "stp": ("sp",), "ldr": ("sp",),
    "och": ("sp",), "ldc": ("sp",), "oy": ("sp",), "xn": ("act", "pool", "dve"), "xT": ("pe", "act", "dve"), "glr": ("pe", "act"),
    "z": ("pe", "dve", "act"), "ln": ("act",), "lg": ("dve",), "c": ("pe", "act"), "e": ("act",),
    "q": ("pe", "dve", "act"), "k": ("pe", "dve", "act"), "qlo": ("dve",), "klo": ("dve",),
    "v": ("pe", "act", "dve"), "vs": ("pe", "act", "dve"), "kT": ("pe", "act", "dve"), "sc": ("pe", "dve", "act"),
    "sclo": ("dve",), "gt": ("pe", "act", "dve"), "gts": ("pe", "act", "dve"), "U": ("pe", "dve", "act"),
    "Slo": ("dve",), "os": ("pe", "act", "pool", "dve"), "o": ("pe", "act", "pool", "dve"), "Us": ("pe", "dve"),
    "oT": ("pe", "act", "dve"), "y": ("pe", "act", "dve"), "ys": ("pe", "act", "dve"), "r": ("pool", "dve", "act"),
    "rx": ("pool", "dve"), "lc": ("pe", "act", "pool", "dve"), "lcs": ("pe", "act", "pool", "dve"), "lr": ("pe", "dve"),
    "cn": ("act", "dve"), "cT": ("pe", "act", "dve"), "qa": ("pe", "act", "dve"), "qas": ("pe", "act", "dve"),
    "qb": ("pe", "act", "dve"), "qs": ("pool", "dve"), "gb": ("pe", "act", "dve"), "gbs": ("pe", "act", "dve"),
    "qT": ("pe", "act", "dve"), "qr": ("pe", "dve"), "qrT": ("pe", "act", "dve"), "qn": ("pe", "act", "dve"),
    "wt": ("pe", "act"), "kh": ("pe", "act", "dve"), "vh": ("pe", "act", "dve"), "qabs": ("pe", "act", "dve"),
    "S": ("pe", "dve", "act"), "T": ("pe", "act", "dve"), "O": ("pe", "dve"), "ct": ("pe", "act", "dve"),
    "cr": ("pe", "act", "dve"), "ss": ("pe", "dve", "act"), "cs": ("act", "dve"), "sn": ("dve",),
    "st": ("pe", "act", "dve"), "sv": ("pe", "act", "dve"), "so": ("pe", "dve"),
}
def parts(step):
    if step[0] == "piece" and not any(w[5] for w in SLABS[step[1]][step[2]]):
        return ("sp", "act", "dve")
    return PARTS[step[0]]


LAST_READER = {k: [e for e in p if e in ("act", "dve")][-1] for k, p in PARTS.items() if "pe" in p}
LAST_READER.update({k: "dve" for k in ("q", "k", "sc", "U")})
LAST_READER["S"] = LAST_READER["ss"] = LAST_READER["z"] = "act"
STEPS = steps()
assert len(set(STEPS)) == len(STEPS)


def count_parts():
    at = {e: {} for e in ("pe", "act", "dve", "pool")}
    for s in STEPS:
        for e in at.keys() & set(parts(s)):
            at[e][s] = len(at[e]) + 1
    return at


AT = count_parts()
BANKED = [s for s in STEPS if "pe" in PARTS[s[0]]]
BANK_NO = {s: n for n, s in enumerate(BANKED)}
USERS = {"glr": ("glr",), "kvc": ("lcs",), "kvr": ("lr",), "ql0": ("qas",), "ql1": ("qb",), "uqr": ("qr", NT - 1), "uv": ("so",)}
for _h in range(HA):
    USERS["qk", _h], USERS["v", _h], USERS["g", _h] = ("k", _h), ("vs", _h), ("gts", _h)
for _s in range(4):
    USERS["wo", "A", _s], USERS["wo", "B", _s], USERS["gb", _s] = ("ys", "A", _s), ("ys", "B", _s), ("gbs", _s)
for _h in range(HB):
    USERS["hd", _h] = ("vh", _h)

STAT = {}
for _name, _n in [(("x", t), 1) for t in range(NT)] + [(("x1", t), 1) for t in range(NT)] \
        + [(("o", h), NT) for h in range(HA)] + [(("y", ph, t), 4) for ph in "AB" for t in range(NT)] \
        + [(("yr", ph, t), 1) for ph in "AB" for t in range(NT)] + [(("lat",), NT), (("qa",), NT), (("qb",), NT)] \
        + [(("S", h, u), 2) for h in range(HB) for u in range(2)] + [(("ss", b), 1) for b in range(SB)]:
    STAT[_name] = (sum(b - a for a, b in STAT.values()), sum(b - a for a, b in STAT.values()) + _n)
NSTAT = max(b for _, b in STAT.values())

UNITS = ((3, 0), (2, 1))


def program(nc, dram, outs):
    fp32, fp32r = mybir.dt.float32, mybir.dt.float32r
    ALU, ACT, AX = mybir.AluOpType, mybir.ActivationFunctionType, mybir.AxisListType
    MUL, ADD, SUB = ALU.mult, ALU.add, ALU.subtract
    (y_prompt, y_sample, st_prompt, st_sample, ckv_prompt, krope_prompt, ckv_sample, krope_sample) = outs
    w_dram = {n: dram[n].rearrange("(k p) n -> p k n", p=P) for n in
              ("kv_w_down", "kv_w_uk", "kv_w_uv")}
    for n in ("a_w_in", "a_w_out", "b_w_in", "b_w_uq", "b_w_out"):
        w_dram[n] = dram[n][0].rearrange("(k p) n -> p k n", p=P)
    uq_rope = w_dram["b_w_uq"].rearrange("p k (h n) -> p k h n", n=NOPE + ROPE)

    ctx = ExitStack()
    with ctx:
        def sem(name):
            return ctx.enter_context(nc.semaphore(name))

        place = [-(-nc.sbuf_base // 64) * 64]

        def sb(name, shape, dt=fp32):
            size = 4
            for n in shape[1:]:
                size *= n
            at = place[0]
            place[0] += -(-size // 32) * 32
            assert place[0] <= nc.sbuf_usable_end, (name, place[0])
            return nc.alloc_sbuf_tensor_at(name, shape, dt, offset=at)

        def pair(name, shape):
            return sb(name + "_hi", shape, fp32r), sb(name + "_lo", shape, fp32r)

        def raw(ap):
            return ap.bitcast(fp32)

        def over(ap, n):
            return ap.unsqueeze(2).to_broadcast([ap.shape[0], ap.shape[1], n])

        def times(ap, n):
            return ap.unsqueeze(1).to_broadcast([ap.shape[0], n, ap.shape[1]])

        stage = [sb(f"stage{i}", [P, PIECE]) for i in range(NSTAGE)]
        slab = [pair(f"slab{i}", [P, 2 * PIECE]) for i in range(2)]
        const = sb("const", [P, NCONST])
        const_r = sb("const_r", [P, NCONST_R], fp32r)
        gain = {n: sb("gain_" + n, [P, k]) for n, k in
                (("a_norm_pre", KD), ("a_head_norm", KD), ("kv_norm", KD), ("b_norm_pre", KD), ("b_q_norm", KQ))}
        post = sb("post", [P, D])
        lat_gain = sb("lat_gain", [P, KL])
        minus_half = sb("minus_half", [P, 8])
        stat = sb("stat", [P, NSTAT])
        stat2 = sb("stat2", [P, NSTAT])
        junk = sb("junk", [P, D])
        rows = sb("rows", [P, NT, D])
        gate_w = sb("gate_w", [RANK + 1, HA * DK])
        hat_at = place[0]
        hat = pair("hat", [P, KD, TOK])
        phase_at = place[0]
        glrT = sb("glrT", [RANK + 1, TOK])
        cumT = sb("cumT", [P, HA, TOK])
        decay = sb("decay", [P, HA, NT])
        Ep, Em = sb("Ep", [P, TOK]), sb("Em", [P, TOK])
        eB = sb("eB", [P, NT])
        ec = sb("ec", [P, NP])
        tmp, kt = sb("tmp", [P, TOK]), sb("kt", [P, TOK])
        z_at = place[0]
        qT, kT = pair("qT", [P, TOK]), pair("kT", [P, TOK])
        kn = pair("kn", [P, NT, DK])
        vv = pair("vv", [P, NT, DV])
        v_s = sb("v_s", [P, DV])
        scT = pair("scT", [P, TOK])
        st_in = sb("st_in", [P, NP, DV])
        st = pair("st", [P, NP, DV])
        st_s = sb("st_s", [P, SB, DV])
        q_own = sb("q_own", [P, SB, P])
        k_own = sb("k_own", [P, SB, DK])
        th = st_in[:, :, :].rearrange("p t n -> p (t n)")
        place[0] = z_at
        z_abs, z_min = sb("z_abs", [P, NT, HA * DK]), sb("z_min", [P, NT, HA * DK])
        lg = pair("lg", [P, NT, HA * DK])
        place[0] = phase_at
        x1 = sb("x1", [P, NT, D])
        ql_at = place[0]
        qlT = pair("qlT", [P, KQ, TOK])
        ckvn = sb("ckvn", [P, NT, KL])
        cT = pair("cT", [P, KC, TOK])
        krn = sb("krn", [P, NT, ROPE])
        cn_s = pair("cn_s", [P, KL])
        krS = sb("krS", [P, TOK], fp32r)
        krL = sb("krL", [ROPE, TOK], fp32r)
        qS_at = place[0]
        qS = sb("qS", [P, HB, SEQ], fp32r)
        qS_s = sb("qS_s", [P, SB, HB, SL], fp32r)
        prob = [sb(f"prob{i}", [P, NT, P]) for i in range(2)]
        qln = rows[:, :, 0:QL]
        place[0] = qS_at
        thb = sb("thb", [P, D])
        place[0] = hat_at
        qab = pair("qab", [P, KC, SB, HB, SL])
        head_at = place[0]
        qrn, rtmp = sb("qrn", [P, HB * ROPE]), sb("rtmp", [P, HB * ROPE])
        place[0] = head_at
        qN = pair("qN", [P, TOK])
        kN = pair("kN", [P, SEQ])
        vN = pair("vN", [P, NP, VB])
        wT = pair("wT", [P, KL])
        pT = pair("pT", [P, TOK])
        assert place[0] <= phase_at
        place[0] = head_at
        sT = pair("sT", [P, KC, PAST])
        cn = pair("cn", [P, PAST // P, KL])
        spT = pair("spT", [P, TOK])
        skS = sb("skS", [P, PAST], fp32r)
        assert place[0] <= phase_at
        place[0] = ql_at
        ctxT = pair("ctxT", [P, KC, HB, P])
        assert place[0] <= ql_at + 15360 + 5120
        place[0] = qS_at
        craw = [sb(f"craw{i}", [P, PAST // P, KL + ROPE]) for i in range(2)]
        skL = sb("skL", [ROPE, PAST], fp32r)

        pb = [ctx.enter_context(nc.psum_tensor(f"bank{i}", [P, 2, 512], fp32)) for i in range(NBANK)]
        flat = [b[:, :, :].rearrange("p a n -> p (a n)") for b in pb]

        def cst(name, p=P):
            a, b = CONST[name]
            return const[0:p, a:b]

        def cst_r(name, p=P):
            a, b = CONST_R[name]
            return const_r[0:p, a:b]

        ident = cst("ident")

        def rotary_to(t, p):
            return qS[p, :, t * P:(t + 1) * P] if t < NP else qS_s[p, :, :, :].rearrange("p b h n -> p h b n")

        def rotary_from(row, t):
            v = row[0:ROPE, :].rearrange("p (h n) -> p h n", n=P)
            return v if t < NP else v.rearrange("p h (b n) -> p h b n", n=SL)

        def by_stream(bank):
            return bank[:, 0, 0:KL].rearrange("p (k b n) -> p k b n", k=KC, n=SL)

        def S1(name, src=None, t=None):
            a, b = STAT[name]
            src = stat if src is None else src
            return src[:, a:b] if t is None else src[:, a + t:a + t + 1]

        done = {"pe": sem("tensor_done"), "act": sem("scalar_done"), "dve": sem("vector_done"), "pool": sem("gpsimd_done")}
        act_own, dve_own, pool_own = sem("scalar_own"), sem("vector_own"), sem("gpsimd_own")
        consts_in, x_in, gains_in = sem("consts_in"), [sem(f"x{t}_in") for t in range(NT)], sem("gains_in")
        stage_in = [sem(f"stage{i}_in") for i in range(NSTAGE)]
        state_in, state_out, final_out, rest_in, post_in = sem("state_in"), sem("state_out"), sem("final_out"), sem("rest_in"), sem("post_in")
        cache_in = [sem(f"cache{i}_in") for i in range(2)]
        latent_out, y_out = sem("latent_out"), sem("y_out")
        ones_set, own_set, gate_in = sem("ones_set"), sem("own_set"), sem("gate_in")

        def after(eng, who, *step):
            eng.wait_ge(done[who], AT[who][step])

        def before_bank(eng, step):
            n = BANK_NO[step]
            if n >= NBANK:
                last = BANKED[n - NBANK]
                after(eng, LAST_READER[last[0]], *last)
            return pb[n % NBANK], flat[n % NBANK]

        def banks(step):
            n = BANK_NO[step] % NBANK
            return pb[n], flat[n]

        def weights(name):
            return slab[SLAB_NO[name] % 2]

        def used(name, j):
            return sum((w[2] - w[1]) * w[4] for w in SLABS[name][j])

        block = ctx.enter_context(nc.Block())

        @block.sync
        def _(sp):
            def load_piece(name, j):
                n = PIECE_NO[name, j]
                if n >= NSTAGE:
                    after(sp, "dve", "piece", *PIECES[n - NSTAGE])
                at = 0
                for w, k0, k1, c0, nc_, _g in SLABS[name][j]:
                    size = (k1 - k0) * nc_
                    if w == "uq_rope":
                        h0 = c0 // ROPE
                        for k in range(k0, k1):
                            sp.dma_start(stage[n % NSTAGE][:, at + k * nc_:at + (k + 1) * nc_].rearrange("p (h n) -> p h n", n=ROPE),
                                         uq_rope[:, k, h0:h0 + 4, NOPE:NOPE + ROPE]).then_inc(stage_in[n % NSTAGE], 16)
                    else:
                        sp.dma_start(stage[n % NSTAGE][:, at:at + size].rearrange("p (k n) -> p k n", n=nc_),
                                     w_dram[w][:, k0:k1, c0:c0 + nc_]).then_inc(stage_in[n % NSTAGE], 16)
                    at += size

            sp.dma_start(junk[:, 0:NCONST_R], dram["const_r"]).then_inc(consts_in, 16)
            sp.dma_start(const[:, :], dram["const"]).then_inc(consts_in, 16)
            for n, g in gain.items():
                sp.dma_start(g[:, :], dram[n]).then_inc(gains_in, 16)
            for t in range(NT):
                sp.dma_start(rows[:, t, :], dram["x_prompt"][0, t * P:(t + 1) * P, :] if t < NP
                             else dram["x_sample"].rearrange("b l d -> (b l) d")).then_inc(x_in[t], 16)
            sp.dma_start(gate_w[0:RANK, :], dram["a_w_gate2"][0]).then_inc(gate_in, 16)
            sp.dma_start(gate_w[RANK:RANK + 1, :], dram["a_b_gate"]).then_inc(gate_in, 16)
            sp.dma_start(post[:, :], dram["a_norm_post"].to_broadcast([P, D])).then_inc(post_in, 16)
            sp.dma_start(lat_gain[:, :], dram["kv_latent_norm"].unsqueeze(0).to_broadcast([P, KL])).then_inc(post_in, 16)
            for name, j in PIECES[:2]:
                load_piece(name, j)
            for step in STEPS:
                if "sp" not in parts(step):
                    continue
                kind = step[0]
                if kind == "piece":
                    n = PIECE_NO[step[1], step[2]] + 2
                    if n < len(PIECES):
                        load_piece(*PIECES[n])
                elif kind == "lds":
                    h = step[1]
                    if h:
                        sp.wait_ge(state_out, 16 * h)
                    sp.dma_start(st_s[:, :, :], dram["state_gla"][0, :, h].rearrange("b k v -> k b v")).then_inc(state_in, 16)
                elif kind == "sts":
                    h = step[1]
                    after(sp, "dve", "Us", h, 1)
                    sp.dma_start(st_sample[0, :, h].rearrange("b k v -> k b v"), st_s[:, :, :]).then_inc(state_out, 16)
                elif kind == "stp":
                    h = step[1]
                    after(sp, "dve", "U", h)
                    sp.dma_start(st_prompt[0, 0, h], st_in[:, 0, :]).then_inc(final_out, 16)
                elif kind == "ldr":
                    for who, s in (("dve", ("Us", HA - 1, 1)), ("act", ("o", HA - 1)), ("pe", ("Us", HA - 1, 1))):
                        after(sp, who, *s)
                    sp.dma_start(x1[:, 0:NP, :], dram["x_prompt"][0].rearrange("(t p) d -> p t d", p=P)).then_inc(rest_in, 16)
                    sp.dma_start(x1[:, NP, :], dram["x_sample"].rearrange("b l d -> (b l) d")).then_inc(rest_in, 16)
                elif kind == "och":
                    after(sp, "dve", "lcs")
                    after(sp, "dve", "lr")
                    after(sp, "dve", "r", "A", NT - 1)
                    sp.dma_start(post[:, :], dram["b_norm_post"].to_broadcast([P, D])).then_inc(post_in, 16)
                    sp.dma_start(ckv_prompt[0].rearrange("(t p) n -> p t n", p=P), ckvn[:, 0:NP, :]).then_inc(latent_out, 16)
                    sp.dma_start(ckv_sample.rearrange("b l n -> (b l) n"), ckvn[:, NP, :]).then_inc(latent_out, 16)
                    sp.dma_start(krope_prompt[0].rearrange("(t p) n -> p t n", p=P), krn[:, 0:NP, :]).then_inc(latent_out, 16)
                    sp.dma_start(krope_sample.rearrange("b l n -> (b l) n"), krn[:, NP, :]).then_inc(latent_out, 16)
                elif kind == "ldc":
                    b = step[1]
                    if b < 2:
                        after(sp, "pe", "S", HB - 1, 1)
                    else:
                        after(sp, "dve", "cs", b - 2)
                        after(sp, "pe", "cr", b - 2)
                    sp.dma_start(craw[b % 2][:, :, 0:KL], dram["cache_ckv"][b].rearrange("(s p) n -> p s n", p=P)).then_inc(cache_in[b % 2], 16)
                    sp.dma_start(craw[b % 2][:, :, KL:], dram["cache_krope"][b].rearrange("(s p) n -> p s n", p=P)).then_inc(cache_in[b % 2], 16)
                elif kind == "oy":
                    t = step[1]
                    after(sp, "dve", "r", "B", t)
                    sp.dma_start(y_prompt[0, t * P:(t + 1) * P, :] if t < NP else y_sample.rearrange("b l d -> (b l) d"),
                                 x1[:, t, :]).then_inc(y_out, 16)
            sp.wait_ge(y_out, 16 * NT)
            sp.wait_ge(latent_out, 16 * 4)
            sp.wait_ge(state_out, 16 * HA)
            sp.wait_ge(final_out, 16 * HA)

        @block.gpsimd
        def _(pool):
            own = [0]

            def link(ins):
                own[0] += 1
                ins.then_inc(pool_own, 1)
                pool.wait_ge(pool_own, own[0])

            def rms(name, width, count, factor=1.0):
                s, r = S1(name), S1(name, stat2)
                link(pool.tensor_scalar(r, s, 1.0 / width, EPS, MUL, ADD))
                if factor == 1.0:
                    return pool.tensor_tensor(r, r, minus_half[:, 0:count], ALU.pow)
                link(pool.tensor_tensor(r, r, minus_half[:, 0:count], ALU.pow))
                return pool.tensor_scalar(r, r, factor, None, MUL)

            pool.memset(q_own[:, :, :], 0.0).then_inc(own_set, 1)
            pool.memset(glrT[:, :], 1.0).then_inc(ones_set, 1)
            link(pool.memset(minus_half[:, :], -0.5))
            pool.wait_ge(gains_in, 16 * len(gain))
            for step in STEPS:
                if "pool" not in parts(step):
                    continue
                kind = step[0]
                if kind == "piece":
                    _, name, j = step
                    n = PIECE_NO[name, j]
                    pool.wait_ge(stage_in[n % NSTAGE], STAGE_COUNT[n])
                    at = 0
                    for w, k0, k1, c0, cols, g in SLABS[name][j]:
                        if g:
                            v = stage[n % NSTAGE][:, at:at + (k1 - k0) * cols].rearrange("p (k n) -> p k n", n=cols)
                            last = pool.tensor_tensor(v, v, over(gain[g][:, k0:k1], cols), MUL)
                        at += (k1 - k0) * cols
                elif kind == "xn":
                    after(pool, "act", *step)
                    last = rms(("x", step[1]), D, 1)
                elif kind in ("o", "os"):
                    after(pool, "act", *step)
                    h = step[1]
                    a, _b = STAT["o", h]
                    a, m = (a, NP) if kind == "o" else (a + NP, 1)
                    s, r = stat[:, a:a + m], stat2[:, a:a + m]
                    link(pool.tensor_scalar(r, s, 1.0 / DV, EPS, MUL, ADD))
                    link(pool.tensor_tensor(r, r, minus_half[:, 0:m], ALU.pow))
                    last = pool.tensor_scalar(r, r, 0.5, None, MUL)
                elif kind == "r":
                    _, ph, t = step
                    after(pool, "act", "y" if t < NP else "ys", ph, 3)
                    s, r = S1(("y", ph, t)), S1(("yr", ph, t), stat2)
                    link(pool.tensor_tensor(s[:, 0:2], s[:, 0:2], s[:, 2:4], ADD))
                    link(pool.tensor_tensor(r, s[:, 0:1], s[:, 1:2], ADD))
                    link(pool.tensor_scalar(r, r, 1.0 / D, EPS, MUL, ADD))
                    last = pool.tensor_tensor(r, r, minus_half[:, 0:1], ALU.pow)
                elif kind == "rx":
                    after(pool, "act", "r", "A", step[1])
                    last = rms(("x1", step[1]), D, 1)
                elif kind in ("lc", "lcs"):
                    after(pool, "act", *step)
                    a, _b = STAT["lat",]
                    a, m = (a, NP) if kind == "lc" else (a + NP, 1)
                    s, r = stat[:, a:a + m], stat2[:, a:a + m]
                    link(pool.tensor_scalar(r, s, 1.0 / KL, EPS, MUL, ADD))
                    last = pool.tensor_tensor(r, r, minus_half[:, 0:m], ALU.pow)
                elif kind == "qs":
                    after(pool, "act", "qb")
                    s, r = S1(("qa",)), S1(("qa",), stat2)
                    link(pool.tensor_tensor(r, s, S1(("qb",)), ADD))
                    link(pool.tensor_scalar(r, r, 1.0 / QL, EPS, MUL, ADD))
                    last = pool.tensor_tensor(r, r, minus_half[:, 0:NT], ALU.pow)
                last.then_inc(done["pool"], 1)
                pool.wait_ge(done["pool"], AT["pool"][step])

        @block.scalar
        def _(act):
            def copy(out, in_):
                return act.activation(out, in_, ACT.Copy)

            act.wait_ge(consts_in, 32)
            for step in STEPS:
                if "act" not in parts(step):
                    continue
                kind = step[0]
                who = parts(step)[parts(step).index("act") - 1] if parts(step)[0] != "act" else None
                if who and who != "sp":
                    after(act, who, *step)
                bank, row = banks(step) if step in BANK_NO else (None, None)
                if kind == "const":
                    last = copy(const_r[:, :], junk[:, 0:NCONST_R])
                elif kind == "piece":
                    _, name, j = step
                    n = PIECE_NO[name, j]
                    if who == "sp":
                        act.wait_ge(stage_in[n % NSTAGE], STAGE_COUNT[n])
                    if SLAB_NO[name] >= 2:
                        after(act, "pe", *USERS[SLAB_NAMES[SLAB_NO[name] - 2]])
                    m = used(name, j)
                    last = copy(weights(name)[0][:, j * PIECE:j * PIECE + m], stage[n % NSTAGE][:, 0:m])
                elif kind == "xn":
                    t = step[1]
                    act.wait_ge(x_in[t], 16)
                    last = act.activation(junk[:, :], rows[:, t, :], ACT.Square, accum_out=S1(("x", t)))
                elif kind in ("xT", "oT"):
                    t = step[-1]
                    last = copy(hat[0][:, :, t * P:(t + 1) * P], row.rearrange("p (k n) -> p k n", n=P))
                elif kind == "glr":
                    act.wait_ge(ones_set, 1)
                    last = copy(glrT[0:RANK, :].rearrange("p (a n) -> p a n", a=2), bank[0:RANK, :, 0:HALF])
                elif kind == "z":
                    v = z_abs[:, step[1], :]
                    act.activation(v, bank[:, 0, :], ACT.Abs).then_inc(act_own, 1)
                    act.wait_ge(act_own, step[1] + 1)
                    last = act.activation(v, v, ACT.Exp, scale=-1.0)
                elif kind == "ln":
                    last = act.activation(z_abs[:, :, :], z_abs[:, :, :], ACT.Ln, bias=1.0)
                elif kind == "c":
                    t = step[1]
                    v = bank[:, :, 0:2 * (P + 2)].rearrange("p a (h n) -> p a h n", n=P + 2)
                    copy(cumT[:, :, t * P:(t + 1) * P].rearrange("p (a h) n -> p a h n", a=2), v[:, :, :, 0:P])
                    last = copy(decay[:, :, t:t + 1].rearrange("p (a h) n -> p a h n", a=2), v[:, :, :, P:P + 1])
                elif kind == "e":
                    h = step[1]
                    if h:
                        after(act, "dve", "k", h - 1)
                        after(act, "dve", "Us", h - 1, 1)
                    act.activation(Ep[:, :], cumT[:, h, :], ACT.Exp)
                    act.activation(Em[:, :], cumT[:, h, :], ACT.Exp, scale=-1.0)
                    last = act.activation(eB[:, :], decay[:, h, :], ACT.Exp)
                elif kind == "q":
                    last = copy(qT[0][:, :], tmp[:, :])
                elif kind == "k":
                    last = copy(kT[0][:, :], kt[:, :])
                elif kind == "sc":
                    last = copy(scT[0][:, :], tmp[:, :])
                elif kind == "v":
                    last = copy(vv[0][:, 0:NP, :], row.rearrange("p (t n) -> p t n", n=DV))
                elif kind == "vs":
                    copy(v_s[:, :], bank[:, 0, 0:DV])
                    last = copy(vv[0][:, NP, :], bank[:, 0, 0:DV])
                elif kind == "kT":
                    last = copy(kn[0][:, :, :], row[:, 0:TOK].rearrange("p (t n) -> p t n", n=DK))
                elif kind == "gt":
                    h = step[1]
                    if h:
                        after(act, "dve", "Slo", h - 1)
                        act.wait_ge(final_out, 16 * h)
                    last = act.activation(th, row, ACT.Tanh, scale=0.5)
                elif kind == "gts":
                    after(act, "dve", "gt", step[1])
                    last = act.activation(th[:, 0:DV], bank[:, 0, 0:DV], ACT.Tanh, scale=0.5)
                elif kind == "U":
                    last = copy(st[0][:, 1:, :], st_in[:, 1:, :])
                elif kind == "o":
                    for t in range(NP):
                        last = act.activation(junk[:, t * DV:(t + 1) * DV], row[:, t * DV:(t + 1) * DV], ACT.Square, accum_out=S1(("o", step[1]), t=t))
                elif kind == "os":
                    last = act.activation(junk[:, 0:DV], row[:, 0:DV], ACT.Square, accum_out=S1(("o", step[1]), t=NP))
                elif kind in ("y", "ys"):
                    _, ph, s = step
                    for i, t in enumerate(range(NP) if kind == "y" else [NP]):
                        last = act.activation(junk[:, i * 256:(i + 1) * 256], row[:, i * 256:(i + 1) * 256], ACT.Square, accum_out=S1(("y", ph, t), t=s))
                elif kind == "r":
                    if step[1] == "A":
                        t = step[2]
                        last = act.activation(junk[:, :], x1[:, t, :], ACT.Square, accum_out=S1(("x1", t)))
                    else:
                        last = copy(junk[:, 0:1], stat[:, 0:1])
                elif kind in ("lc", "lcs"):
                    for i, t in enumerate(range(NP) if kind == "lc" else [NP]):
                        last = act.activation(junk[:, i * KL:(i + 1) * KL], row[:, i * KL:(i + 1) * KL], ACT.Square, accum_out=S1(("lat",), t=t))
                elif kind == "cn":
                    after(act, "dve", "lcs")
                    last = copy(cn_s[0][:, :], ckvn[:, NP, :])
                elif kind == "cT":
                    t = step[1]
                    c = slice(t * P, (t + 1) * P)
                    copy(cT[0][:, :, c], bank[:, 0, 0:KL].rearrange("p (k n) -> p k n", n=P))
                    copy(krS[0:ROPE, c], bank[0:ROPE, 1, 0:P])
                    last = copy(krS[ROPE:P, c], bank[0:ROPE, 1, 0:P])
                elif kind in ("qa", "qas", "qb"):
                    m = QL - 256 if kind == "qb" else 256
                    for i, t in enumerate({"qa": range(NP), "qas": [NP], "qb": range(NT)}[kind]):
                        last = act.activation(junk[:, i * m:(i + 1) * m], row[:, i * m:(i + 1) * m], ACT.Square,
                                              accum_out=S1(("qb" if kind == "qb" else "qa",), t=t))
                elif kind == "qT":
                    t = step[1]
                    last = copy(qlT[0][:, :, t * P:(t + 1) * P], bank[:, 0, 0:QL].rearrange("p (k n) -> p k n", n=P))
                elif kind == "gb":
                    if step[1]:
                        after(act, "dve", "gbs", step[1] - 1)
                    last = act.activation(thb[:, :], row, ACT.Tanh, scale=0.5)
                elif kind == "gbs":
                    after(act, "dve", "gb", step[1])
                    last = act.activation(thb[:, 0:256], row[:, 0:256], ACT.Tanh, scale=0.5)
                elif kind == "qrT":
                    t = step[1]
                    if t == 0:
                        after(act, "dve", "gbs", 3)
                    last = copy(rotary_to(t, slice(0, ROPE)), rotary_from(row, t))
                elif kind == "qn":
                    if step[1] == 0:
                        after(act, "dve", "qr", NT - 1)
                    last = copy(qN[0][:, :].rearrange("p (a n) -> p a n", a=2), bank[:, :, 0:HALF])
                elif kind == "wt":
                    copy(wT[0][:, :], bank[:, 0, 0:KL])
                    last = copy(wT[1][:, :], bank[:, 1, 0:KL])
                elif kind == "kh":
                    last = copy(kN[0][:, :], bank[:, 0, :])
                elif kind == "vh":
                    last = copy(vN[0][:, :, :], bank[:, 0, :].rearrange("p (t n) -> p t n", n=VB))
                elif kind == "qabs":
                    last = copy(qab[0][:, :, :, step[1], :], by_stream(bank))
                elif kind == "S":
                    _, h, u = step
                    for j, (i, c0) in enumerate(zip(UNITS[u], (0, UNITS[u][0] + 1))):
                        last = act.activation(prob[u][:, c0:c0 + i + 1, :], bank[:, j, 0:(i + 1) * P].rearrange("p (s n) -> p s n", n=P),
                                              ACT.Exp, scale=SCALE, bias=S1(("S", h, u), stat2, j), accum_out=S1(("S", h, u), t=j))
                elif kind == "T":
                    last = copy(pT[0][:, :], row[:, 0:TOK])
                elif kind == "ct":
                    last = copy(sT[0][:, :, :], bank[:, :, :])
                elif kind == "cr":
                    copy(skS[0:ROPE, :], bank[0:ROPE, 0, :])
                    last = copy(skS[ROPE:P, :], bank[0:ROPE, 0, :])
                elif kind == "cs":
                    b = step[1]
                    act.wait_ge(cache_in[b % 2], 32 * (b // 2 + 1))
                    if b:
                        after(act, "pe", "sv", b - 1)
                    last = copy(cn[0][:, :, :], craw[b % 2][:, :, 0:KL])
                elif kind == "ss":
                    b = step[1]
                    last = act.activation(prob[b % 2][:, :, :], row[:, 0:TOK].rearrange("p (s n) -> p s n", n=P), ACT.Exp,
                                          scale=SCALE, bias=S1(("ss", b), stat2), accum_out=S1(("ss", b)))
                elif kind == "st":
                    last = copy(spT[0][:, :], row[:, 0:TOK])
                elif kind == "sv":
                    b = step[1]
                    for c in range(KC):
                        last = copy(ctxT[0][:, c, :, b * SL:(b + 1) * SL], bank[:, 0, c * P:(c + 1) * P].rearrange("p (h n) -> p h n", n=SL))
                last.then_inc(done["act"], 1)
                act.wait_ge(done["act"], AT["act"][step])

        @block.vector
        def _(dve):
            own = [0]

            def link(ins):
                own[0] += 1
                ins.then_inc(dve_own, 1)
                dve.wait_ge(dve_own, own[0])

            def tt(out, a, b, op):
                return dve.tensor_tensor(out, a, b, op)

            def low(lo, full, hi):
                return dve.tensor_tensor(lo, full, raw(hi), SUB)

            def rotate(out, src, tables, scratch):
                cos, sin = tables
                m = src.shape[1]
                t1, t2 = (scratch[:, i * m * RH:(i + 1) * m * RH].rearrange("p (m n) -> p m n", n=RH) for i in range(2))
                a, b = src[:, :, 0:RH], src[:, :, RH:ROPE]
                tt(t1, a, cos, MUL)
                link(tt(t2, b, sin, MUL))
                link(tt(out[:, :, 0:RH], t1, t2, SUB))
                tt(t1, b, cos, MUL)
                link(tt(t2, a, sin, MUL))
                return tt(out[:, :, RH:ROPE], t1, t2, ADD)

            dve.wait_ge(consts_in, 32)
            for step in STEPS:
                if "dve" not in parts(step):
                    continue
                kind = step[0]
                if parts(step)[0] != "dve":
                    after(dve, parts(step)[parts(step).index("dve") - 1], *step)
                bank, row = banks(step) if step in BANK_NO else (None, None)
                if kind == "piece":
                    _, name, j = step
                    m = used(name, j)
                    hi, lo = weights(name)
                    c = slice(j * PIECE, j * PIECE + m)
                    last = low(lo[:, c], stage[PIECE_NO[name, j] % NSTAGE][:, 0:m], hi[:, c])
                elif kind == "xn":
                    t = step[1]
                    last = dve.tensor_scalar(rows[:, t, :], rows[:, t, :], S1(("x", t), stat2), None, MUL)
                elif kind in ("xT", "oT"):
                    t = step[-1]
                    c = slice(t * P, (t + 1) * P)
                    last = low(hat[1][:, :, c], row.rearrange("p (k n) -> p k n", n=P), hat[0][:, :, c])
                elif kind == "z":
                    last = dve.tensor_scalar(z_min[:, step[1], :], bank[:, 0, :], 0.0, None, ALU.min)
                elif kind == "lg":
                    after(dve, "act", "ln")
                    t = step[1]
                    link(tt(z_min[:, t, :], z_min[:, t, :], z_abs[:, t, :], SUB))
                    link(dve.tensor_copy(lg[0][:, t, :], z_min[:, t, :]))
                    last = low(lg[1][:, t, :], z_min[:, t, :], lg[0][:, t, :])
                elif kind == "q":
                    h = step[1]
                    after(dve, "act", "e", h)
                    if h == 0:
                        after(dve, "act", "const")
                        dve.wait_ge(own_set, 1)
                    v = bank[:, :, 0:HALF]
                    link(dve.scalar_tensor_tensor(tmp[:, :].rearrange("p (a n) -> p a n", a=2), v, DK ** -0.5,
                                                  Ep[:, :].rearrange("p (a n) -> p a n", a=2), MUL, MUL))
                    for b in range(SB):
                        last = dve.tensor_copy(q_own[:, b, b * SL:(b + 1) * SL], tmp[:, SEQ + b * SL:SEQ + (b + 1) * SL])
                elif kind == "k":
                    last = tt(kt[:, :].rearrange("p (a n) -> p a n", a=2), bank[:, :, 0:HALF], Em[:, :].rearrange("p (a n) -> p a n", a=2), MUL)
                elif kind == "qlo":
                    after(dve, "act", "q", step[1])
                    last = low(qT[1][:, :], tmp[:, :], qT[0][:, :])
                elif kind == "klo":
                    after(dve, "act", "k", step[1])
                    last = low(kT[1][:, :], kt[:, :], kT[0][:, :])
                elif kind == "sc":
                    tt(tmp[:, 0:SEQ].rearrange("p (t n) -> p t n", n=P), bank[:, 0, :].rearrange("p (t n) -> p t n", n=P),
                       times(cst("mask_p"), NP), MUL)
                    last = tt(tmp[:, SEQ:TOK], bank[:, 1, 0:P], cst("mask_s"), MUL)
                elif kind == "sclo":
                    after(dve, "act", "sc", step[1])
                    last = low(scT[1][:, :], tmp[:, :], scT[0][:, :])
                elif kind == "v":
                    last = low(vv[1][:, 0:NP, :], row.rearrange("p (t n) -> p t n", n=DV), vv[0][:, 0:NP, :])
                elif kind == "vs":
                    last = low(vv[1][:, NP, :], v_s[:, :], vv[0][:, NP, :])
                elif kind == "kT":
                    low(kn[1][:, :, :], row[:, 0:TOK].rearrange("p (t n) -> p t n", n=DK), kn[0][:, :, :])
                    last = tt(k_own[:, :, :], times(bank[:, 1, 0:P], SB), over(cst("member"), DK), MUL)
                elif kind == "gt":
                    h = step[1]
                    last = dve.scalar_tensor_tensor(rows[:, 0:NP, h * DV:(h + 1) * DV], th.rearrange("p (t n) -> p t n", n=DV), 1.0,
                                                    row.rearrange("p (t n) -> p t n", n=DV), ADD, MUL)
                elif kind == "gts":
                    h = step[1]
                    last = dve.scalar_tensor_tensor(rows[:, NP, h * DV:(h + 1) * DV], th[:, 0:DV], 1.0, bank[:, 0, 0:DV], ADD, MUL)
                elif kind == "U":
                    if step[1]:
                        dve.wait_ge(final_out, 16 * step[1])
                    for t in range(NP):
                        e_end = Ep[:, t * P + P - 1:t * P + P]
                        u = row[:, t * DV:(t + 1) * DV]
                        nxt = (t + 1) % NP
                        if t:
                            link(tt(st_in[:, 0, :], u, st_in[:, t, :], ADD))
                            u = st_in[:, 0, :]
                        if t < NP - 1:
                            link(dve.tensor_scalar(st_in[:, nxt, :], u, e_end, eB[:, t + 1:t + 2], MUL, MUL))
                        else:
                            last = dve.tensor_scalar(st_in[:, 0, :], u, e_end, None, MUL)
                elif kind == "Slo":
                    after(dve, "act", "U", step[1])
                    last = low(st[1][:, 1:, :], st_in[:, 1:, :], st[0][:, 1:, :])
                elif kind == "Us":
                    _, h, j = step
                    dve.wait_ge(state_in, 16 * (h + 1))
                    v = st_s[:, 4 * j:4 * j + 4, :]
                    link(tt(v, row.rearrange("p (b n) -> p b n", n=DV), v, ADD))
                    for b in range(4 * j, 4 * j + 4):
                        e = Ep[:, SEQ + b * SL + SL - 1:SEQ + (b + 1) * SL]
                        last = dve.tensor_scalar(st_s[:, b, :], st_s[:, b, :], e, None, MUL)
                elif kind in ("o", "os"):
                    h = step[1]
                    for i, t in enumerate(range(NP) if kind == "o" else [NP]):
                        v = rows[:, t, h * DV:(h + 1) * DV]
                        last = dve.scalar_tensor_tensor(v, row[:, i * DV:(i + 1) * DV], S1(("o", h), stat2, t), v, MUL, MUL)
                elif kind in ("y", "ys"):
                    _, ph, s = step
                    t = slice(0, NP) if kind == "y" else slice(NP, NT)
                    m = NP if kind == "y" else 1
                    last = dve.tensor_copy(rows[:, t, s * 256:(s + 1) * 256], row[:, 0:m * 256].rearrange("p (t n) -> p t n", n=256))
                elif kind == "r":
                    _, ph, t = step
                    dve.wait_ge(rest_in, 32)
                    dve.wait_ge(post_in, 32 if ph == "A" else 48)
                    link(dve.scalar_tensor_tensor(rows[:, t, :], rows[:, t, :], S1(("yr", ph, t), stat2), post[:, :], MUL, MUL))
                    last = tt(x1[:, t, :], rows[:, t, :], x1[:, t, :], ADD)
                elif kind == "rx":
                    t = step[1]
                    last = dve.tensor_scalar(rows[:, t, :], x1[:, t, :], S1(("x1", t), stat2), None, MUL)
                elif kind in ("lc", "lcs"):
                    dve.wait_ge(state_out, 16 * HA)
                    dve.wait_ge(final_out, 16 * HA)
                    for i, t in enumerate(range(NP) if kind == "lc" else [NP]):
                        last = dve.scalar_tensor_tensor(ckvn[:, t, :], row[:, i * KL:(i + 1) * KL], S1(("lat",), stat2, t), lat_gain[:, :], MUL, MUL)
                elif kind == "lr":
                    v = bank[:, 0, 0:NT * ROPE].rearrange("p (t n) -> p t n", n=ROPE)
                    last = rotate(krn[:, :, :], v, [cst(n).rearrange("p (t n) -> p t n", n=RH) for n in ("cos", "sin")],
                                  prob[0][:, :, :].rearrange("p t n -> p (t n)"))
                elif kind == "cn":
                    last = low(cn_s[1][:, :], ckvn[:, NP, :], cn_s[0][:, :])
                elif kind == "cT":
                    t = step[1]
                    c = slice(t * P, (t + 1) * P)
                    low(cT[1][:, :, c], bank[:, 0, 0:KL].rearrange("p (k n) -> p k n", n=P), cT[0][:, :, c])
                    last = low(krL[:, c], bank[0:ROPE, 1, 0:P], krS[0:ROPE, c])
                elif kind in ("qa", "qas", "qb"):
                    c = slice(256, QL) if kind == "qb" else slice(0, 256)
                    m = c.stop - c.start
                    t = {"qa": slice(0, NP), "qas": slice(NP, NT), "qb": slice(0, NT)}[kind]
                    n = t.stop - t.start
                    last = dve.tensor_copy(qln[:, t, c], row[:, 0:n * m].rearrange("p (t n) -> p t n", n=m))
                elif kind == "qs":
                    for t in range(NT):
                        last = dve.tensor_scalar(qln[:, t, :], qln[:, t, :], S1(("qa",), stat2, t), None, MUL)
                elif kind == "qT":
                    t = step[1]
                    c = slice(t * P, (t + 1) * P)
                    last = low(qlT[1][:, :, c], bank[:, 0, 0:QL].rearrange("p (k n) -> p k n", n=P), qlT[0][:, :, c])
                elif kind in ("gb", "gbs"):
                    s = step[1]
                    t = slice(0, NP) if kind == "gb" else slice(NP, NT)
                    m = NP if kind == "gb" else 1
                    last = dve.scalar_tensor_tensor(rows[:, t, s * 256:(s + 1) * 256], thb[:, 0:m * 256].rearrange("p (t n) -> p t n", n=256),
                                                    1.0, row[:, 0:m * 256].rearrange("p (t n) -> p t n", n=256), ADD, MUL)
                elif kind == "qr":
                    t = step[1]
                    if t:
                        after(dve, "pe", "qrT", t - 1)
                    v = bank[:, 0, :].rearrange("p (h n) -> p h n", n=ROPE)
                    tables = [times(cst(n)[:, t * RH:(t + 1) * RH], HB) for n in ("cos", "sin")]
                    last = rotate(qrn[:, :].rearrange("p (h n) -> p h n", n=ROPE), v, tables, rtmp)
                elif kind == "qrT":
                    t = step[1]
                    last = low(rotary_to(t, slice(ROPE, P)), rotary_from(row, t), rotary_to(t, slice(0, ROPE)))
                elif kind == "qn":
                    last = low(qN[1][:, :].rearrange("p (a n) -> p a n", a=2), bank[:, :, 0:HALF], qN[0][:, :].rearrange("p (a n) -> p a n", a=2))
                elif kind == "kh":
                    last = low(kN[1][:, :], bank[:, 0, :], kN[0][:, :])
                elif kind == "vh":
                    last = low(vN[1][:, :, :], bank[:, 0, :].rearrange("p (t n) -> p t n", n=VB), vN[0][:, :, :])
                elif kind == "qabs":
                    last = low(qab[1][:, :, :, step[1], :], by_stream(bank), qab[0][:, :, :, step[1], :])
                elif kind == "S":
                    _, h, u = step
                    for j, i in enumerate(UNITS[u]):
                        ins = dve.reduce_max(S1(("S", h, u), t=j), bank[:, j, 0:(i + 1) * P], AX.X)
                    link(ins)
                    last = dve.tensor_scalar(S1(("S", h, u), stat2), S1(("S", h, u)), -SCALE, None, MUL)
                elif kind == "T":
                    last = low(pT[1][:, :], row[:, 0:TOK], pT[0][:, :])
                elif kind == "O":
                    _, h, u = step
                    r = S1(("S", h, u), stat2)
                    link(dve.reciprocal(r, S1(("S", h, u))))
                    link(dve.tensor_scalar(r, r, 0.5, None, MUL))
                    for j, t in enumerate(UNITS[u]):
                        v = rows[:, t, h * VB:(h + 1) * VB]
                        last = dve.scalar_tensor_tensor(v, bank[:, 0, j * VB:(j + 1) * VB], r[:, j:j + 1], v, MUL, MUL)
                elif kind == "ct":
                    last = low(sT[1][:, :, :], bank[:, :, :], sT[0][:, :, :])
                elif kind == "cr":
                    last = low(skL[:, :], bank[0:ROPE, 0, :], skS[0:ROPE, :])
                elif kind == "cs":
                    b = step[1]
                    last = low(cn[1][:, :, :], craw[b % 2][:, :, 0:KL], cn[0][:, :, :])
                elif kind == "ss":
                    b = step[1]
                    link(dve.reduce_max(S1(("ss", b)), row[:, 0:TOK], AX.X))
                    last = dve.tensor_scalar(S1(("ss", b), stat2), S1(("ss", b)), -SCALE, None, MUL)
                elif kind == "sn":
                    b = step[1]
                    after(dve, "act", "ss", b)
                    r = S1(("ss", b), stat2)
                    link(dve.reciprocal(r, S1(("ss", b))))
                    last = dve.tensor_scalar(prob[b % 2][:, :, :], prob[b % 2][:, :, :], r, 0.5, MUL, MUL)
                elif kind == "st":
                    last = low(spT[1][:, :], row[:, 0:TOK], spT[0][:, :])
                elif kind == "sv":
                    b = step[1]
                    for c in range(KC):
                        o = [x[:, c, :, b * SL:(b + 1) * SL] for x in ctxT]
                        last = low(o[1], bank[:, 0, c * P:(c + 1) * P].rearrange("p (h n) -> p h n", n=SL), o[0])
                elif kind == "so":
                    v = rows[:, NP, :]
                    last = tt(v, row, v, MUL)
                last.then_inc(done["dve"], 1)
                dve.wait_ge(done["dve"], AT["dve"][step])

        @block.tensor
        def _(pe):
            def mm3(out, a, b, first, last):
                pe.matmul(out, a[0], b[0], start=first, stop=False)
                pe.matmul(out, a[0], b[1], start=False, stop=False)
                return pe.matmul(out, a[1], b[0], start=False, stop=last)

            def cut(pair_, *idx):
                return tuple(x[idx] for x in pair_)

            A_ = slice(None)

            def natural(row, name, tiles, cols, kts, src, width=None, off=0, seg=None):
                w = seg or [x[:, 0:kts * cols].rearrange("p (k n) -> p k n", n=cols) for x in weights(name)]
                for i, t in enumerate(tiles):
                    for k in range(kts):
                        last = mm3(row[:, i * cols:(i + 1) * cols], cut(src, A_, k, slice(t * P, (t + 1) * P)),
                                   cut(w, A_, k), k == 0, k == kts - 1)
                return last

            def ready(name):
                after(pe, "dve", "piece", name, len(SLABS[name]) - 1)

            for step in STEPS:
                if "pe" not in parts(step):
                    continue
                kind = step[0]
                bank, row = before_bank(pe, step)
                if kind in ("xT", "oT"):
                    t = step[-1]
                    if kind == "oT":
                        ph = step[1]
                        after(pe, "dve", *((("Us", HA - 1, 1)) if ph == "A" else ("so",)))
                    else:
                        after(pe, "dve", *(("xn", t) if step[1] == "A" else ("rx", t)))
                    for k in range(KD):
                        last = pe.transpose(row[:, k * P:(k + 1) * P], rows[:, t, k * P:(k + 1) * P], ident)
                elif kind == "glr":
                    ready("glr")
                    after(pe, "dve", "xT", "A", NT - 1)
                    w = [x[:, 0:KD * RANK].rearrange("p (k n) -> p k n", n=RANK) for x in weights("glr")]
                    for a in range(2):
                        for k in range(KD):
                            last = mm3(bank[0:RANK, a, 0:HALF], cut(w, A_, k), cut(hat, A_, k, slice(a * HALF, (a + 1) * HALF)), k == 0, k == KD - 1)
                elif kind == "z":
                    t = step[1]
                    after(pe, "act", "glr")
                    pe.wait_ge(gate_in, 32)
                    last = pe.matmul(bank[:, 0, :], glrT[:, t * P:(t + 1) * P], gate_w[:, :], start=True, stop=True)
                elif kind == "c":
                    t = step[1]
                    after(pe, "dve", "lg", t)
                    after(pe, "act", "const")
                    m = cst_r("cum_p" if t < NP else "cum_s")
                    for h in range(HA):
                        o = bank[:, h // 2, (h % 2) * (P + 2):(h % 2 + 1) * (P + 2)]
                        pe.matmul(o, lg[0][:, t, h * DK:(h + 1) * DK], m, start=True, stop=False)
                        last = pe.matmul(o, lg[1][:, t, h * DK:(h + 1) * DK], m, start=False, stop=True)
                elif kind in ("q", "k"):
                    h = step[1]
                    after(pe, "dve", "piece", ("qk", h), 0 if kind == "q" else 1)
                    off = 0 if kind == "q" else PIECE
                    w = [x[:, off:off + KD * DK].rearrange("p (k n) -> p k n", n=DK) for x in weights(("qk", h))]
                    for a in range(2):
                        for k in range(KD):
                            last = mm3(bank[:, a, 0:HALF], cut(w, A_, k), cut(hat, A_, k, slice(a * HALF, (a + 1) * HALF)), k == 0, k == KD - 1)
                elif kind in ("v", "vs", "gt", "gts"):
                    name = ("v" if kind[0] == "v" else "g", step[1])
                    ready(name)
                    last = natural(row, name, [NP] if kind[-1] == "s" else range(NP), DV, KD, hat)
                elif kind == "kT":
                    after(pe, "dve", "k", step[1])
                    for t in range(NT):
                        last = pe.transpose(row[:, t * P:(t + 1) * P], kt[:, t * P:(t + 1) * P], ident)
                elif kind == "sc":
                    h = step[1]
                    after(pe, "dve", "klo", h)
                    for t in range(NT):
                        c = slice(t * P, (t + 1) * P)
                        last = mm3(row[:, c], cut(kT, A_, c), cut(qT, A_, c), True, True)
                elif kind == "U":
                    after(pe, "dve", "v", step[1])
                    after(pe, "dve", "kT", step[1])
                    for t in range(NP):
                        last = mm3(row[:, t * DV:(t + 1) * DV], cut(kn, A_, t), cut(vv, A_, t), True, True)
                elif kind == "Us":
                    _, h, j = step
                    after(pe, "act", "vs", h)
                    for b in range(4):
                        last = pe.matmul(row[:, b * DV:(b + 1) * DV], k_own[:, 4 * j + b, :], v_s[:, :], start=True, stop=True)
                elif kind == "o":
                    h = step[1]
                    after(pe, "dve", "sclo", h)
                    after(pe, "dve", "Slo", h)
                    for t in range(NP):
                        c = slice(t * P, (t + 1) * P)
                        o = row[:, t * DV:(t + 1) * DV]
                        last = mm3(o, cut(scT, A_, c), cut(vv, A_, t), True, t == 0)
                        if t:
                            last = mm3(o, cut(qT, A_, c), cut(st, A_, t), False, True)
                elif kind == "os":
                    h = step[1]
                    after(pe, "dve", "sclo", h)
                    after(pe, "dve", "vs", h)
                    pe.wait_ge(state_in, 16 * (h + 1))
                    c = slice(SEQ, TOK)
                    mm3(row[:, 0:DV], cut(scT, A_, c), cut(vv, A_, NP), True, False)
                    for b in range(SB):
                        last = pe.matmul(row[:, 0:DV], q_own[:, b, :], st_s[:, b, :], start=False, stop=b == SB - 1)
                elif kind in ("y", "ys"):
                    _, ph, s = step
                    ready(("wo", ph, s))
                    after(pe, "dve", "oT", ph, NT - 1)
                    last = natural(row, ("wo", ph, s), range(NP) if kind == "y" else [NP], 256, KD, hat)
                elif kind in ("lc", "lcs"):
                    ready("kvc")
                    after(pe, "dve", "xT", "B", NT - 1)
                    last = natural(row, "kvc", range(NP) if kind == "lc" else [NP], KL, KD, hat)
                elif kind == "lr":
                    ready("kvr")
                    last = natural(row, "kvr", range(NT), ROPE, KD, hat)
                elif kind == "cT":
                    t = step[1]
                    after(pe, "dve", "lr")
                    for c in range(KC):
                        pe.transpose(bank[:, 0, c * P:(c + 1) * P], ckvn[:, t, c * P:(c + 1) * P], ident)
                    last = pe.transpose(bank[0:ROPE, 1, 0:P], krn[:, t, :], ident)
                elif kind in ("qa", "qas"):
                    ready("ql0")
                    last = natural(row, "ql0", range(NP) if kind == "qa" else [NP], 256, KD, hat)
                elif kind == "qb":
                    ready("ql1")
                    last = natural(row, "ql1", range(NT), QL - 256, KD, hat)
                elif kind == "qT":
                    t = step[1]
                    after(pe, "dve", "qs")
                    for k in range(KQ):
                        last = pe.transpose(bank[:, 0, k * P:(k + 1) * P], qln[:, t, k * P:(k + 1) * P], ident)
                elif kind in ("gb", "gbs"):
                    s = step[1]
                    ready(("gb", s))
                    last = natural(row, ("gb", s), range(NP) if kind == "gb" else [NP], 256, KD, hat)
                elif kind == "qr":
                    t = step[1]
                    ready("uqr")
                    after(pe, "dve", "qT", NT - 1)
                    for g in range(2):
                        w = [x[:, g * PIECE:g * PIECE + KQ * 256].rearrange("p (k n) -> p k n", n=256) for x in weights("uqr")]
                        for k in range(KQ):
                            last = mm3(bank[:, 0, g * 256:(g + 1) * 256], cut(qlT, A_, k, slice(t * P, (t + 1) * P)), cut(w, A_, k), k == 0, k == KQ - 1)
                elif kind == "qrT":
                    t = step[1]
                    after(pe, "dve", "qr", t)
                    for h in range(HB):
                        last = pe.transpose(row[0:ROPE, h * P:(h + 1) * P], qrn[:, h * ROPE:(h + 1) * ROPE], ident)
                elif kind == "qn":
                    h = step[1]
                    ready(("hd", h))
                    w = [x[:, 0:KQ * NOPE].rearrange("p (k n) -> p k n", n=NOPE) for x in weights(("hd", h))]
                    for a in range(2):
                        for k in range(KQ):
                            last = mm3(bank[:, a, 0:HALF], cut(w, A_, k), cut(qlT, A_, k, slice(a * HALF, (a + 1) * HALF)), k == 0, k == KQ - 1)
                elif kind in ("wt", "kh", "vh"):
                    h = step[1]
                    off = KQ * NOPE + (KC * NOPE if kind == "vh" else 0)
                    w = [x[:, off:off + KC * P].rearrange("p (k n) -> p k n", n=P) for x in weights(("hd", h))]
                    if kind == "wt":
                        for i in range(2):
                            for c in range(KC):
                                last = pe.transpose(bank[:, i, c * P:(c + 1) * P], raw(w[i][:, c, :]), ident)
                    elif kind == "kh":
                        after(pe, "dve", "cT", NT - 1)
                        for c in range(KC):
                            last = mm3(bank[:, 0, :], cut(w, A_, c), cut(cT, A_, c, slice(0, SEQ)), c == 0, c == KC - 1)
                    else:
                        for t in range(NP):
                            for c in range(KC):
                                last = mm3(bank[:, 0, t * VB:(t + 1) * VB], cut(cT, A_, c, slice(t * P, (t + 1) * P)), cut(w, A_, c), c == 0, c == KC - 1)
                elif kind == "qabs":
                    h = step[1]
                    after(pe, "act", "wt", h)
                    after(pe, "dve", "qn", h)
                    for c in range(KC):
                        last = mm3(bank[:, 0, c * P:(c + 1) * P], cut(wT, A_, slice(c * P, (c + 1) * P)), cut(qN, A_, slice(SEQ, TOK)), True, True)
                elif kind == "S":
                    _, h, u = step
                    after(pe, "dve", "qn", h)
                    after(pe, "dve", "kh", h)
                    after(pe, "dve", "qrT", NT - 1)
                    for j, i in enumerate(UNITS[u]):
                        q, keys = slice(i * P, (i + 1) * P), slice(0, (i + 1) * P)
                        o = bank[:, j, keys]
                        mm3(o, cut(qN, A_, q), cut(kN, A_, keys), True, False)
                        pe.matmul(o, qS[:, h, q], krS[:, keys], start=False, stop=False)
                        pe.matmul(o, qS[0:ROPE, h, q], krL[:, keys], start=False, stop=False)
                        last = pe.matmul(bank[:, j, q], cst_r("early", 1), cst_r("late", 1), start=False, stop=True)
                elif kind == "T":
                    _, h, u = step
                    after(pe, "act", "S", h, u)
                    for s in range(NT):
                        last = pe.transpose(row[:, s * P:(s + 1) * P], prob[u][:, s, :], ident)
                elif kind == "O":
                    _, h, u = step
                    after(pe, "dve", "T", h, u)
                    after(pe, "dve", "vh", h)
                    for j, (i, c0) in enumerate(zip(UNITS[u], (0, UNITS[u][0] + 1))):
                        for s in range(i + 1):
                            last = mm3(bank[:, 0, j * VB:(j + 1) * VB], cut(pT, A_, slice((c0 + s) * P, (c0 + s + 1) * P)), cut(vN, A_, s), s == 0, s == i)
                elif kind == "ct":
                    b = step[1]
                    pe.wait_ge(cache_in[b % 2], 32 * (b // 2 + 1))
                    for c in range(KC):
                        for s in range(PAST // P):
                            last = pe.transpose(bank[:, c, s * P:(s + 1) * P], craw[b % 2][:, s, c * P:(c + 1) * P], ident)
                elif kind == "cr":
                    b = step[1]
                    for s in range(PAST // P):
                        last = pe.transpose(bank[0:ROPE, 0, s * P:(s + 1) * P], craw[b % 2][:, s, KL:KL + ROPE], ident)
                elif kind == "ss":
                    b = step[1]
                    after(pe, "dve", "cr", b)
                    after(pe, "dve", "qabs", HB - 1)
                    for o, keys, kr, kl in ((bank[:, 0, :], sT, skS[:, :], skL[:, :]),
                                            (bank[:, 1, 0:P], cut(cT, A_, A_, slice(SEQ, TOK)), krS[:, SEQ:TOK], krL[:, SEQ:TOK])):
                        for c in range(KC):
                            mm3(o, [x[:, c, b, :, :].rearrange("p h n -> p (h n)") for x in qab], cut(keys, A_, c), c == 0, False)
                        q = qS_s[:, b, :, :].rearrange("p h n -> p (h n)")
                        pe.matmul(o, q, kr, start=False, stop=False)
                        last = pe.matmul(o, q[0:ROPE, :], kl, start=False, stop=keys is sT)
                    a, _b = CONST_R["others"]
                    at = a + P - b * SL
                    last = pe.matmul(bank[:, 1, 0:P], cst_r("ones", 1), const_r[0:1, at:at + P], start=False, stop=True)
                elif kind == "st":
                    b = step[1]
                    after(pe, "dve", "sn", b)
                    for s in range(NT):
                        last = pe.transpose(row[:, s * P:(s + 1) * P], prob[b % 2][:, s, :], ident)
                elif kind == "sv":
                    b = step[1]
                    after(pe, "dve", "st", b)
                    after(pe, "dve", "cs", b)
                    after(pe, "dve", "cn")
                    for c in range(KC):
                        cc = slice(c * P, (c + 1) * P)
                        for s in range(NT):
                            rows_ = cut(cn, A_, s, cc) if s < NT - 1 else cut(cn_s, A_, cc)
                            last = mm3(bank[:, 0, cc], rows_, cut(spT, A_, slice(s * P, (s + 1) * P)), s == 0, s == NT - 1)
                elif kind == "so":
                    ready("uv")
                    after(pe, "dve", "sv", SB - 1)
                    w = [x[:, :].rearrange("p (k n) -> p k n", n=HB * VB) for x in weights("uv")]
                    for h in range(HB):
                        for c in range(KC):
                            last = mm3(row[:, h * VB:(h + 1) * VB], cut(ctxT, A_, c, h), cut(w, A_, c, slice(h * VB, (h + 1) * VB)), c == 0, c == KC - 1)
                last.then_inc(done["pe"], 1)


_INS = ["x_prompt", "x_sample", "state_gla", "cache_ckv", "cache_krope", "a_norm_pre", "a_w_in", "a_w_gate2", "a_b_gate",
        "a_head_norm", "a_w_out", "a_norm_post", "kv_norm", "kv_w_down", "kv_latent_norm", "kv_w_uk", "kv_w_uv",
        "b_norm_pre", "b_w_in", "b_q_norm", "b_w_uq", "b_w_out", "b_norm_post"]
_GAINS = ["a_norm_pre", "a_head_norm", "kv_norm", "b_norm_pre", "b_q_norm"]
_OUTS = [(1, SEQ, D), (SB, SL, D), (1, 1, HA, DK, DV), (1, SB, HA, DK, DV), (1, SEQ, KL), (1, SEQ, ROPE), (SB, SL, KL), (SB, SL, ROPE)]


def constants():
    import numpy as np
    i = np.arange(P)
    before = (i[:, None] <= i[None, :]).astype(np.float32)
    same = (i[:, None] // SL == i[None, :] // SL).astype(np.float32)
    half = (i < P // 2).astype(np.float32)[:, None]
    tau = np.float32(1.0 / 16.0)
    cum_p = np.zeros((P, P + 2), np.float32)
    cum_p[:, :P] = (before - half) * tau
    cum_p[:, P:P + 1] = half * tau
    cum_s = np.zeros((P, P + 2), np.float32)
    cum_s[:, :P] = before * same * tau
    pos = np.concatenate([np.arange(SEQ), PAST + np.arange(P) % SL]).astype(np.float32)
    inv = np.power(np.float32(10000.0), -np.arange(RH, dtype=np.float32) / np.float32(RH)).astype(np.float32)
    ang = (pos[:, None] * inv[None, :]).reshape(NT, P, RH).transpose(1, 0, 2).reshape(P, NT * RH)
    row = np.ones((P, 1), np.float32)
    others = np.full(2 * P, NEG, np.float32)
    others[P:P + SL] = 0.0
    const = [np.eye(P), before, before * same, (i[:, None] // SL == np.arange(SB)[None, :]), np.cos(ang), np.sin(ang)]
    const_r = [cum_p, cum_s, row * (1 - half.T * 0 - (i >= P // 2)[None, :]), row * np.where(i >= P // 2, NEG, 0.0)[None, :], row * np.ones((1, P)), row * others[None, :]]
    return [np.ascontiguousarray(np.concatenate(x, axis=1).astype(np.float32)) for x in (const, const_r)]


def kernel(**inputs):
    import numpy as _np
    import concourse.bacc as _bacc
    from concourse import mybir as _mybir
    from concourse.bass_utils import run_bass_kernel_spmd as _run

    nc = _bacc.Bacc("TRN2", target_bir_lowering=False, num_devices=1)
    arrays, dram = {}, {}
    data = {name: _np.ascontiguousarray(inputs[name]) for name in _INS}
    data["const"], data["const_r"] = constants()
    for name in _GAINS:
        data[name] = _np.ascontiguousarray(data[name].reshape(-1, P).T)
    for name, a in data.items():
        arrays[f"in_{name}_dram"] = a
        dram[name] = nc.dram_tensor(f"in_{name}_dram", a.shape, _mybir.dt.from_np(a.dtype), kind="ExternalInput").ap()
    outs = [nc.dram_tensor(f"out_{i}_dram", shape, _mybir.dt.float32, kind="ExternalOutput").ap() for i, shape in enumerate(_OUTS)]
    program(nc, dram, outs)
    r = _run(nc, [arrays], core_ids=[0])
    return tuple(r.results[0][f"out_{i}_dram"] for i in range(len(_OUTS)))
```

```python
import concourse.bass as bass
from concourse import mybir
from contextlib import ExitStack

P = 128
D = 1024
KD = D // P
SEQ = 512
SB, SL = 8, 16
PAST = 512
NP = SEQ // P
NT = NP + 1
TOK = NT * P
HALF = TOK // 2
HA, DK, DV = 4, 128, 256
RANK = 16
HB, NOPE, ROPE, VB = 8, 128, 64, 128
RH = ROPE // 2
QL, KL = 384, 256
KQ, KC = QL // P, KL // P
EPS = 1e-6
NEG = -float(2 ** 120)
SCALE = (NOPE + ROPE) ** -0.5
PIECE = 1024
NSTAGE = 3
NBANK = 4

def columns(sizes):
    out, at = {}, 0
    for name, n in sizes:
        out[name] = (at, at + n)
        at += n
    return out, at


CONST, NCONST = columns((("ident", P), ("mask_p", P), ("mask_s", P), ("member", SB), ("cos", NT * RH), ("sin", NT * RH)))
CONST_R, NCONST_R = columns((("cum_p", P + 2), ("cum_s", P + 2), ("early", P), ("late", P), ("ones", P), ("others", 2 * P)))


def slabs():
    def halves(w, base, gain):
        return [[(w, k, k + 4, base, 256, gain)] for k in (0, 4)]

    def nope(h):
        return ("b_w_uq", 0, KQ, h * (NOPE + ROPE), NOPE, "b_q_norm"), ("kv_w_uk", 0, KC, h * NOPE, NOPE, None)

    out = {"glr": [[("a_w_in", 0, KD, 2 * HA * DK + 2 * HA * DV, RANK, "a_norm_pre")]]}
    for h in range(HA):
        qk = [[("a_w_in", 0, KD, h * DK, DK, "a_norm_pre")], [("a_w_in", 0, KD, (HA + h) * DK, DK, "a_norm_pre")]]
        v, g = (halves("a_w_in", base + h * DV, "a_norm_pre") for base in (2 * HA * DK, 2 * HA * DK + HA * DV))
        for name, x in ((("v", h), v), (("qk", h), qk), (("g", h), g)) if h == 0 else ((("qk", h), qk), (("v", h), v), (("g", h), g)):
            out[name] = x
    for s in range(4):
        out["wo", "A", s] = halves("a_w_out", s * 256, "a_head_norm")
    out["kvc"] = halves("kv_w_down", 0, "kv_norm")
    out["kvr"] = [[("kv_w_down", 0, KD, KL, ROPE, "kv_norm")]]
    out["ql0"] = halves("b_w_in", 0, "b_norm_pre")
    out["ql1"] = [[("b_w_in", 0, KD, 256, 128, "b_norm_pre")]]
    gb = {("gb", s): halves("b_w_in", QL + s * 256, "b_norm_pre") for s in range(4)}
    uqr = [[("uq_rope", 0, KQ, h * ROPE, 4 * ROPE, "b_q_norm")] for h in (0, 4)]
    pre = {("pre", p): [list(nope(2 * p + i)) for i in range(2)] for p in range(HB // 2)}
    for name in (("gb", 3), ("gb", 2), "uqr", ("pre", 0), ("gb", 1), ("pre", 1), ("gb", 0), ("pre", 2), ("pre", 3)):
        out[name] = uqr if name == "uqr" else gb.get(name) or pre[name]
    for h in range(HB):
        out["hd", h] = [[*nope(h), ("kv_w_uv", h % 2, h % 2 + 1, (h // 2) * 2 * VB, 2 * VB, None)]]
    out["uv"] = [[("kv_w_uv", k, k + 1, 0, HB * VB, None)] for k in range(KC)]
    for s in range(4):
        out["wo", "B", s] = halves("b_w_out", s * 256, None)
    return out


SLABS = slabs()
SLAB_NO = {name: n for n, name in enumerate(SLABS)}
PIECES = [(name, j) for name, pieces in SLABS.items() for j in range(len(pieces))]
PIECE_NO = {p: n for n, p in enumerate(PIECES)}
SLAB_NAMES = list(SLABS)


def stage_counts():
    count, out = [0] * NSTAGE, []
    for n, (name, j) in enumerate(PIECES):
        for w, k0, k1, *_ in SLABS[name][j]:
            count[n % NSTAGE] += 16 * (k1 - k0 if w == "uq_rope" else 1)
        out.append(count[n % NSTAGE])
    return out


STAGE_COUNT = stage_counts()


def steps():
    out = []

    def load(name):
        out.extend(("piece", name, j) for j in range(len(SLABS[name])))

    out += [("const",), ("xn", 0), ("xn", 1)]
    load("glr")
    for t in range(NT):
        out += [("xT", "A", t)]
        if t + 2 < NT:
            out += [("xn", t + 2)]
    load(("v", 0))
    out += [("glr",)]
    load(("qk", 0))
    for t in range(NT):
        out += [("z", t)]
    out += [("ln",), ("v", 0), ("vs", 0)]
    for t in range(NT):
        out += [("lg", t), ("c", t)]
    out += [("lds", 0)]
    for h in range(HA):
        last = h + 1 == HA
        out += [("e", h), ("q", h), ("k", h), ("qlo", h), ("klo", h)]
        load(("g", h))
        if h:
            out += [("v", h)]
        out += [("kT", h)]
        if h:
            out += [("vs", h)]
        else:
            out += [("gt", h)]
        out += [("sc", h)]
        load(("wo", "A", 0) if last else ("qk", h + 1))
        if h:
            out += [("gt", h)]
        out += [("gts", h), ("sclo", h), ("U", h), ("Slo", h)]
        load(("wo", "A", 1) if last else ("v", h + 1))
        out += [("stp", h), ("os", h), ("o", h), ("Us", h, 0), ("Us", h, 1), ("sts", h)]
        if not last:
            out += [("lds", h + 1)]
    out += [("ldr",)]
    project_out(out, load, "A")
    latent_layer(out, load)
    project_out(out, load, "B")
    return out


def project_out(out, load, ph):
    if ph == "A":
        out += [("oT", ph, t) for t in range(NT)]
    for s in range(2):
        out += [("y", ph, s), ("ys", ph, s)]
        load(("wo", ph, s + 2))
    for t in range(NT + 2):
        if t < NT:
            out += [("yt", ph, t)]
        if ph == "A" and t >= 2:
            out += [("xT", "B", t - 2)]
        if ph == "A" and 0 <= t - 1 < NT:
            out += [("rx", t - 1)]
        if t < NT:
            out += [("r", ph, t), ("keep", t) if ph == "A" else ("oy", t)]
        if ph == "A" and t == NT - 1:
            load("kvc")
            load("kvr")


def latent_layer(out, load):
    out += [("lc",), ("lcs",)]
    load("ql0")
    out += [("lr",)]
    load("ql1")
    out += [("cn",), ("och",), ("qa",), ("qas",)]
    load(("gb", 3))
    out += [("qb",), ("qs",)]
    load(("gb", 2))
    out += [("gb", 3, 0), ("cT", 0), ("cT", 1), ("gb", 3, 1), ("cT", 2), ("cT", 3), ("cT", 4)]
    load("uqr")
    out += [("gb", 2, 0)] + [("qT", t) for t in range(NT)] + [("gb", 2, 1)]
    load(("pre", 0))
    out += [("qr", 0), ("qr", 1), ("qrT", 0), ("qr", 2), ("qrT", 1), ("qr", 3), ("qrT", 2), ("qr", 4)]
    load(("gb", 1))
    out += [("qns", 0), ("wt", 0), ("qrT", 3)]
    load(("pre", 1))
    out += [("gb", 1, 0), ("qrT", 4), ("qabs", 0), ("gb", 1, 1)]
    load(("gb", 0))
    out += [("qns", 1), ("wt", 1)]
    load(("pre", 2))
    out += [("gb", 0, 0), ("qabs", 1), ("gb", 0, 1)]
    load(("pre", 3))
    out += [("qns", 2), ("wt", 2)]
    load(("hd", 0))
    out += [("ldc", 0), ("ldc", 1), ("qabs", 2), ("qns", 3), ("wt", 3)]
    load(("hd", 1))
    out += [("ct", 0), ("cr", 0), ("qn", 0), ("kh", 0), ("vh", 0), ("qabs", 3)]
    for h in range(HB):
        more = h + 1 < HB
        out += [("S", h, 0), ("S", h, 1), ("ss", h), ("cs", h), ("N", h, 0), ("N", h, 1)]
        if h:
            out += [("cx", h - 1)]
        if more:
            out += [("qn", h + 1)]
        out += [("T", h, 0), ("T", h, 1), ("st", h)]
        if more:
            out += [("kh", h + 1)]
            load(("hd", h + 2) if h + 2 < HB else "uv")
        out += [("sv", h)] if not more else []
        out += [("O", h), ("Oh", h)]
        if more:
            out += [("ct", h + 1), ("cr", h + 1)]
            if h + 2 < HB:
                out += [("ldc", h + 2)]
            if h % 2:
                out += [("vh", h // 2 + 1)]
            out += [("sv", h)]
    out += [("cx", SB - 1), ("ldk",)]
    load(("wo", "B", 0))
    out += [("so",), ("soh",)]
    load(("wo", "B", 1))


PARTS = {
    "const": ("act",), "piece": ("sp", "pool", "act", "dve"), "lds": ("sp",), "sts": ("sp",), "stp": ("sp",), "ldr": ("sp",),
    "och": ("sp",), "ldc": ("sp",), "oy": ("sp",), "keep": ("sp",), "ldk": ("sp",), "yt": ("pe", "act"), "qns": ("pe", "act", "dve"), "xn": ("act", "pool", "dve"), "xT": ("pe", "act", "dve"), "glr": ("pe", "act"),
    "z": ("pe", "dve", "act"), "ln": ("act",), "lg": ("dve",), "c": ("pe", "act"), "e": ("act",),
    "q": ("pe", "dve", "act"), "k": ("pe", "dve", "act"), "qlo": ("dve",), "klo": ("dve",),
    "v": ("pe", "act", "dve"), "vs": ("pe", "act", "dve"), "kT": ("pe", "act", "dve"), "sc": ("pe", "dve", "act"),
    "sclo": ("dve",), "gt": ("pe", "act", "dve"), "gts": ("pe", "act", "dve"), "U": ("pe", "dve", "act"),
    "Slo": ("dve",), "os": ("pe", "act", "pool", "dve"), "o": ("pe", "act", "pool", "dve"), "Us": ("pe", "dve"),
    "oT": ("pe", "act", "dve"), "y": ("pe", "act", "dve"), "ys": ("pe", "act", "dve"), "r": ("pool", "dve", "act"),
    "rx": ("pool", "dve"), "lc": ("pe", "act", "pool", "dve"), "lcs": ("pe", "act", "pool", "dve"), "lr": ("pe", "dve"),
    "cn": ("act", "dve"), "cT": ("pe", "act", "dve"), "qa": ("pe", "act", "dve"), "qas": ("pe", "act", "dve"),
    "qb": ("pe", "act", "dve"), "qs": ("pool", "dve"), "gb": ("pe", "act", "dve"),
    "qT": ("pe", "act", "dve"), "qr": ("pe", "dve"), "qrT": ("pe", "act", "dve"), "qn": ("pe", "act", "dve"),
    "wt": ("pe", "act"), "N": ("dve",), "Oh": ("act", "dve"), "cx": ("pe", "act", "dve"), "soh": ("act", "dve"), "kh": ("pe", "act", "dve"), "vh": ("pe", "act", "dve"), "qabs": ("pe", "act", "dve"),
    "S": ("pe", "dve", "act"), "T": ("pe", "act", "dve"), "O": ("pe", "dve"), "ct": ("pe", "act", "dve"),
    "cr": ("pe", "act", "dve"), "ss": ("pe", "dve", "act"), "cs": ("pool",), 
    "st": ("pe", "act", "dve"), "sv": ("pe", "dve"), "so": ("pe", "dve"),
}
def parts(step):
    if step[0] == "piece" and not any(w[5] for w in SLABS[step[1]][step[2]]):
        return ("sp", "act", "dve")
    return PARTS[step[0]]


LAST_READER = {k: [e for e in p if e in ("act", "dve")][-1] for k, p in PARTS.items() if "pe" in p}
LAST_READER.update({k: "dve" for k in ("q", "k", "sc", "U")})
LAST_READER["S"] = LAST_READER["ss"] = LAST_READER["z"] = "act"

STEPS = steps()
assert len(set(STEPS)) == len(STEPS)


def count_parts():
    at = {e: {} for e in ("pe", "act", "dve", "pool")}
    for s in STEPS:
        for e in at.keys() & set(parts(s)):
            at[e][s] = len(at[e]) + 1
    return at


AT = count_parts()


def read_out(step):
    return ("dve", "r", *step[1:]) if step[0] == "yt" else (LAST_READER[step[0]], *step)


BANKED = [s for s in STEPS if "pe" in PARTS[s[0]]]
BANK_NO = {s: n for n, s in enumerate(BANKED)}
USERS = {"glr": ("glr",), "kvc": ("lcs",), "kvr": ("lr",), "ql0": ("qas",), "ql1": ("qb",), "uqr": ("qr", NT - 1), "uv": ("so",)}
for _h in range(HA):
    USERS["qk", _h], USERS["v", _h], USERS["g", _h] = ("k", _h), ("vs", _h), ("gts", _h)
for _ph in "AB":
    for _s in range(4):
        USERS["wo", _ph, _s] = ("ys", _ph, _s) if _s < 2 else ("yt", _ph, NT - 1)
for _s in range(4):
    USERS["gb", _s], USERS["pre", _s] = ("gb", _s, 1), ("wt", _s)
for _h in range(HB):
    USERS["hd", _h] = ("kh", _h) if _h % 2 else ("vh", _h // 2)

STAT = {}
for _name, _n in [(("x", t), 1) for t in range(NT)] + [(("x1", t), 1) for t in range(NT)] \
        + [(("o", h), NT) for h in range(HA)] + [(("y", ph, t), 4) for ph in "AB" for t in range(NT)] \
        + [(("yr", ph, t), 1) for ph in "AB" for t in range(NT)] + [(("lat",), NT), (("qa",), NT), (("qb",), NT)] \
        + [(("S", h, u), 2) for h in range(HB) for u in range(2)] + [(("ss", b), 1) for b in range(SB)]:
    STAT[_name] = (sum(b - a for a, b in STAT.values()), sum(b - a for a, b in STAT.values()) + _n)
NSTAT = max(b for _, b in STAT.values())

UNITS = ((3, 0), (2, 1))
KEY_UNITS = ((0, 3), (1, 2))


def program(nc, dram, outs):
    fp32, fp32r = mybir.dt.float32, mybir.dt.float32r
    ALU, ACT, AX = mybir.AluOpType, mybir.ActivationFunctionType, mybir.AxisListType
    MUL, ADD, SUB = ALU.mult, ALU.add, ALU.subtract
    (y_prompt, y_sample, st_prompt, st_sample, ckv_prompt, krope_prompt, ckv_sample, krope_sample) = outs
    kept = nc.dram_tensor("kept_rows", (P, NT, D), fp32, kind="Internal").ap()
    w_dram = {n: dram[n].rearrange("(k p) n -> p k n", p=P) for n in
              ("kv_w_down", "kv_w_uk", "kv_w_uv")}
    for n in ("a_w_in", "a_w_out", "b_w_in", "b_w_uq", "b_w_out"):
        w_dram[n] = dram[n][0].rearrange("(k p) n -> p k n", p=P)
    uq_rope = w_dram["b_w_uq"].rearrange("p k (h n) -> p k h n", n=NOPE + ROPE)

    ctx = ExitStack()
    with ctx:
        def sem(name):
            return ctx.enter_context(nc.semaphore(name))

        place = [-(-nc.sbuf_base // 64) * 64]

        def sb(name, shape, dt=fp32):
            size = 4
            for n in shape[1:]:
                size *= n
            at = place[0]
            place[0] += -(-size // 32) * 32
            assert place[0] <= nc.sbuf_usable_end, (name, place[0])
            return nc.alloc_sbuf_tensor_at(name, shape, dt, offset=at)

        def pair(name, shape):
            return sb(name + "_hi", shape, fp32r), sb(name + "_lo", shape, fp32r)

        def raw(ap):
            return ap.bitcast(fp32)

        def over(ap, n):
            return ap.unsqueeze(2).to_broadcast([ap.shape[0], ap.shape[1], n])

        def times(ap, n):
            return ap.unsqueeze(1).to_broadcast([ap.shape[0], n, ap.shape[1]])

        stage = [sb(f"stage{i}", [P, PIECE]) for i in range(NSTAGE)]
        slab_at = [place[0] + 8 * PIECE * i for i in range(4)]
        slab = [pair(f"slab{i}", [P, 2 * PIECE]) for i in range(2)]
        const = sb("const", [P, NCONST])
        const_r = sb("const_r", [P, NCONST_R], fp32r)
        gain = {n: sb("gain_" + n, [P, k]) for n, k in
                (("a_norm_pre", KD), ("a_head_norm", KD), ("kv_norm", KD), ("b_norm_pre", KD), ("b_q_norm", KQ))}
        post = sb("post", [P, D])
        lat_gain = sb("lat_gain", [P, KL])
        minus_half = sb("minus_half", [P, 8])
        stat = sb("stat", [P, NSTAT])
        stat2 = sb("stat2", [P, NSTAT])
        junk = sb("junk", [P, D])
        rows_at = place[0]
        rows = sb("rows", [P, NT, D])
        gate_at = place[0]
        gate_w = sb("gate_w", [RANK + 1, HA * DK])
        hat_at = place[0]
        hat = pair("hat", [P, KD, TOK])
        phase_at = place[0]
        glrT = sb("glrT", [RANK + 1, TOK])
        cumT = sb("cumT", [P, HA, TOK])
        decay = sb("decay", [P, HA, NT])
        Ep, Em = sb("Ep", [P, TOK]), sb("Em", [P, TOK])
        eB = sb("eB", [P, NT])
        ec = sb("ec", [P, NP])
        tmp, kt = sb("tmp", [P, TOK]), sb("kt", [P, TOK])
        vv = pair("vv", [P, NT, DV])
        v_s = sb("v_s", [P, DV])
        z_at = place[0]
        qT, kT = pair("qT", [P, TOK]), pair("kT", [P, TOK])
        kn = pair("kn", [P, NT, DK])
        scT = pair("scT", [P, TOK])
        st_in = sb("st_in", [P, NP, DV])
        st = pair("st", [P, NP, DV])
        st_s = sb("st_s", [P, SB, DV])
        k_own = sb("k_own", [P, SB, DK])
        q_own = sb("q_own", [P, SB, P])
        th = st_in[:, :, :].rearrange("p t n -> p (t n)")
        place[0] = z_at
        z_abs, z_min = sb("z_abs", [P, NT, HA * DK]), sb("z_min", [P, NT, HA * DK])
        lg = pair("lg", [P, NT, HA * DK])
        const_raw = sb("const_raw", [P, NCONST_R])
        place[0] = phase_at
        qS_at = place[0]
        x1 = sb("x1", [P, NT, D])
        qlT_at = place[0]
        qlT = pair("qlT", [P, KQ, TOK])
        cT = pair("cT", [P, KC, TOK])
        krS = sb("krS", [P, TOK], fp32r)
        krL = sb("krL", [ROPE, TOK], fp32r)
        cn_s = pair("cn_s", [P, KL])
        qab = pair("qab", [P, KC, SB, HB * SL])
        temp_at = place[0]
        ckvn = sb("ckvn", [P, NT, KL])
        krn = sb("krn", [P, NT, ROPE])
        thb = sb("thb", [P, 2 * TOK])
        wT = pair("wT", [P, 2 * KL])
        qN_s = pair("qN_s", [P, 2 * P])
        flat_rows = rows[:, :, :].rearrange("p t d -> p (t d)")
        qln = flat_rows[:, 0:NT * QL].rearrange("p (t n) -> p t n", n=QL)
        gateT = flat_rows.rearrange("p (h n) -> p h n", n=TOK)
        place[0] = rows_at
        oT_lo = sb("oT_lo", [P, HB, TOK], fp32r)
        place[0] = qlT_at
        y_rows = sb("y_rows", [P, NT, D])
        place[0] = qS_at
        qS = sb("qS", [P, HB, SEQ], fp32r)
        qS_s_at = place[0]
        qS_s = sb("qS_s", [P, SB, HB, SL], fp32r)
        place[0] = qS_s_at
        oS_s = sb("oS_s", [P, HB, P], fp32r)
        place[0] = temp_at
        qrn, rtmp = sb("qrn", [P, HB * ROPE]), sb("rtmp", [P, HB * ROPE])
        place[0] = temp_at
        pT = [pair(f"pT{i}", [P, TOK]) for i in range(2)]
        prob = [sb(f"prob{i}", [P, NT, P]) for i in range(2)]
        place[0] = hat_at
        qN = pair("qN", [P, SEQ])
        kN = pair("kN", [P, SEQ])
        sT = pair("sT", [P, KC, PAST])
        cn = pair("cn", [P, PAST // P, KL])
        spT = pair("spT", [P, TOK])
        skS = sb("skS", [P, PAST], fp32r)
        skL = sb("skL", [ROPE, PAST], fp32r)
        sprob = sb("sprob", [P, NT, P])
        ctxn = sb("ctxn", [P, KL])
        assert place[0] <= phase_at
        place[0] = hat_at
        xB = sb("xB", [P, NT, D])
        place[0] = slab_at[2] + 4 * PIECE
        vN_hi = sb("vN_hi", [P, NP, 2 * VB], fp32r)
        place[0] = slab_at[3] + 4 * PIECE
        vN_lo = sb("vN_lo", [P, NP, 2 * VB], fp32r)
        vN = (vN_hi, vN_lo)
        craw = []
        for i in range(2):
            place[0] = slab_at[i] + 4 * PIECE
            craw.append(sb(f"craw{i}", [P, PAST // P, KL]))
        place[0] = gate_at
        kraw = [sb(f"kraw{i}", [P, PAST // P, ROPE]) for i in range(2)]

        pb = [ctx.enter_context(nc.psum_tensor(f"bank{i}", [P, 2, 512], fp32)) for i in range(NBANK)]
        flat = [b[:, :, :].rearrange("p a n -> p (a n)") for b in pb]

        def cst(name, p=P):
            a, b = CONST[name]
            return const[0:p, a:b]

        def cst_r(name, p=P):
            a, b = CONST_R[name]
            return const_r[0:p, a:b]

        ident = cst("ident")

        def rotary_to(t, p):
            return qS[p, :, t * P:(t + 1) * P] if t < NP else qS_s[p, :, :, :].rearrange("p b h n -> p h b n")

        def rotary_from(row, t):
            v = row[0:ROPE, :].rearrange("p (h n) -> p h n", n=P)
            return v if t < NP else v.rearrange("p h (b n) -> p h b n", n=SL)

        def by_stream(x, h):
            return x.rearrange("p k b (h n) -> p k b h n", n=SL)[:, :, :, h, :]

        def S1(name, src=None, t=None):
            a, b = STAT[name]
            src = stat if src is None else src
            return src[:, a:b] if t is None else src[:, a + t:a + t + 1]

        done = {"pe": sem("tensor_done"), "act": sem("scalar_done"), "dve": sem("vector_done"), "pool": sem("gpsimd_done")}
        act_own, dve_own, pool_own = sem("scalar_own"), sem("vector_own"), sem("gpsimd_own")
        consts_in, x_in, gains_in = sem("consts_in"), [sem(f"x{t}_in") for t in range(NT)], sem("gains_in")
        stage_in = [sem(f"stage{i}_in") for i in range(NSTAGE)]
        state_in, state_out, final_out, rest_in, post_in = sem("state_in"), sem("state_out"), sem("final_out"), sem("rest_in"), sem("post_in")
        cache_in = [sem(f"cache{i}_in") for i in range(2)]
        latent_out, y_out, kept_out = sem("latent_out"), sem("y_out"), sem("kept_out")
        ones_set, own_set, gate_in = sem("ones_set"), sem("own_set"), sem("gate_in")

        def after(eng, who, *step):
            eng.wait_ge(done[who], AT[who][step])

        def before_bank(eng, step):
            n = BANK_NO[step]
            if n >= NBANK:
                after(eng, *read_out(BANKED[n - NBANK]))
            return pb[n % NBANK], flat[n % NBANK]

        def banks(step):
            n = BANK_NO[step] % NBANK
            return pb[n], flat[n]

        def weights(name):
            return slab[SLAB_NO[name] % 2]

        def used(name, j):
            return sum((w[2] - w[1]) * w[4] for w in SLABS[name][j])

        block = ctx.enter_context(nc.Block())

        @block.sync
        def _(sp):
            def load_piece(name, j):
                n = PIECE_NO[name, j]
                if n >= NSTAGE:
                    after(sp, "dve", "piece", *PIECES[n - NSTAGE])
                at = 0
                for w, k0, k1, c0, nc_, _g in SLABS[name][j]:
                    size = (k1 - k0) * nc_
                    if w == "uq_rope":
                        h0 = c0 // ROPE
                        for k in range(k0, k1):
                            sp.dma_start(stage[n % NSTAGE][:, at + k * nc_:at + (k + 1) * nc_].rearrange("p (h n) -> p h n", n=ROPE),
                                         uq_rope[:, k, h0:h0 + 4, NOPE:NOPE + ROPE]).then_inc(stage_in[n % NSTAGE], 16)
                    else:
                        sp.dma_start(stage[n % NSTAGE][:, at:at + size].rearrange("p (k n) -> p k n", n=nc_),
                                     w_dram[w][:, k0:k1, c0:c0 + nc_]).then_inc(stage_in[n % NSTAGE], 16)
                    at += size

            def load_x(t):
                sp.dma_start(rows[:, t, :], dram["x_prompt"][0, t * P:(t + 1) * P, :] if t < NP
                             else dram["x_sample"].rearrange("b l d -> (b l) d")).then_inc(x_in[t], 16)

            load_x(0)
            sp.dma_start(const[:, :], dram["const"]).then_inc(consts_in, 16)
            load_x(1)
            sp.dma_start(const_raw[:, :], dram["const_r"]).then_inc(consts_in, 16)
            for n, g in gain.items():
                sp.dma_start(g[:, :], dram[n]).then_inc(gains_in, 16)
            load_piece(*PIECES[0])
            for t in range(2, NT):
                load_x(t)
            sp.dma_start(gate_w[0:RANK, :], dram["a_w_gate2"][0]).then_inc(gate_in, 16)
            sp.dma_start(gate_w[RANK:RANK + 1, :], dram["a_b_gate"]).then_inc(gate_in, 16)
            sp.dma_start(post[:, :], dram["a_norm_post"].to_broadcast([P, D])).then_inc(post_in, 16)
            sp.dma_start(lat_gain[:, :], dram["kv_latent_norm"].unsqueeze(0).to_broadcast([P, KL])).then_inc(post_in, 16)
            for name, j in PIECES[1:2]:
                load_piece(name, j)
            for step in STEPS:
                if "sp" not in parts(step):
                    continue
                kind = step[0]
                if kind == "piece":
                    n = PIECE_NO[step[1], step[2]] + 2
                    if n < len(PIECES):
                        load_piece(*PIECES[n])
                elif kind == "lds":
                    h = step[1]
                    if h:
                        sp.wait_ge(state_out, 16 * h)
                    else:
                        after(sp, "pe", "c", NT - 1)
                    sp.dma_start(st_s[:, :, :], dram["state_gla"][0, :, h].rearrange("b k v -> k b v")).then_inc(state_in, 16)
                elif kind == "sts":
                    h = step[1]
                    after(sp, "dve", "Us", h, 1)
                    sp.dma_start(st_sample[0, :, h].rearrange("b k v -> k b v"), st_s[:, :, :]).then_inc(state_out, 16)
                elif kind == "stp":
                    h = step[1]
                    after(sp, "dve", "U", h)
                    sp.dma_start(st_prompt[0, 0, h], st_in[:, 0, :]).then_inc(final_out, 16)
                elif kind == "ldr":
                    for who, s in (("dve", ("Us", HA - 1, 1)), ("act", ("o", HA - 1)), ("pe", ("Us", HA - 1, 1))):
                        after(sp, who, *s)
                    sp.dma_start(x1[:, 0:NP, :], dram["x_prompt"][0].rearrange("(t p) d -> p t d", p=P)).then_inc(rest_in, 16)
                    sp.dma_start(x1[:, NP, :], dram["x_sample"].rearrange("b l d -> (b l) d")).then_inc(rest_in, 16)
                elif kind == "keep":
                    t = step[1]
                    after(sp, "dve", "r", "A", t)
                    sp.dma_start(kept[:, t, :], x1[:, t, :]).then_inc(kept_out, 16)
                elif kind == "ldk":
                    after(sp, "pe", "cx", SB - 1)
                    sp.wait_ge(kept_out, 16 * NT)
                    sp.dma_start(xB[:, :, :], kept).then_inc(rest_in, 16)
                elif kind == "och":
                    after(sp, "dve", "lcs")
                    after(sp, "dve", "lr")
                    after(sp, "dve", "r", "A", NT - 1)
                    sp.dma_start(post[:, :], dram["b_norm_post"].to_broadcast([P, D])).then_inc(post_in, 16)
                    sp.dma_start(ckv_prompt[0].rearrange("(t p) n -> p t n", p=P), ckvn[:, 0:NP, :]).then_inc(latent_out, 16)
                    sp.dma_start(ckv_sample.rearrange("b l n -> (b l) n"), ckvn[:, NP, :]).then_inc(latent_out, 16)
                    sp.dma_start(krope_prompt[0].rearrange("(t p) n -> p t n", p=P), krn[:, 0:NP, :]).then_inc(latent_out, 16)
                    sp.dma_start(krope_sample.rearrange("b l n -> (b l) n"), krn[:, NP, :]).then_inc(latent_out, 16)
                elif kind == "ldc":
                    b = step[1]
                    if b < 2:
                        after(sp, "pe", "wt", 2)
                    else:
                        after(sp, "pool", "cs", b - 2)
                        after(sp, "pe", "cr", b - 2)
                    sp.dma_start(craw[b % 2][:, :, :], dram["cache_ckv"][b].rearrange("(s p) n -> p s n", p=P)).then_inc(cache_in[b % 2], 16)
                    sp.dma_start(kraw[b % 2][:, :, :], dram["cache_krope"][b].rearrange("(s p) n -> p s n", p=P)).then_inc(cache_in[b % 2], 16)
                elif kind == "oy":
                    t = step[1]
                    after(sp, "dve", "r", "B", t)
                    sp.dma_start(y_prompt[0, t * P:(t + 1) * P, :] if t < NP else y_sample.rearrange("b l d -> (b l) d"),
                                 xB[:, t, :]).then_inc(y_out, 16)
            sp.wait_ge(y_out, 16 * NT)
            sp.wait_ge(latent_out, 16 * 4)
            sp.wait_ge(state_out, 16 * HA)
            sp.wait_ge(final_out, 16 * HA)

        @block.gpsimd
        def _(pool):
            own = [0]

            def link(ins):
                own[0] += 1
                ins.then_inc(pool_own, 1)
                pool.wait_ge(pool_own, own[0])

            def rms(name, width, count, factor=1.0):
                s, r = S1(name), S1(name, stat2)
                link(pool.tensor_scalar(r, s, 1.0 / width, EPS, MUL, ADD))
                if factor == 1.0:
                    return pool.tensor_tensor(r, r, minus_half[:, 0:count], ALU.pow)
                link(pool.tensor_tensor(r, r, minus_half[:, 0:count], ALU.pow))
                return pool.tensor_scalar(r, r, factor, None, MUL)

            pool.memset(q_own[:, :, :], 0.0).then_inc(own_set, 1)
            pool.memset(glrT[:, :], 1.0).then_inc(ones_set, 1)
            link(pool.memset(minus_half[:, :], -0.5))
            pool.wait_ge(gains_in, 16 * len(gain))
            for step in STEPS:
                if "pool" not in parts(step):
                    continue
                kind = step[0]
                if kind == "piece":
                    _, name, j = step
                    n = PIECE_NO[name, j]
                    pool.wait_ge(stage_in[n % NSTAGE], STAGE_COUNT[n])
                    at = 0
                    for w, k0, k1, c0, cols, g in SLABS[name][j]:
                        if g:
                            v = stage[n % NSTAGE][:, at:at + (k1 - k0) * cols].rearrange("p (k n) -> p k n", n=cols)
                            last = pool.tensor_tensor(v, v, over(gain[g][:, k0:k1], cols), MUL)
                        at += (k1 - k0) * cols
                elif kind == "xn":
                    after(pool, "act", *step)
                    last = rms(("x", step[1]), D, 1)
                elif kind in ("o", "os"):
                    after(pool, "act", *step)
                    h = step[1]
                    a, _b = STAT["o", h]
                    a, m = (a, NP) if kind == "o" else (a + NP, 1)
                    s, r = stat[:, a:a + m], stat2[:, a:a + m]
                    link(pool.tensor_scalar(r, s, 1.0 / DV, EPS, MUL, ADD))
                    link(pool.tensor_tensor(r, r, minus_half[:, 0:m], ALU.pow))
                    last = pool.tensor_scalar(r, r, 0.5, None, MUL)
                elif kind == "r":
                    _, ph, t = step
                    after(pool, "act", "yt", ph, t)
                    s, r = S1(("y", ph, t)), S1(("yr", ph, t), stat2)
                    link(pool.tensor_tensor(r, s[:, 0:1], s[:, 1:2], ADD))
                    link(pool.tensor_tensor(r, r, s[:, 2:3], ADD))
                    link(pool.tensor_scalar(r, r, 1.0 / D, EPS, MUL, ADD))
                    last = pool.tensor_tensor(r, r, minus_half[:, 0:1], ALU.pow)
                elif kind == "cs":
                    b = step[1]
                    pool.wait_ge(cache_in[b % 2], 32 * (b // 2 + 1))
                    after(pool, "pe", *(("sv", b - 1) if b else ("gb", 0, 1)))
                    link(pool.tensor_copy(cn[0][:, :, :], craw[b % 2][:, :, :]))
                    last = pool.tensor_tensor(cn[1][:, :, :], craw[b % 2][:, :, :], raw(cn[0][:, :, :]), SUB)
                elif kind == "rx":
                    after(pool, "act", "r", "A", step[1])
                    last = rms(("x1", step[1]), D, 1)
                elif kind in ("lc", "lcs"):
                    after(pool, "act", *step)
                    a, _b = STAT["lat",]
                    a, m = (a, NP) if kind == "lc" else (a + NP, 1)
                    s, r = stat[:, a:a + m], stat2[:, a:a + m]
                    link(pool.tensor_scalar(r, s, 1.0 / KL, EPS, MUL, ADD))
                    last = pool.tensor_tensor(r, r, minus_half[:, 0:m], ALU.pow)
                elif kind == "qs":
                    after(pool, "act", "qb")
                    s, r = S1(("qa",)), S1(("qa",), stat2)
                    link(pool.tensor_tensor(r, s, S1(("qb",)), ADD))
                    link(pool.tensor_scalar(r, r, 1.0 / QL, EPS, MUL, ADD))
                    last = pool.tensor_tensor(r, r, minus_half[:, 0:NT], ALU.pow)
                last.then_inc(done["pool"], 1)
                pool.wait_ge(done["pool"], AT["pool"][step])

        @block.scalar
        def _(act):
            def copy(out, in_):
                return act.activation(out, in_, ACT.Copy)

            act.wait_ge(consts_in, 32)
            for step in STEPS:
                if "act" not in parts(step):
                    continue
                kind = step[0]
                who = parts(step)[parts(step).index("act") - 1] if parts(step)[0] != "act" else None
                if who and who != "sp":
                    after(act, who, *step)
                bank, row = banks(step) if step in BANK_NO else (None, None)
                if kind == "const":
                    last = copy(const_r[:, :], const_raw[:, :])
                elif kind == "piece":
                    _, name, j = step
                    n = PIECE_NO[name, j]
                    if who == "sp":
                        act.wait_ge(stage_in[n % NSTAGE], STAGE_COUNT[n])
                    if name == "uv":
                        after(act, "pe", "cr", SB - 1)
                        after(act, "pool", "cs", SB - 1)
                    elif name == ("wo", "B", 0):
                        after(act, "pe", "O", HB - 1)
                    if SLAB_NO[name] >= 2:
                        after(act, "pe", *USERS[SLAB_NAMES[SLAB_NO[name] - 2]])
                    m = used(name, j)
                    last = copy(weights(name)[0][:, j * PIECE:j * PIECE + m], stage[n % NSTAGE][:, 0:m])
                elif kind == "xn":
                    t = step[1]
                    act.wait_ge(x_in[t], 16)
                    last = act.activation(junk[:, :], rows[:, t, :], ACT.Square, accum_out=S1(("x", t)))
                elif kind in ("xT", "oT"):
                    t = step[-1]
                    last = copy(hat[0][:, :, t * P:(t + 1) * P], row.rearrange("p (k n) -> p k n", n=P))
                elif kind == "glr":
                    act.wait_ge(ones_set, 1)
                    last = copy(glrT[0:RANK, :].rearrange("p (a n) -> p a n", a=2), bank[0:RANK, :, 0:HALF])
                elif kind == "z":
                    v = z_abs[:, step[1], :]
                    act.activation(v, bank[:, 0, :], ACT.Abs).then_inc(act_own, 1)
                    act.wait_ge(act_own, step[1] + 1)
                    last = act.activation(v, v, ACT.Exp, scale=-1.0)
                elif kind == "ln":
                    last = act.activation(z_abs[:, :, :], z_abs[:, :, :], ACT.Ln, bias=1.0)
                elif kind == "c":
                    t = step[1]
                    v = bank[:, :, 0:2 * (P + 2)].rearrange("p a (h n) -> p a h n", n=P + 2)
                    copy(cumT[:, :, t * P:(t + 1) * P].rearrange("p (a h) n -> p a h n", a=2), v[:, :, :, 0:P])
                    last = copy(decay[:, :, t:t + 1].rearrange("p (a h) n -> p a h n", a=2), v[:, :, :, P:P + 1])
                elif kind == "e":
                    h = step[1]
                    if h:
                        after(act, "dve", "k", h - 1)
                        after(act, "dve", "Us", h - 1, 1)
                    act.activation(Ep[:, :], cumT[:, h, :], ACT.Exp)
                    act.activation(Em[:, :], cumT[:, h, :], ACT.Exp, scale=-1.0)
                    last = act.activation(eB[:, :], decay[:, h, :], ACT.Exp)
                elif kind == "q":
                    last = copy(qT[0][:, :], tmp[:, :])
                elif kind == "k":
                    last = copy(kT[0][:, :], kt[:, :])
                elif kind == "sc":
                    last = copy(scT[0][:, :], tmp[:, :])
                elif kind == "v":
                    last = copy(vv[0][:, 0:NP, :], row.rearrange("p (t n) -> p t n", n=DV))
                elif kind == "vs":
                    copy(v_s[:, :], bank[:, 0, 0:DV])
                    last = copy(vv[0][:, NP, :], bank[:, 0, 0:DV])
                elif kind == "kT":
                    last = copy(kn[0][:, :, :], row[:, 0:TOK].rearrange("p (t n) -> p t n", n=DK))
                elif kind == "gt":
                    h = step[1]
                    if h:
                        after(act, "dve", "Slo", h - 1)
                        act.wait_ge(final_out, 16 * h)
                    last = act.activation(th, row, ACT.Tanh, scale=0.5)
                elif kind == "gts":
                    after(act, "dve", "gt", step[1])
                    last = act.activation(th[:, 0:DV], bank[:, 0, 0:DV], ACT.Tanh, scale=0.5)
                elif kind == "U":
                    last = copy(st[0][:, 1:, :], st_in[:, 1:, :])
                elif kind == "o":
                    for t in range(NP):
                        last = act.activation(junk[:, t * DV:(t + 1) * DV], row[:, t * DV:(t + 1) * DV], ACT.Square, accum_out=S1(("o", step[1]), t=t))
                elif kind == "os":
                    last = act.activation(junk[:, 0:DV], row[:, 0:DV], ACT.Square, accum_out=S1(("o", step[1]), t=NP))
                elif kind in ("y", "ys"):
                    _, ph, s = step
                    for i, t in enumerate(range(NP) if kind == "y" else [NP]):
                        last = act.activation(junk[:, i * 256:(i + 1) * 256], row[:, i * 256:(i + 1) * 256], ACT.Square, accum_out=S1(("y", ph, t), t=s))
                elif kind == "yt":
                    _, ph, t = step
                    last = act.activation(junk[:, 0:512], bank[:, 0, :], ACT.Square, accum_out=S1(("y", ph, t), t=2))
                elif kind == "r":
                    if step[1] == "A":
                        t = step[2]
                        last = act.activation(junk[:, :], x1[:, t, :], ACT.Square, accum_out=S1(("x1", t)))
                    else:
                        last = copy(junk[:, 0:1], stat[:, 0:1])
                elif kind in ("lc", "lcs"):
                    for i, t in enumerate(range(NP) if kind == "lc" else [NP]):
                        last = act.activation(junk[:, i * KL:(i + 1) * KL], row[:, i * KL:(i + 1) * KL], ACT.Square, accum_out=S1(("lat",), t=t))
                elif kind == "cn":
                    after(act, "dve", "lcs")
                    last = copy(cn_s[0][:, :], ckvn[:, NP, :])
                elif kind == "cT":
                    t = step[1]
                    c = slice(t * P, (t + 1) * P)
                    copy(cT[0][:, :, c], bank[:, 0, 0:KL].rearrange("p (k n) -> p k n", n=P))
                    copy(krS[0:ROPE, c], bank[0:ROPE, 1, 0:P])
                    last = copy(krS[ROPE:P, c], bank[0:ROPE, 1, 0:P])
                elif kind in ("qa", "qas", "qb"):
                    m = QL - 256 if kind == "qb" else 256
                    for i, t in enumerate({"qa": range(NP), "qas": [NP], "qb": range(NT)}[kind]):
                        last = act.activation(junk[:, i * m:(i + 1) * m], row[:, i * m:(i + 1) * m], ACT.Square,
                                              accum_out=S1(("qb" if kind == "qb" else "qa",), t=t))
                elif kind == "qT":
                    t = step[1]
                    last = copy(qlT[0][:, :, t * P:(t + 1) * P], bank[:, 0, 0:QL].rearrange("p (k n) -> p k n", n=P))
                elif kind == "gb":
                    _, s, j = step
                    if s != 3:
                        after(act, "dve", "gb", s + 1, j)
                    last = act.activation(thb[:, j * TOK:(j + 1) * TOK].rearrange("p (a n) -> p a n", a=2), bank[:, :, 0:HALF], ACT.Tanh, scale=0.5)
                elif kind == "qrT":
                    t = step[1]
                    if t == 0:
                        act.wait_ge(kept_out, 16 * NT)
                    last = copy(rotary_to(t, slice(0, ROPE)), rotary_from(row, t))
                elif kind == "qn":
                    last = copy(qN[0][:, :], bank[:, 0, :])
                elif kind == "qns":
                    last = copy(qN_s[0][:, :], bank[:, 0, 0:2 * P])
                elif kind == "wt":
                    copy(wT[0][:, :], bank[:, 0, :])
                    last = copy(wT[1][:, :], bank[:, 1, :])
                elif kind == "kh":
                    last = copy(kN[0][:, :], bank[:, 0, :])
                elif kind == "vh":
                    last = copy(vN[0][:, :, :], row.rearrange("p (t n) -> p t n", n=2 * VB))
                elif kind == "qabs":
                    for i in range(2):
                        last = copy(by_stream(qab[0][:, :, :, :], 2 * step[1] + i),
                                    bank[:, 0, i * KL:(i + 1) * KL].rearrange("p (k b n) -> p k b n", k=KC, n=SL))
                elif kind == "S":
                    _, h, u = step
                    for j, (i, c0) in enumerate(zip(UNITS[u], (0, UNITS[u][0] + 1))):
                        last = act.activation(prob[u][:, c0:c0 + i + 1, :], bank[:, j, 0:(i + 1) * P].rearrange("p (s n) -> p s n", n=P),
                                              ACT.Exp, scale=SCALE, bias=S1(("S", h, u), stat2, j), accum_out=S1(("S", h, u), t=j))
                elif kind == "T":
                    last = copy(pT[step[2]][0][:, :], row[:, 0:TOK])
                elif kind == "ct":
                    last = copy(sT[0][:, :, :], bank[:, :, :])
                elif kind == "cr":
                    copy(skS[0:ROPE, :], bank[0:ROPE, 0, :])
                    last = copy(skS[ROPE:P, :], bank[0:ROPE, 0, :])
                elif kind == "ss":
                    b = step[1]
                    last = act.activation(sprob[:, :, :], row[:, 0:TOK].rearrange("p (s n) -> p s n", n=P), ACT.Exp,
                                          scale=SCALE, bias=S1(("ss", b), stat2), accum_out=S1(("ss", b)))
                elif kind == "st":
                    last = copy(spT[0][:, :], row[:, 0:TOK])
                elif kind == "cx":
                    last = copy(qab[0][:, :, step[1], :], bank[:, 0, 0:KL].rearrange("p (k n) -> p k n", n=P))
                elif kind == "Oh":
                    after(act, "dve", "O", step[1])
                    last = copy(qS[:, step[1], :], gateT[:, step[1], 0:SEQ])
                elif kind == "soh":
                    after(act, "dve", "so")
                    last = copy(oS_s[:, :, :], gateT[:, :, SEQ:TOK])
                last.then_inc(done["act"], 1)
                act.wait_ge(done["act"], AT["act"][step])

        @block.vector
        def _(dve):
            own = [0]

            def link(ins):
                own[0] += 1
                ins.then_inc(dve_own, 1)
                dve.wait_ge(dve_own, own[0])

            def tt(out, a, b, op):
                return dve.tensor_tensor(out, a, b, op)

            def low(lo, full, hi):
                return dve.tensor_tensor(lo, full, raw(hi), SUB)

            def rotate(out, src, tables, scratch):
                cos, sin = tables
                m = src.shape[1]
                t1, t2 = (scratch[:, i * m * RH:(i + 1) * m * RH].rearrange("p (m n) -> p m n", n=RH) for i in range(2))
                a, b = src[:, :, 0:RH], src[:, :, RH:ROPE]
                tt(t1, a, cos, MUL)
                link(tt(t2, b, sin, MUL))
                link(tt(out[:, :, 0:RH], t1, t2, SUB))
                tt(t1, b, cos, MUL)
                link(tt(t2, a, sin, MUL))
                return tt(out[:, :, RH:ROPE], t1, t2, ADD)

            dve.wait_ge(consts_in, 32)
            for step in STEPS:
                if "dve" not in parts(step):
                    continue
                kind = step[0]
                if parts(step)[0] != "dve":
                    after(dve, parts(step)[parts(step).index("dve") - 1], *step)
                bank, row = banks(step) if step in BANK_NO else (None, None)
                if kind == "piece":
                    _, name, j = step
                    m = used(name, j)
                    hi, lo = weights(name)
                    c = slice(j * PIECE, j * PIECE + m)
                    last = low(lo[:, c], stage[PIECE_NO[name, j] % NSTAGE][:, 0:m], hi[:, c])
                elif kind == "xn":
                    t = step[1]
                    last = dve.tensor_scalar(rows[:, t, :], rows[:, t, :], S1(("x", t), stat2), None, MUL)
                elif kind in ("xT", "oT"):
                    t = step[-1]
                    c = slice(t * P, (t + 1) * P)
                    last = low(hat[1][:, :, c], row.rearrange("p (k n) -> p k n", n=P), hat[0][:, :, c])
                elif kind == "z":
                    last = dve.tensor_scalar(z_min[:, step[1], :], bank[:, 0, :], 0.0, None, ALU.min)
                elif kind == "lg":
                    after(dve, "act", "ln")
                    t = step[1]
                    link(tt(z_min[:, t, :], z_min[:, t, :], z_abs[:, t, :], SUB))
                    link(dve.tensor_copy(lg[0][:, t, :], z_min[:, t, :]))
                    last = low(lg[1][:, t, :], z_min[:, t, :], lg[0][:, t, :])
                elif kind == "q":
                    h = step[1]
                    after(dve, "act", "e", h)
                    if h == 0:
                        after(dve, "act", "const")
                        dve.wait_ge(own_set, 1)
                    v = bank[:, :, 0:HALF]
                    link(dve.scalar_tensor_tensor(tmp[:, :].rearrange("p (a n) -> p a n", a=2), v, DK ** -0.5,
                                                  Ep[:, :].rearrange("p (a n) -> p a n", a=2), MUL, MUL))
                    for b in range(SB):
                        last = dve.tensor_copy(q_own[:, b, b * SL:(b + 1) * SL], tmp[:, SEQ + b * SL:SEQ + (b + 1) * SL])
                elif kind == "k":
                    last = tt(kt[:, :].rearrange("p (a n) -> p a n", a=2), bank[:, :, 0:HALF], Em[:, :].rearrange("p (a n) -> p a n", a=2), MUL)
                elif kind == "qlo":
                    after(dve, "act", "q", step[1])
                    last = low(qT[1][:, :], tmp[:, :], qT[0][:, :])
                elif kind == "klo":
                    after(dve, "act", "k", step[1])
                    last = low(kT[1][:, :], kt[:, :], kT[0][:, :])
                elif kind == "sc":
                    tt(tmp[:, 0:SEQ].rearrange("p (t n) -> p t n", n=P), bank[:, 0, :].rearrange("p (t n) -> p t n", n=P),
                       times(cst("mask_p"), NP), MUL)
                    last = tt(tmp[:, SEQ:TOK], bank[:, 1, 0:P], cst("mask_s"), MUL)
                elif kind == "sclo":
                    after(dve, "act", "sc", step[1])
                    last = low(scT[1][:, :], tmp[:, :], scT[0][:, :])
                elif kind == "v":
                    last = low(vv[1][:, 0:NP, :], row.rearrange("p (t n) -> p t n", n=DV), vv[0][:, 0:NP, :])
                elif kind == "vs":
                    last = low(vv[1][:, NP, :], v_s[:, :], vv[0][:, NP, :])
                elif kind == "kT":
                    low(kn[1][:, :, :], row[:, 0:TOK].rearrange("p (t n) -> p t n", n=DK), kn[0][:, :, :])
                    last = tt(k_own[:, :, :], times(bank[:, 1, 0:P], SB), over(cst("member"), DK), MUL)
                elif kind == "gt":
                    h = step[1]
                    last = dve.scalar_tensor_tensor(rows[:, 0:NP, h * DV:(h + 1) * DV], th.rearrange("p (t n) -> p t n", n=DV), 1.0,
                                                    row.rearrange("p (t n) -> p t n", n=DV), ADD, MUL)
                elif kind == "gts":
                    h = step[1]
                    last = dve.scalar_tensor_tensor(rows[:, NP, h * DV:(h + 1) * DV], th[:, 0:DV], 1.0, bank[:, 0, 0:DV], ADD, MUL)
                elif kind == "U":
                    if step[1]:
                        dve.wait_ge(final_out, 16 * step[1])
                    for t in range(NP):
                        e_end = Ep[:, t * P + P - 1:t * P + P]
                        u = row[:, t * DV:(t + 1) * DV]
                        nxt = (t + 1) % NP
                        if t:
                            link(tt(st_in[:, 0, :], u, st_in[:, t, :], ADD))
                            u = st_in[:, 0, :]
                        if t < NP - 1:
                            link(dve.tensor_scalar(st_in[:, nxt, :], u, e_end, eB[:, t + 1:t + 2], MUL, MUL))
                        else:
                            last = dve.tensor_scalar(st_in[:, 0, :], u, e_end, None, MUL)
                elif kind == "Slo":
                    after(dve, "act", "U", step[1])
                    last = low(st[1][:, 1:, :], st_in[:, 1:, :], st[0][:, 1:, :])
                elif kind == "Us":
                    _, h, j = step
                    dve.wait_ge(state_in, 16 * (h + 1))
                    v = st_s[:, 4 * j:4 * j + 4, :]
                    link(tt(v, row.rearrange("p (b n) -> p b n", n=DV), v, ADD))
                    for b in range(4 * j, 4 * j + 4):
                        e = Ep[:, SEQ + b * SL + SL - 1:SEQ + (b + 1) * SL]
                        last = dve.tensor_scalar(st_s[:, b, :], st_s[:, b, :], e, None, MUL)
                elif kind in ("o", "os"):
                    h = step[1]
                    for i, t in enumerate(range(NP) if kind == "o" else [NP]):
                        v = rows[:, t, h * DV:(h + 1) * DV]
                        last = dve.scalar_tensor_tensor(v, row[:, i * DV:(i + 1) * DV], S1(("o", h), stat2, t), v, MUL, MUL)
                elif kind in ("y", "ys"):
                    _, ph, s = step
                    t = slice(0, NP) if kind == "y" else slice(NP, NT)
                    m = NP if kind == "y" else 1
                    y = rows if ph == "A" else y_rows
                    last = dve.tensor_copy(y[:, t, s * 256:(s + 1) * 256], row[:, 0:m * 256].rearrange("p (t n) -> p t n", n=256))
                elif kind == "r":
                    _, ph, t = step
                    dve.wait_ge(rest_in, 32 if ph == "A" else 48)
                    dve.wait_ge(post_in, 32 if ph == "A" else 48)
                    r = S1(("yr", ph, t), stat2)
                    y, x = (rows, x1) if ph == "A" else (y_rows, xB)
                    dve.scalar_tensor_tensor(y[:, t, 0:512], y[:, t, 0:512], r, post[:, 0:512], MUL, MUL)
                    yb, _row = banks(("yt", ph, t))
                    link(dve.scalar_tensor_tensor(y[:, t, 512:D], yb[:, 0, :], r, post[:, 512:D], MUL, MUL))
                    last = tt(x[:, t, :], y[:, t, :], x[:, t, :], ADD)
                elif kind == "rx":
                    t = step[1]
                    last = dve.tensor_scalar(rows[:, t, :], x1[:, t, :], S1(("x1", t), stat2), None, MUL)
                elif kind in ("lc", "lcs"):
                    dve.wait_ge(state_out, 16 * HA)
                    dve.wait_ge(final_out, 16 * HA)
                    for i, t in enumerate(range(NP) if kind == "lc" else [NP]):
                        last = dve.scalar_tensor_tensor(ckvn[:, t, :], row[:, i * KL:(i + 1) * KL], S1(("lat",), stat2, t), lat_gain[:, :], MUL, MUL)
                elif kind == "lr":
                    v = bank[:, 0, 0:NT * ROPE].rearrange("p (t n) -> p t n", n=ROPE)
                    last = rotate(krn[:, :, :], v, [cst(n).rearrange("p (t n) -> p t n", n=RH) for n in ("cos", "sin")],
                                  thb)
                elif kind == "cn":
                    last = low(cn_s[1][:, :], ckvn[:, NP, :], cn_s[0][:, :])
                elif kind == "cT":
                    t = step[1]
                    c = slice(t * P, (t + 1) * P)
                    low(cT[1][:, :, c], bank[:, 0, 0:KL].rearrange("p (k n) -> p k n", n=P), cT[0][:, :, c])
                    last = low(krL[:, c], bank[0:ROPE, 1, 0:P], krS[0:ROPE, c])
                elif kind in ("qa", "qas", "qb"):
                    c = slice(256, QL) if kind == "qb" else slice(0, 256)
                    m = c.stop - c.start
                    t = {"qa": slice(0, NP), "qas": slice(NP, NT), "qb": slice(0, NT)}[kind]
                    n = t.stop - t.start
                    last = dve.tensor_copy(qln[:, t, c], row[:, 0:n * m].rearrange("p (t n) -> p t n", n=m))
                elif kind == "qs":
                    for t in range(NT):
                        last = dve.tensor_scalar(qln[:, t, :], qln[:, t, :], S1(("qa",), stat2, t), None, MUL)
                elif kind == "qT":
                    t = step[1]
                    c = slice(t * P, (t + 1) * P)
                    last = low(qlT[1][:, :, c], bank[:, 0, 0:QL].rearrange("p (k n) -> p k n", n=P), qlT[0][:, :, c])
                elif kind == "gb":
                    _, s, j = step
                    last = dve.scalar_tensor_tensor(gateT[:, 2 * s + j, :].rearrange("p (a n) -> p a n", a=2),
                                                    thb[:, j * TOK:(j + 1) * TOK].rearrange("p (a n) -> p a n", a=2),
                                                    1.0, bank[:, :, 0:HALF], ADD, MUL)
                elif kind == "qr":
                    t = step[1]
                    if t:
                        after(dve, "pe", "qrT", t - 1)
                    else:
                        dve.wait_ge(latent_out, 16 * 4)
                        after(dve, "pe", "cT", NT - 1)
                    v = bank[:, 0, :].rearrange("p (h n) -> p h n", n=ROPE)
                    tables = [times(cst(n)[:, t * RH:(t + 1) * RH], HB) for n in ("cos", "sin")]
                    last = rotate(qrn[:, :].rearrange("p (h n) -> p h n", n=ROPE), v, tables, rtmp)
                elif kind == "qrT":
                    t = step[1]
                    last = low(rotary_to(t, slice(ROPE, P)), rotary_from(row, t), rotary_to(t, slice(0, ROPE)))
                elif kind == "qn":
                    last = low(qN[1][:, :], bank[:, 0, :], qN[0][:, :])
                elif kind == "qns":
                    last = low(qN_s[1][:, :], bank[:, 0, 0:2 * P], qN_s[0][:, :])
                elif kind == "kh":
                    last = low(kN[1][:, :], bank[:, 0, :], kN[0][:, :])
                elif kind == "vh":
                    last = low(vN[1][:, :, :], row.rearrange("p (t n) -> p t n", n=2 * VB), vN[0][:, :, :])
                elif kind == "qabs":
                    for i in range(2):
                        hi, lo = (by_stream(x[:, :, :, :], 2 * step[1] + i) for x in qab)
                        last = low(lo, bank[:, 0, i * KL:(i + 1) * KL].rearrange("p (k b n) -> p k b n", k=KC, n=SL), hi)
                elif kind == "S":
                    _, h, u = step
                    for j, i in enumerate(UNITS[u]):
                        ins = dve.reduce_max(S1(("S", h, u), t=j), bank[:, j, 0:(i + 1) * P], AX.X)
                    link(ins)
                    last = dve.tensor_scalar(S1(("S", h, u), stat2), S1(("S", h, u)), -SCALE, None, MUL)
                elif kind == "T":
                    last = low(pT[step[2]][1][:, :], row[:, 0:TOK], pT[step[2]][0][:, :])
                elif kind == "N":
                    _, h, u = step
                    after(dve, "act", "S", h, u)
                    r = S1(("S", h, u), stat2)
                    link(dve.reciprocal(r, S1(("S", h, u))))
                    for j, (i, c0) in enumerate(zip(UNITS[u], (0, UNITS[u][0] + 1))):
                        v = prob[u][:, c0:c0 + i + 1, :]
                        last = dve.tensor_scalar(v, v, r[:, j:j + 1], 0.5, MUL, MUL)
                elif kind == "O":
                    v = gateT[:, step[1], 0:SEQ]
                    last = tt(v, bank[:, 0, :], v, MUL)
                elif kind == "Oh":
                    h = step[1]
                    last = low(oT_lo[:, h, 0:SEQ], gateT[:, h, 0:SEQ], qS[:, h, :])
                elif kind == "ct":
                    last = low(sT[1][:, :, :], bank[:, :, :], sT[0][:, :, :])
                elif kind == "cr":
                    last = low(skL[:, :], bank[0:ROPE, 0, :], skS[0:ROPE, :])
                elif kind == "ss":
                    b = step[1]
                    link(dve.reduce_max(S1(("ss", b)), row[:, 0:TOK], AX.X))
                    last = dve.tensor_scalar(S1(("ss", b), stat2), S1(("ss", b)), -SCALE, None, MUL)
                elif kind == "st":
                    last = low(spT[1][:, :], row[:, 0:TOK], spT[0][:, :])
                elif kind == "sv":
                    b = step[1]
                    after(dve, "act", "ss", b)
                    r = S1(("ss", b), stat2)
                    link(dve.reciprocal(r, S1(("ss", b))))
                    last = dve.tensor_scalar(ctxn[:, :], bank[:, 0, 0:KL], r, 0.5, MUL, MUL)
                elif kind == "cx":
                    last = low(qab[1][:, :, step[1], :], bank[:, 0, 0:KL].rearrange("p (k n) -> p k n", n=P), qab[0][:, :, step[1], :])
                elif kind == "so":
                    v = gateT[:, :, SEQ:TOK]
                    last = tt(v, row.rearrange("p (h n) -> p h n", n=P), v, MUL)
                elif kind == "soh":
                    last = low(oT_lo[:, :, SEQ:TOK], gateT[:, :, SEQ:TOK], oS_s[:, :, :])
                last.then_inc(done["dve"], 1)
                dve.wait_ge(done["dve"], AT["dve"][step])

        @block.tensor
        def _(pe):
            def mm3(out, a, b, first, last):
                pe.matmul(out, a[0], b[0], start=first, stop=False)
                pe.matmul(out, a[0], b[1], start=False, stop=False)
                return pe.matmul(out, a[1], b[0], start=False, stop=last)

            def cut(pair_, *idx):
                return tuple(x[idx] for x in pair_)

            A_ = slice(None)

            def natural(row, name, tiles, cols, kts, src):
                w = [x[:, 0:kts * cols].rearrange("p (k n) -> p k n", n=cols) for x in weights(name)]
                for i, t in enumerate(tiles):
                    for k in range(kts):
                        last = mm3(row[:, i * cols:(i + 1) * cols], cut(src, A_, k, slice(t * P, (t + 1) * P)) if src else outT(k, t),
                                   cut(w, A_, k), k == 0, k == kts - 1)
                return last

            def outT(k, t):
                return qS[:, k, t * P:(t + 1) * P] if t < NP else oS_s[:, k, :], oT_lo[:, k, t * P:(t + 1) * P]

            def ready(name):
                after(pe, "dve", "piece", name, len(SLABS[name]) - 1)

            for step in STEPS:
                if "pe" not in parts(step):
                    continue
                kind = step[0]
                bank, row = before_bank(pe, step)
                if kind in ("xT", "oT"):
                    t = step[-1]
                    if kind == "oT":
                        after(pe, "dve", "Us", HA - 1, 1)
                    else:
                        after(pe, "dve", *(("xn", t) if step[1] == "A" else ("rx", t)))
                    for k in range(KD):
                        last = pe.transpose(row[:, k * P:(k + 1) * P], rows[:, t, k * P:(k + 1) * P], ident)
                elif kind == "glr":
                    ready("glr")
                    after(pe, "dve", "xT", "A", NT - 1)
                    w = [x[:, 0:KD * RANK].rearrange("p (k n) -> p k n", n=RANK) for x in weights("glr")]
                    for a in range(2):
                        for k in range(KD):
                            last = mm3(bank[0:RANK, a, 0:HALF], cut(w, A_, k), cut(hat, A_, k, slice(a * HALF, (a + 1) * HALF)), k == 0, k == KD - 1)
                elif kind == "z":
                    t = step[1]
                    after(pe, "act", "glr")
                    pe.wait_ge(gate_in, 32)
                    last = pe.matmul(bank[:, 0, :], glrT[:, t * P:(t + 1) * P], gate_w[:, :], start=True, stop=True)
                elif kind == "c":
                    t = step[1]
                    after(pe, "dve", "lg", t)
                    after(pe, "act", "const")
                    m = cst_r("cum_p" if t < NP else "cum_s")
                    for h in range(HA):
                        o = bank[:, h // 2, (h % 2) * (P + 2):(h % 2 + 1) * (P + 2)]
                        pe.matmul(o, lg[0][:, t, h * DK:(h + 1) * DK], m, start=True, stop=False)
                        last = pe.matmul(o, lg[1][:, t, h * DK:(h + 1) * DK], m, start=False, stop=True)
                elif kind in ("q", "k"):
                    h = step[1]
                    after(pe, "dve", "piece", ("qk", h), 0 if kind == "q" else 1)
                    off = 0 if kind == "q" else PIECE
                    w = [x[:, off:off + KD * DK].rearrange("p (k n) -> p k n", n=DK) for x in weights(("qk", h))]
                    for a in range(2):
                        for k in range(KD):
                            last = mm3(bank[:, a, 0:HALF], cut(w, A_, k), cut(hat, A_, k, slice(a * HALF, (a + 1) * HALF)), k == 0, k == KD - 1)
                elif kind in ("v", "vs", "gt", "gts"):
                    name = ("v" if kind[0] == "v" else "g", step[1])
                    ready(name)
                    last = natural(row, name, [NP] if kind[-1] == "s" else range(NP), DV, KD, hat)
                elif kind == "kT":
                    after(pe, "dve", "k", step[1])
                    for t in range(NT):
                        last = pe.transpose(row[:, t * P:(t + 1) * P], kt[:, t * P:(t + 1) * P], ident)
                elif kind == "sc":
                    h = step[1]
                    after(pe, "dve", "klo", h)
                    for t in range(NT):
                        c = slice(t * P, (t + 1) * P)
                        last = mm3(row[:, c], cut(kT, A_, c), cut(qT, A_, c), True, True)
                elif kind == "U":
                    after(pe, "dve", "v", step[1])
                    after(pe, "dve", "kT", step[1])
                    for t in range(NP):
                        last = mm3(row[:, t * DV:(t + 1) * DV], cut(kn, A_, t), cut(vv, A_, t), True, True)
                elif kind == "Us":
                    _, h, j = step
                    after(pe, "act", "vs", h)
                    for b in range(4):
                        last = pe.matmul(row[:, b * DV:(b + 1) * DV], k_own[:, 4 * j + b, :], v_s[:, :], start=True, stop=True)
                elif kind == "o":
                    h = step[1]
                    after(pe, "dve", "sclo", h)
                    after(pe, "dve", "Slo", h)
                    for t in range(NP):
                        c = slice(t * P, (t + 1) * P)
                        o = row[:, t * DV:(t + 1) * DV]
                        last = mm3(o, cut(scT, A_, c), cut(vv, A_, t), True, t == 0)
                        if t:
                            last = mm3(o, cut(qT, A_, c), cut(st, A_, t), False, True)
                elif kind == "os":
                    h = step[1]
                    after(pe, "dve", "sclo", h)
                    after(pe, "dve", "vs", h)
                    pe.wait_ge(state_in, 16 * (h + 1))
                    c = slice(SEQ, TOK)
                    mm3(row[:, 0:DV], cut(scT, A_, c), cut(vv, A_, NP), True, False)
                    for b in range(SB):
                        last = pe.matmul(row[:, 0:DV], q_own[:, b, :], st_s[:, b, :], start=False, stop=b == SB - 1)
                elif kind in ("y", "ys"):
                    _, ph, s = step
                    ready(("wo", ph, s))
                    after(pe, "dve", *(("oT", ph, NT - 1) if ph == "A" else ("Oh", HB - 1) if kind == "y" else ("soh",)))
                    last = natural(row, ("wo", ph, s), range(NP) if kind == "y" else [NP], 256, KD, hat if ph == "A" else None)
                elif kind == "yt":
                    _, ph, t = step
                    for i, s in enumerate((2, 3)):
                        ready(("wo", ph, s))
                        last = natural(bank[:, 0, i * 256:(i + 1) * 256], ("wo", ph, s), [t], 256, KD, hat if ph == "A" else None)
                elif kind in ("lc", "lcs"):
                    ready("kvc")
                    after(pe, "dve", "xT", "B", NT - 1)
                    last = natural(row, "kvc", range(NP) if kind == "lc" else [NP], KL, KD, hat)
                elif kind == "lr":
                    ready("kvr")
                    last = natural(row, "kvr", range(NT), ROPE, KD, hat)
                elif kind == "cT":
                    t = step[1]
                    after(pe, "dve", "lr")
                    for c in range(KC):
                        pe.transpose(bank[:, 0, c * P:(c + 1) * P], ckvn[:, t, c * P:(c + 1) * P], ident)
                    last = pe.transpose(bank[0:ROPE, 1, 0:P], krn[:, t, :], ident)
                elif kind in ("qa", "qas"):
                    ready("ql0")
                    last = natural(row, "ql0", range(NP) if kind == "qa" else [NP], 256, KD, hat)
                elif kind == "qb":
                    ready("ql1")
                    last = natural(row, "ql1", range(NT), QL - 256, KD, hat)
                elif kind == "qT":
                    t = step[1]
                    after(pe, "dve", "qs")
                    for k in range(KQ):
                        last = pe.transpose(bank[:, 0, k * P:(k + 1) * P], qln[:, t, k * P:(k + 1) * P], ident)
                elif kind == "gb":
                    _, s, j = step
                    ready(("gb", s))
                    w = [x[:, :].rearrange("p (k n) -> p k n", n=256) for x in weights(("gb", s))]
                    for a in range(2):
                        for k in range(KD):
                            last = mm3(bank[:, a, 0:HALF], cut(w, A_, k, slice(j * P, (j + 1) * P)), cut(hat, A_, k, slice(a * HALF, (a + 1) * HALF)), k == 0, k == KD - 1)
                elif kind == "qr":
                    t = step[1]
                    ready("uqr")
                    after(pe, "dve", "qT", NT - 1)
                    for g in range(2):
                        w = [x[:, g * PIECE:g * PIECE + KQ * 256].rearrange("p (k n) -> p k n", n=256) for x in weights("uqr")]
                        for k in range(KQ):
                            last = mm3(bank[:, 0, g * 256:(g + 1) * 256], cut(qlT, A_, k, slice(t * P, (t + 1) * P)), cut(w, A_, k), k == 0, k == KQ - 1)
                elif kind == "qrT":
                    t = step[1]
                    after(pe, "dve", "qr", t)
                    for h in range(HB):
                        last = pe.transpose(row[0:ROPE, h * P:(h + 1) * P], qrn[:, h * ROPE:(h + 1) * ROPE], ident)
                elif kind == "qn":
                    h = step[1]
                    ready(("hd", h))
                    w = [x[:, 0:KQ * NOPE].rearrange("p (k n) -> p k n", n=NOPE) for x in weights(("hd", h))]
                    for k in range(KQ):
                        last = mm3(bank[:, 0, :], cut(w, A_, k), cut(qlT, A_, k, slice(0, SEQ)), k == 0, k == KQ - 1)
                elif kind == "qns":
                    ready(("pre", step[1]))
                    for i in range(2):
                        w = [x[:, i * PIECE:i * PIECE + KQ * NOPE].rearrange("p (k n) -> p k n", n=NOPE) for x in weights(("pre", step[1]))]
                        for k in range(KQ):
                            last = mm3(bank[:, 0, i * P:(i + 1) * P], cut(w, A_, k), cut(qlT, A_, k, slice(SEQ, TOK)), k == 0, k == KQ - 1)
                elif kind == "wt":
                    for j, x in enumerate(weights(("pre", step[1]))):
                        for i in range(2):
                            for c in range(KC):
                                at = i * PIECE + KQ * NOPE + c * NOPE
                                last = pe.transpose(bank[:, j, (i * KC + c) * P:(i * KC + c + 1) * P], raw(x[:, at:at + NOPE]), ident)
                elif kind == "kh":
                    h = step[1]
                    w = [x[:, KQ * NOPE:(KQ + KC) * NOPE].rearrange("p (k n) -> p k n", n=P) for x in weights(("hd", h))]
                    for c in range(KC):
                        last = mm3(bank[:, 0, :], cut(w, A_, c), cut(cT, A_, c, slice(0, SEQ)), c == 0, c == KC - 1)
                elif kind == "vh":
                    w = [cut(weights(("hd", 2 * step[1] + c)), A_, slice((KQ + KC) * NOPE, (KQ + KC) * NOPE + 2 * VB)) for c in range(KC)]
                    ready(("hd", 2 * step[1] + 1))
                    for t in range(NP):
                        for c in range(KC):
                            last = mm3(row[:, t * 2 * VB:(t + 1) * 2 * VB], cut(cT, A_, c, slice(t * P, (t + 1) * P)), w[c], c == 0, c == KC - 1)
                elif kind == "qabs":
                    after(pe, "act", "wt", step[1])
                    after(pe, "dve", "qns", step[1])
                    for i in range(2):
                        for c in range(KC):
                            j = (i * KC + c) * P
                            last = mm3(bank[:, 0, j:j + P], cut(wT, A_, slice(j, j + P)), cut(qN_s, A_, slice(i * P, (i + 1) * P)), True, True)
                elif kind == "S":
                    _, h, u = step
                    after(pe, "dve", "qn", h)
                    after(pe, "dve", "kh", h)
                    after(pe, "dve", "qrT", NT - 1)
                    for j, i in enumerate(UNITS[u]):
                        q, keys = slice(i * P, (i + 1) * P), slice(0, (i + 1) * P)
                        o = bank[:, j, keys]
                        mm3(o, cut(qN, A_, q), cut(kN, A_, keys), True, False)
                        pe.matmul(o, qS[:, h, q], krS[:, keys], start=False, stop=False)
                        pe.matmul(o, qS[0:ROPE, h, q], krL[:, keys], start=False, stop=False)
                        last = pe.matmul(bank[:, j, q], cst_r("early", 1), cst_r("late", 1), start=False, stop=True)
                elif kind == "T":
                    _, h, u = step
                    after(pe, "dve", "N", h, 1)
                    for n, (s, i) in enumerate((s, i) for s in KEY_UNITS[u] for i in range(s, NP)):
                        v = [x for x in range(2) if i in UNITS[x]][0]
                        at = s + (0 if UNITS[v][0] == i else UNITS[v][0] + 1)
                        last = pe.transpose(row[:, n * P:(n + 1) * P], prob[v][:, at, :], ident)
                elif kind == "O":
                    h = step[1]
                    after(pe, "dve", "T", h, 1)
                    after(pe, "dve", "vh", h // 2)
                    for s, u, at in ((s, u, n * (NP - KEY_UNITS[u][0]) * P) for u in range(2) for n, s in enumerate(KEY_UNITS[u])):
                        last = mm3(bank[:, 0, s * P:SEQ], cut(vN, A_, s, slice((h % 2) * VB, (h % 2 + 1) * VB)),
                                   cut(pT[u], A_, slice(at, at + (NP - s) * P)), s == 0, (u, s) == (1, KEY_UNITS[1][-1]))
                elif kind == "ct":
                    b = step[1]
                    pe.wait_ge(cache_in[b % 2], 32 * (b // 2 + 1))
                    for c in range(KC):
                        for s in range(PAST // P):
                            last = pe.transpose(bank[:, c, s * P:(s + 1) * P], craw[b % 2][:, s, c * P:(c + 1) * P], ident)
                elif kind == "cr":
                    b = step[1]
                    for s in range(PAST // P):
                        last = pe.transpose(bank[0:ROPE, 0, s * P:(s + 1) * P], kraw[b % 2][:, s, :], ident)
                elif kind == "ss":
                    b = step[1]
                    after(pe, "dve", "cr", b)
                    after(pe, "dve", "qabs", HB // 2 - 1)
                    for o, keys, kr, kl in ((bank[:, 0, :], sT, skS[:, :], skL[:, :]),
                                            (bank[:, 1, 0:P], cut(cT, A_, A_, slice(SEQ, TOK)), krS[:, SEQ:TOK], krL[:, SEQ:TOK])):
                        for c in range(KC):
                            mm3(o, cut(qab, A_, c, b), cut(keys, A_, c), c == 0, False)
                        q = qS_s[:, b, :, :].rearrange("p h n -> p (h n)")
                        pe.matmul(o, q, kr, start=False, stop=False)
                        last = pe.matmul(o, q[0:ROPE, :], kl, start=False, stop=keys is sT)
                    a, _b = CONST_R["others"]
                    at = a + P - b * SL
                    last = pe.matmul(bank[:, 1, 0:P], cst_r("ones", 1), const_r[0:1, at:at + P], start=False, stop=True)
                elif kind == "st":
                    b = step[1]
                    after(pe, "act", "ss", b)
                    for s in range(NT):
                        last = pe.transpose(row[:, s * P:(s + 1) * P], sprob[:, s, :], ident)
                elif kind == "sv":
                    b = step[1]
                    after(pe, "dve", "st", b)
                    after(pe, "pool", "cs", b)
                    after(pe, "dve", "cn")
                    for s in range(NT):
                        last = mm3(bank[:, 0, 0:KL], cut(spT, A_, slice(s * P, (s + 1) * P)), cut(cn, A_, s) if s < NT - 1 else cut(cn_s, A_, A_), s == 0, s == NT - 1)
                elif kind == "cx":
                    after(pe, "dve", "sv", step[1])
                    for c in range(KC):
                        last = pe.transpose(bank[:, 0, c * P:(c + 1) * P], ctxn[:, c * P:(c + 1) * P], ident)
                elif kind == "so":
                    ready("uv")
                    after(pe, "dve", "cx", SB - 1)
                    w = [x[:, :].rearrange("p (k n) -> p k n", n=HB * VB) for x in weights("uv")]
                    for h in range(HB):
                        for c in range(KC):
                            ctx_h = [x[:, c, :, h * SL:(h + 1) * SL] for x in qab]
                            last = mm3(row[:, h * P:(h + 1) * P].rearrange("p (b n) -> p b n", n=SL), cut(w, A_, c, slice(h * VB, (h + 1) * VB)), ctx_h, c == 0, c == KC - 1)
                last.then_inc(done["pe"], 1)


_INS = ["x_prompt", "x_sample", "state_gla", "cache_ckv", "cache_krope", "a_norm_pre", "a_w_in", "a_w_gate2", "a_b_gate",
        "a_head_norm", "a_w_out", "a_norm_post", "kv_norm", "kv_w_down", "kv_latent_norm", "kv_w_uk", "kv_w_uv",
        "b_norm_pre", "b_w_in", "b_q_norm", "b_w_uq", "b_w_out", "b_norm_post"]
_GAINS = ["a_norm_pre", "a_head_norm", "kv_norm", "b_norm_pre", "b_q_norm"]
_OUTS = [(1, SEQ, D), (SB, SL, D), (1, 1, HA, DK, DV), (1, SB, HA, DK, DV), (1, SEQ, KL), (1, SEQ, ROPE), (SB, SL, KL), (SB, SL, ROPE)]


def constants():
    import numpy as np
    i = np.arange(P)
    before = (i[:, None] <= i[None, :]).astype(np.float32)
    same = (i[:, None] // SL == i[None, :] // SL).astype(np.float32)
    half = (i < P // 2).astype(np.float32)[:, None]
    tau = np.float32(1.0 / 16.0)
    cum_p = np.zeros((P, P + 2), np.float32)
    cum_p[:, :P] = (before - half) * tau
    cum_p[:, P:P + 1] = half * tau
    cum_s = np.zeros((P, P + 2), np.float32)
    cum_s[:, :P] = before * same * tau
    pos = np.concatenate([np.arange(SEQ), PAST + np.arange(P) % SL]).astype(np.float32)
    inv = np.power(np.float32(10000.0), -np.arange(RH, dtype=np.float32) / np.float32(RH)).astype(np.float32)
    ang = (pos[:, None] * inv[None, :]).reshape(NT, P, RH).transpose(1, 0, 2).reshape(P, NT * RH)
    row = np.ones((P, 1), np.float32)
    others = np.full(2 * P, NEG, np.float32)
    others[P:P + SL] = 0.0
    const = [np.eye(P), before, before * same, (i[:, None] // SL == np.arange(SB)[None, :]), np.cos(ang), np.sin(ang)]
    const_r = [cum_p, cum_s, row * (1 - half.T * 0 - (i >= P // 2)[None, :]), row * np.where(i >= P // 2, NEG, 0.0)[None, :], row * np.ones((1, P)), row * others[None, :]]
    return [np.ascontiguousarray(np.concatenate(x, axis=1).astype(np.float32)) for x in (const, const_r)]


def kernel(**inputs):
    import numpy as _np
    import concourse.bacc as _bacc
    from concourse import mybir as _mybir
    from concourse.bass_utils import run_bass_kernel_spmd as _run

    nc = _bacc.Bacc("TRN2", target_bir_lowering=False, num_devices=1)
    arrays, dram = {}, {}
    data = {name: _np.ascontiguousarray(inputs[name]) for name in _INS}
    data["const"], data["const_r"] = constants()
    for name in _GAINS:
        data[name] = _np.ascontiguousarray(data[name].reshape(-1, P).T)
    for name, a in data.items():
        arrays[f"in_{name}_dram"] = a
        dram[name] = nc.dram_tensor(f"in_{name}_dram", a.shape, _mybir.dt.from_np(a.dtype), kind="ExternalInput").ap()
    outs = [nc.dram_tensor(f"out_{i}_dram", shape, _mybir.dt.float32, kind="ExternalOutput").ap() for i, shape in enumerate(_OUTS)]
    program(nc, dram, outs)
    r = _run(nc, [arrays], core_ids=[0])
    return tuple(r.results[0][f"out_{i}_dram"] for i in range(len(_OUTS)))
```

```python
import concourse.bass as bass
from concourse import mybir
from contextlib import ExitStack

P = 128
D = 1024
KD = D // P
SEQ = 512
SB, SL = 8, 16
PAST = 512
NP = SEQ // P
NT = NP + 1
TOK = NT * P
HALF = TOK // 2
HA, DK, DV = 4, 128, 256
RANK = 16
HB, NOPE, ROPE, VB = 8, 128, 64, 128
RH = ROPE // 2
QL, KL = 384, 256
KQ, KC = QL // P, KL // P
EPS = 1e-6
NEG = -float(2 ** 120)
SCALE = (NOPE + ROPE) ** -0.5
PIECE = 1024
NSTAGE = 4
NBANK = 4

def columns(sizes):
    out, at = {}, 0
    for name, n in sizes:
        out[name] = (at, at + n)
        at += n
    return out, at


CONST, NCONST = columns((("ident", P), ("mask_p", P), ("mask_s", P), ("member", SB), ("cos", NT * RH), ("sin", NT * RH)))
CONST_R, NCONST_R = columns((("cum_p", P + 2), ("cum_s", P + 2), ("early", P), ("late", P), ("ones", P), ("others", 2 * P)))


def slabs():
    def halves(w, base, gain):
        return [[(w, k, k + 4, base, 256, gain)] for k in (0, 4)]

    def nope(h):
        return ("b_w_uq", 0, KQ, h * (NOPE + ROPE), NOPE, "b_q_norm"), ("kv_w_uk", 0, KC, h * NOPE, NOPE, None)

    out = {"glr": [[("a_w_in", 0, KD, 2 * HA * DK + 2 * HA * DV, RANK, "a_norm_pre")]]}
    for h in range(HA):
        qk = [[("a_w_in", 0, KD, h * DK, DK, "a_norm_pre")], [("a_w_in", 0, KD, (HA + h) * DK, DK, "a_norm_pre")]]
        v, g = (halves("a_w_in", base + h * DV, "a_norm_pre") for base in (2 * HA * DK, 2 * HA * DK + HA * DV))
        for name, x in ((("v", h), v), (("qk", h), qk), (("g", h), g)) if h == 0 else ((("qk", h), qk), (("v", h), v), (("g", h), g)):
            out[name] = x
    for s in range(4):
        out["wo", "A", s] = halves("a_w_out", s * 256, "a_head_norm")
    out["kvc"] = halves("kv_w_down", 0, "kv_norm")
    out["ql0"] = halves("b_w_in", 0, "b_norm_pre")
    out["kq"] = [[("kv_w_down", k, k + 4, KL, ROPE, "kv_norm"), ("b_w_in", k, k + 4, 256, QL - 256, "b_norm_pre")] for k in (0, 4)]
    gb = {("gb", s): halves("b_w_in", QL + s * 256, "b_norm_pre") for s in range(4)}
    uqr = [[("uq_rope", 0, KQ, h * ROPE, 4 * ROPE, "b_q_norm")] for h in (0, 4)]
    pre = {("pre", p): [list(nope(2 * p + i)) for i in range(2)] for p in range(HB // 2)}
    for name in (("gb", 3), ("gb", 2), "uqr", ("gb", 1), ("pre", 0), ("pre", 1), ("gb", 0), ("pre", 2), ("pre", 3)):
        out[name] = uqr if name == "uqr" else gb.get(name) or pre[name]
    for h in range(HB):
        out["hd", h] = [[*nope(h), ("kv_w_uv", h % 2, h % 2 + 1, (h // 2) * 2 * VB, 2 * VB, None)]]
    for s in range(4):
        out["wo", "B", s] = halves("b_w_out", s * 256, None)
        if s == 0:
            out["uv"] = [[("kv_w_uv", k, k + 1, 0, HB * VB, None)] for k in range(KC)]
    return out


SLABS = slabs()
SLAB_NO = {name: n for n, name in enumerate(SLABS)}
SLAB_AT = {name: n % 2 for name, n in SLAB_NO.items()}
SLAB_AT["wo", "B", 1], SLAB_AT["wo", "B", 2], SLAB_AT["wo", "B", 3] = 2, SLAB_AT["uv"], SLAB_AT["wo", "B", 0]
BEFORE = {}
for _name in SLABS:
    BEFORE[_name] = ([m for m in list(SLABS)[:SLAB_NO[_name]] if SLAB_AT[m] == SLAB_AT[_name]] or [None])[-1]
PIECES = [(name, j) for name, pieces in SLABS.items() for j in range(len(pieces))]
PIECE_NO = {p: n for n, p in enumerate(PIECES)}


def stage_counts():
    count, out = [0] * NSTAGE, []
    for n, (name, j) in enumerate(PIECES):
        for w, k0, k1, *_ in SLABS[name][j]:
            count[n % NSTAGE] += 16 * (k1 - k0 if w == "uq_rope" else 1)
        out.append(count[n % NSTAGE])
    return out


STAGE_COUNT = stage_counts()


def steps():
    out = []

    def load(name):
        out.extend(("piece", name, j) for j in range(len(SLABS[name])))

    out += [("xn", 0), ("xn", 1)]
    load("glr")
    out += [("xT", "A", 0), ("piece", ("v", 0), 0), ("xT", "A", 1), ("piece", ("v", 0), 1), ("xn", 2), ("xn", 3), ("vt", 0),
            ("xT", "A", 2), ("xn", 4), ("xT", "A", 3), ("xT", "A", 4), ("vt", 1), ("glr",), ("const",)]
    for t in range(NT):
        out += [("z", t)]
    out += [("ln",), ("lg", 0), ("lg", 1), ("lgh", 0), ("vt", 2), ("vt", 3), ("c", 0), ("lgh", 1), ("vt", 4),
            ("lg", 2), ("lg", 3), ("lgh", 2), ("c", 1)]
    load(("qk", 0))
    out += [("lgh", 3), ("lg", 4), ("c", 2), ("lgh", 4), ("qp", 0), ("c", 3), ("c", 4)]
    out += [("lds", 0)]
    for h in range(HA):
        last = h + 1 == HA
        out += [("e", h)]
        if h:
            out += [("qp", h)]
        out += [("q", h)]
        if h == 0:
            load(("g", 0))
        out += [("k", h), ("qlo", h), ("klo", h)]
        if h:
            load(("g", h))
            out += [("v", h)]
        out += [("kT", h)]
        if h:
            out += [("vs", h)]
        else:
            out += [("gt", h)]
        out += [("sc", h)]
        load(("wo", "A", 0) if last else ("qk", h + 1))
        if last:
            out += [("sclo", h), ("U", h), ("Slo", h), ("stp", h), ("os", h), ("Us", h, 0), ("Us", h, 1), ("sts", h), ("o", h), ("ldr",)]
            for t in range(NT):
                out += [("gl", t)]
                if t:
                    out += [("oT", t - 1)]
            load(("wo", "A", 1))
            out += [("oT", NT - 1)]
        else:
            if h:
                out += [("gt", h)]
            out += [("gts", h), ("sclo", h), ("U", h), ("Slo", h), ("stp", h), ("os", h), ("Us", h, 0), ("Us", h, 1), ("sts", h)]
            load(("v", h + 1))
            out += [("o", h), ("lds", h + 1)]
    project_out(out, load, "A")
    latent_layer(out, load)
    project_out(out, load, "B")
    return out


def project_out(out, load, ph):
    if ph == "A":
        for s in range(3):
            out += [("y", ph, s), ("ys", ph, s)]
            load(("wo", ph, s + 2) if s < 2 else "kvc")
    else:
        out += [("y", ph, 0), ("so",), ("soh",)]
        load(("wo", ph, 2))
        out += [("y", ph, 1), ("ys", ph, 0)]
        load(("wo", ph, 3))
        out += [("ys", ph, 1), ("y", ph, 2), ("ys", ph, 2)]
    if ph == "B":
        for t in range(NT):
            out += [("yt", ph, t), ("r", ph, t), ("oy", t)]
        return
    for t in range(NT + 4):
        if t < NT:
            out += [("yt", ph, t), ("r", ph, t), ("keep", t)]
        if 0 <= t - 1 < NT:
            out += [("rs", t - 1), ("rx", t - 1)]
        if 0 <= t - 3 < NT:
            out += [("xT", "B", t - 3)]
        if t == NT + 1:
            load("ql0")
        if 0 <= t - 4 < NT:
            out += [("lc", t - 4)]


def latent_layer(out, load):
    out += [("lcn",)]
    load("kq")
    out += [("qa",), ("qas",)]
    load(("gb", 3))
    out += [("kq",), ("kqs",), ("cn",), ("och",), ("qs",)]
    load(("gb", 2))
    out += [("gb", 3, 0), ("cT", 0), ("cT", 1), ("gb", 3, 1), ("cT", 2), ("cT", 3), ("cT", 4)]
    load("uqr")
    out += [("gb", 2, 0)] + [("qT", t) for t in range(NT)] + [("gb", 2, 1)]
    load(("gb", 1))
    out += [("qr", 0), ("qr", 1), ("gb", 1, 0), ("qrT", 0), ("qr", 2), ("qrT", 1), ("qr", 3), ("qrT", 2), ("qr", 4)]
    load(("pre", 0))
    out += [("gb", 1, 1)]
    out += [("qrT", 3), ("qns", 0), ("wt", 0)]
    load(("pre", 1))
    load(("gb", 0))
    out += [("qrT", 4), ("qabs", 0), ("qns", 1), ("wt", 1)]
    load(("pre", 2))
    out += [("gb", 0, 0), ("qabs", 1), ("qns", 2), ("wt", 2), ("ldc", 0), ("ldc", 1), ("gb", 0, 1)]
    load(("pre", 3))
    load(("hd", 0))
    out += [("qabs", 2), ("ct", 0), ("cr", 0), ("qns", 3), ("wt", 3)]
    load(("hd", 1))
    out += [("qn", 0), ("kh", 0), ("qabs", 3)]
    for h in range(HB):
        more = h + 1 < HB
        out += [("S", h, 0), ("S", h, 1), ("N", h, 0), ("N", h, 1)]
        if not more:
            out += [("sv", h - 1)]
        out += [("ss", h), ("cs", h)]
        if h:
            out += [("cx", h - 1)]
        else:
            out += [("vh", 0)]
        if more:
            out += [("qn", h + 1), ("kh", h + 1)]
        out += [("T", h, 0), ("T", h, 1), ("st", h)]
        if h + 2 < HB:
            load(("hd", h + 2))
        if more:
            out += [("ct", h + 1), ("cr", h + 1)]
            if h + 2 < HB:
                out += [("ldc", h + 2)]
        else:
            load(("wo", "B", 0))
        out += [("O", h), ("Oh", h)]
        if not more:
            out += [("sv", h)]
        if h + 2 < HB:
            if h % 2:
                out += [("vh", h // 2 + 1)]
        if h + 2 < HB:
            out += [("sv", h)]
    load("uv")
    out += [("cx", SB - 1), ("ldk",)]
    load(("wo", "B", 1))


PARTS = {
    "const": ("act",), "piece": ("sp", "pool", "act", "dve"), "lds": ("sp",), "sts": ("sp",), "stp": ("sp",), "ldr": ("sp",),
    "och": ("sp",), "ldc": ("sp",), "oy": ("sp",), "keep": ("sp",), "ldk": ("sp",), "yt": ("pe", "act"),
    "qns": ("pe", "act", "dve"), "xn": ("act", "pool", "dve"), "xT": ("pe", "act", "dve"), "glr": ("pe", "act"),
    "z": ("pe", "dve", "act"), "ln": ("act",), "lg": ("dve",), "lgh": ("act", "dve"), "qp": ("pe",), "rs": ("act",),
    "c": ("pe", "act"), "e": ("act",),
    "q": ("dve", "act"), "k": ("pe", "dve", "act"), "qlo": ("dve",), "klo": ("dve",),
    "v": ("pe", "act", "dve"), "vs": ("pe", "act", "dve"), "kT": ("pe", "act", "dve"), "sc": ("pe", "dve", "act"),
    "sclo": ("dve",), "gt": ("pe", "act", "dve"), "gts": ("pe", "act", "dve"), "U": ("pe", "dve", "act"),
    "Slo": ("dve",), "os": ("pe", "act", "pool", "dve"), "o": ("pe", "act", "pool", "dve"), "Us": ("pe", "dve"),
    "oT": ("pe", "act", "dve"), "y": ("pe", "act", "dve"), "ys": ("pe", "act", "dve"), "r": ("pool", "dve"),
    "rx": ("pool", "dve"), "lc": ("pe", "act", "dve"), "lcn": ("pool", "dve"), "vt": ("pe", "act", "dve"), "gl": ("pe", "act", "dve"),
    "cn": ("act", "dve"), "cT": ("pe", "act", "dve"), "qa": ("pe", "act", "dve"), "qas": ("pe", "act", "dve"),
    "kq": ("pe", "act", "dve"), "kqs": ("pe", "act", "dve"), "qs": ("pool", "dve"), "gb": ("pe", "act", "dve"),
    "qT": ("pe", "act", "dve"), "qr": ("pe", "dve"), "qrT": ("pe", "act", "dve"), "qn": ("pe", "act", "dve"),
    "wt": ("pe", "act"), "N": ("dve",), "Oh": ("act", "dve"), "cx": ("pe", "act", "dve"), "soh": ("act", "dve"),
    "kh": ("pe", "act", "dve"), "vh": ("pe", "act", "dve"), "qabs": ("pe", "act", "dve"),
    "S": ("pe", "dve", "act"), "T": ("pe", "act", "dve"), "O": ("pe", "dve"), "ct": ("pe", "act", "dve"),
    "cr": ("pe", "act", "dve"), "ss": ("pe", "dve", "act"), "cs": ("pool",),
    "st": ("pe", "act", "dve"), "sv": ("pe", "dve"), "so": ("pe", "dve"),
}


def parts(step):
    if step[0] == "piece" and not any(w[5] for w in SLABS[step[1]][step[2]]):
        return ("sp", "act", "dve")
    return PARTS[step[0]]


LAST_READER = {k: [e for e in p if e in ("act", "dve")][-1] for k, p in PARTS.items() if "pe" in p and len(p) > 1}
LAST_READER.update({k: "dve" for k in ("k", "sc", "U")})
LAST_READER["S"] = LAST_READER["ss"] = LAST_READER["z"] = "act"

STEPS = steps()
assert len(set(STEPS)) == len(STEPS)


def count_parts():
    at = {e: {} for e in ("pe", "act", "dve", "pool")}
    for s in STEPS:
        for e in at.keys() & set(parts(s)):
            at[e][s] = len(at[e]) + 1
    return at


AT = count_parts()


def read_out(step):
    if step[0] in ("yt", "qp"):
        return "dve", {"yt": "r", "qp": "q"}[step[0]], *step[1:]
    return LAST_READER[step[0]], *step


BANKED = [s for s in STEPS if "pe" in PARTS[s[0]]]
BANK_NO = {s: n for n, s in enumerate(BANKED)}
USERS = {"glr": ("glr",), "kvc": ("lc", NT - 1), "ql0": ("qas",), "kq": ("kqs",), "uqr": ("qr", NT - 1), "uv": ("so",)}
for _h in range(HA):
    USERS["qk", _h] = ("k", _h)
    USERS["v", _h] = ("vs", _h) if _h else ("vt", NT - 1)
    USERS["g", _h] = ("gts", _h) if _h + 1 < HA else ("gl", NT - 1)
for _ph in "AB":
    for _s in range(4):
        USERS["wo", _ph, _s] = ("ys", _ph, _s) if _s < 3 else ("yt", _ph, NT - 1)
for _s in range(4):
    USERS["gb", _s], USERS["pre", _s] = ("gb", _s, 1), ("wt", _s)
for _h in range(HB):
    USERS["hd", _h] = ("kh", _h) if _h % 2 else ("vh", _h // 2)

STAT = {}
for _name, _n in [(("x", t), 1) for t in range(NT)] + [(("x1", t), 1) for t in range(NT)] \
        + [(("o", h), NT) for h in range(HA)] + [(("y", ph, t), 4) for ph in "AB" for t in range(NT)] \
        + [(("yr", ph, t), 1) for ph in "AB" for t in range(NT)] + [(("lat",), NT), (("qa",), NT), (("qb",), NT)] \
        + [(("S", h, u), 2) for h in range(HB) for u in range(2)] + [(("ss", b), 1) for b in range(SB)]:
    STAT[_name] = (sum(b - a for a, b in STAT.values()), sum(b - a for a, b in STAT.values()) + _n)
NSTAT = max(b for _, b in STAT.values())

UNITS = ((3, 0), (2, 1))
KEY_UNITS = ((0, 3), (1, 2))


def program(nc, dram, outs):
    fp32, fp32r = mybir.dt.float32, mybir.dt.float32r
    ALU, ACT, AX = mybir.AluOpType, mybir.ActivationFunctionType, mybir.AxisListType
    MUL, ADD, SUB = ALU.mult, ALU.add, ALU.subtract
    (y_prompt, y_sample, st_prompt, st_sample, ckv_prompt, krope_prompt, ckv_sample, krope_sample) = outs
    kept = nc.dram_tensor("kept_rows", (P, NT, D), fp32, kind="Internal").ap()
    w_dram = {n: dram[n].rearrange("(k p) n -> p k n", p=P) for n in
              ("kv_w_down", "kv_w_uk", "kv_w_uv")}
    for n in ("a_w_in", "a_w_out", "b_w_in", "b_w_uq", "b_w_out"):
        w_dram[n] = dram[n][0].rearrange("(k p) n -> p k n", p=P)
    uq_rope = w_dram["b_w_uq"].rearrange("p k (h n) -> p k h n", n=NOPE + ROPE)

    ctx = ExitStack()
    with ctx:
        def sem(name):
            return ctx.enter_context(nc.semaphore(name))

        place = [-(-nc.sbuf_base // 64) * 64]

        def sb(name, shape, dt=fp32):
            size = 2 if dt == mybir.dt.bfloat16 else 4
            for n in shape[1:]:
                size *= n
            at = place[0]
            place[0] += -(-size // 32) * 32
            assert place[0] <= nc.sbuf_usable_end, (name, place[0], nc.sbuf_usable_end)
            return nc.alloc_sbuf_tensor_at(name, shape, dt, offset=at)

        def pair(name, shape):
            return sb(name + "_hi", shape, fp32r), sb(name + "_lo", shape, fp32r)

        def raw(ap):
            return ap.bitcast(fp32)

        def over(ap, n):
            return ap.unsqueeze(2).to_broadcast([ap.shape[0], ap.shape[1], n])

        def times(ap, n):
            return ap.unsqueeze(1).to_broadcast([ap.shape[0], n, ap.shape[1]])

        stage = [sb(f"stage{i}", [P, PIECE]) for i in range(NSTAGE)]
        slab_at = [place[0] + 8 * PIECE * i for i in range(4)]
        slab = [pair(f"slab{i}", [P, 2 * PIECE]) for i in range(2)]
        const = sb("const", [P, NCONST])
        const_r = sb("const_r", [P, NCONST_R], fp32r)
        gain = {n: sb("gain_" + n, [P, k]) for n, k in
                (("a_norm_pre", KD), ("a_head_norm", KD), ("kv_norm", KD), ("b_norm_pre", KD), ("b_q_norm", KQ))}
        post = sb("post", [P, D])
        lat_gain = sb("lat_gain", [P, KL])
        minus_half = sb("minus_half", [P, 8])
        stat = sb("stat", [P, NSTAT])
        stat2 = sb("stat2", [P, NSTAT])
        junk = sb("junk", [P, D], mybir.dt.bfloat16)
        rows_at = place[0]
        rows = sb("rows", [P, NT, D])
        gate_at = place[0]
        gate_w = sb("gate_w", [RANK + 1, HA * DK])
        hat_at = place[0]
        hat = pair("hat", [P, KD, TOK])
        phase_at = place[0]
        glrT = sb("glrT", [RANK + 1, TOK])
        cumT = sb("cumT", [P, HA, TOK])
        decay = sb("decay", [P, HA, NT])
        Ep, Em = sb("Ep", [P, TOK]), sb("Em", [P, TOK])
        eB = sb("eB", [P, NT])
        tmp = sb("tmp", [P, TOK])
        vv = pair("vv", [P, NT, DV])
        v_s = sb("v_s", [P, DV])
        z_at = place[0]
        qT, kT = pair("qT", [P, TOK]), pair("kT", [P, TOK])
        kn = pair("kn", [P, NT, DK])
        kt_at = place[0]
        scT = pair("scT", [P, TOK])
        scT_end, place[0] = place[0], kt_at
        kt = sb("kt", [P, TOK])
        place[0] = scT_end
        st_in = sb("st_in", [P, NP, DV])
        st = pair("st", [P, NP, DV])
        st_s = sb("st_s", [P, SB, DV])
        k_own = sb("k_own", [P, SB, DK])
        q_own = sb("q_own", [P, SB, P])
        th = st_in[:, :, :].rearrange("p t n -> p (t n)")
        place[0] = z_at
        z_abs, z_min = sb("z_abs", [P, NT, HA * DK]), sb("z_min", [P, NT, HA * DK])
        lg = pair("lg", [P, NT, HA * DK])
        const_raw = sb("const_raw", [P, NCONST_R])
        place[0] = phase_at
        qS_at = place[0]
        x1 = sb("x1", [P, NT, D])
        qlT_at = place[0]
        qlT = pair("qlT", [P, KQ, TOK])
        cT = pair("cT", [P, KC, TOK])
        krS = sb("krS", [P, TOK], fp32r)
        krL = sb("krL", [ROPE, TOK], fp32r)
        cn_s = pair("cn_s", [P, KL])
        qab = pair("qab", [P, KC, SB, HB * SL])
        temp_at = place[0]
        ckvn = sb("ckvn", [P, NT, KL])
        krn = sb("krn", [P, NT, ROPE])
        thb = sb("thb", [P, TOK])
        wT = pair("wT", [P, 2 * KL])
        qN_s = pair("qN_s", [P, 2 * P])
        flat_rows = rows[:, :, :].rearrange("p t d -> p (t d)")
        qln = flat_rows[:, 0:NT * QL].rearrange("p (t n) -> p t n", n=QL)
        gateT = flat_rows.rearrange("p (h n) -> p h n", n=TOK)
        place[0] = rows_at
        oT_lo = sb("oT_lo", [P, HB, TOK], fp32r)
        place[0] = qlT_at
        y_rows = sb("y_rows", [P, NT, D])
        place[0] = qS_at
        qS = sb("qS", [P, HB, SEQ], fp32r)
        qS_s_at = place[0]
        qS_s = sb("qS_s", [P, SB, HB, SL], fp32r)
        place[0] = qS_s_at
        oS_s = sb("oS_s", [P, HB, P], fp32r)
        place[0] = temp_at
        qrn, rtmp = [sb(f"qrn{i}", [P, HB * ROPE]) for i in range(2)], sb("rtmp", [P, HB * ROPE])
        place[0] = temp_at
        pT = [pair(f"pT{i}", [P, TOK]) for i in range(2)]
        prob = [sb(f"prob{i}", [P, NT, P]) for i in range(2)]
        place[0] = hat_at
        qN = pair("qN", [P, SEQ])
        kN = pair("kN", [P, SEQ])
        sT = pair("sT", [P, KC, PAST])
        cn = pair("cn", [P, PAST // P, KL])
        spT = pair("spT", [P, TOK])
        skS = sb("skS", [P, PAST], fp32r)
        skL = sb("skL", [ROPE, PAST], fp32r)
        sprob = sb("sprob", [P, NT, P])
        ctxn = sb("ctxn", [P, KL])
        assert place[0] <= phase_at
        place[0] = hat_at
        xB = sb("xB", [P, NT, D])
        slab.append(pair("slab2", [P, 2 * PIECE]))
        free = SLAB_AT["pre", 2]
        place[0] = slab_at[2 * (1 - free)] + 4 * PIECE
        vN_hi = sb("vN_hi", [P, NP, 2 * VB], fp32r)
        place[0] = slab_at[2 * (1 - free) + 1] + 4 * PIECE
        vN_lo = sb("vN_lo", [P, NP, 2 * VB], fp32r)
        vN = (vN_hi, vN_lo)
        craw = []
        for i in range(2):
            place[0] = slab_at[2 * free + i] + 4 * PIECE
            craw.append(sb(f"craw{i}", [P, PAST // P, KL]))
        place[0] = gate_at
        kraw = [sb(f"kraw{i}", [P, PAST // P, ROPE]) for i in range(2)]

        pb = [ctx.enter_context(nc.psum_tensor(f"bank{i}", [P, 2, 512], fp32)) for i in range(NBANK)]
        flat = [b[:, :, :].rearrange("p a n -> p (a n)") for b in pb]

        def cst(name, p=P):
            a, b = CONST[name]
            return const[0:p, a:b]

        def cst_r(name, p=P):
            a, b = CONST_R[name]
            return const_r[0:p, a:b]

        ident = cst("ident")

        def rotary_to(t, p):
            return qS[p, :, t * P:(t + 1) * P] if t < NP else qS_s[p, :, :, :].rearrange("p b h n -> p h b n")

        def rotary_from(row, t):
            v = row[0:ROPE, :].rearrange("p (h n) -> p h n", n=P)
            return v if t < NP else v.rearrange("p h (b n) -> p h b n", n=SL)

        def by_stream(x, h):
            return x.rearrange("p k b (h n) -> p k b h n", n=SL)[:, :, :, h, :]

        def S1(name, src=None, t=None):
            a, b = STAT[name]
            src = stat if src is None else src
            return src[:, a:b] if t is None else src[:, a + t:a + t + 1]

        done = {"pe": sem("tensor_done"), "act": sem("scalar_done"), "dve": sem("vector_done"), "pool": sem("gpsimd_done")}
        act_own, dve_own, pool_own = sem("scalar_own"), sem("vector_own"), sem("gpsimd_own")
        consts_in, const_r_in, x_in, gains_in = sem("consts_in"), sem("const_r_in"), [sem(f"x{t}_in") for t in range(NT)], sem("gains_in")
        stage_in = [sem(f"stage{i}_in") for i in range(NSTAGE)]
        state_in, state_out, final_out, rest_in, post_in = sem("state_in"), sem("state_out"), sem("final_out"), sem("rest_in"), sem("post_in")
        cache_in = [sem(f"cache{i}_in") for i in range(2)]
        latent_out, y_out, kept_out = sem("latent_out"), sem("y_out"), sem("kept_out")
        ones_set, own_set, gate_in = sem("ones_set"), sem("own_set"), sem("gate_in")

        def after(eng, who, *step):
            eng.wait_ge(done[who], AT[who][step])

        def before_bank(eng, step):
            n = BANK_NO[step]
            if n >= NBANK:
                after(eng, *read_out(BANKED[n - NBANK]))
            return pb[n % NBANK], flat[n % NBANK]

        def banks(step):
            n = BANK_NO[step] % NBANK
            return pb[n], flat[n]

        def weights(name):
            return slab[SLAB_AT[name]]

        def spot(n, i):
            name, j = PIECES[n]
            _w, k0, k1, _c0, cols, _g = SLABS[name][j][i]
            if name == "kq":
                wide = sum(w[4] for w in SLABS[name][j])
                at = sum(w[4] for w in SLABS[name][j][:i])
                return stage[n % NSTAGE][:, 0:(k1 - k0) * wide].rearrange("p (k n) -> p k n", n=wide)[:, :, at:at + cols]
            at = sum((w[2] - w[1]) * w[4] for w in SLABS[name][j][:i])
            return stage[n % NSTAGE][:, at:at + (k1 - k0) * cols].rearrange("p (k n) -> p k n", n=cols)

        def used(name, j):
            return sum((w[2] - w[1]) * w[4] for w in SLABS[name][j])

        block = ctx.enter_context(nc.Block())

        @block.sync
        def _(sp):
            def load_piece(name, j):
                n = PIECE_NO[name, j]
                if n >= NSTAGE:
                    after(sp, "dve", "piece", *PIECES[n - NSTAGE])
                for i, (w, k0, k1, c0, cols, _g) in enumerate(SLABS[name][j]):
                    to = spot(n, i)
                    if w == "uq_rope":
                        h0 = c0 // ROPE
                        for k in range(k0, k1):
                            sp.dma_start(to[:, k, :].rearrange("p (h n) -> p h n", n=ROPE),
                                         uq_rope[:, k, h0:h0 + 4, NOPE:NOPE + ROPE]).then_inc(stage_in[n % NSTAGE], 16)
                    else:
                        sp.dma_start(to, w_dram[w][:, k0:k1, c0:c0 + cols]).then_inc(stage_in[n % NSTAGE], 16)

            def load_x(t):
                sp.dma_start(rows[:, t, :], dram["x_prompt"][0, t * P:(t + 1) * P, :] if t < NP
                             else dram["x_sample"].rearrange("b l d -> (b l) d")).then_inc(x_in[t], 16)

            load_x(0)
            sp.dma_start(const[:, :], dram["const"]).then_inc(consts_in, 16)
            load_x(1)
            for n, g in gain.items():
                sp.dma_start(g[:, :], dram[n]).then_inc(gains_in, 16)
            load_piece(*PIECES[0])
            load_piece(*PIECES[1])
            load_piece(*PIECES[2])
            load_x(2)
            for t in range(3, NT):
                load_x(t)
            load_piece(*PIECES[3])
            sp.dma_start(gate_w[0:RANK, :], dram["a_w_gate2"][0]).then_inc(gate_in, 16)
            sp.dma_start(gate_w[RANK:RANK + 1, :], dram["a_b_gate"]).then_inc(gate_in, 16)
            sp.dma_start(const_raw[:, :], dram["const_r"]).then_inc(const_r_in, 16)
            sp.dma_start(post[:, :], dram["a_norm_post"].to_broadcast([P, D])).then_inc(post_in, 16)
            sp.dma_start(lat_gain[:, :], dram["kv_latent_norm"].unsqueeze(0).to_broadcast([P, KL])).then_inc(post_in, 16)
            for step in STEPS:
                if "sp" not in parts(step):
                    continue
                kind = step[0]
                if kind == "piece":
                    n = PIECE_NO[step[1], step[2]] + NSTAGE
                    if n < len(PIECES):
                        load_piece(*PIECES[n])
                elif kind == "lds":
                    h = step[1]
                    if h:
                        sp.wait_ge(state_out, 16 * h)
                    else:
                        after(sp, "pe", "c", NT - 1)
                    sp.dma_start(st_s[:, :, :], dram["state_gla"][0, :, h].rearrange("b k v -> k b v")).then_inc(state_in, 16)
                elif kind == "sts":
                    h = step[1]
                    after(sp, "dve", "Us", h, 1)
                    sp.dma_start(st_sample[0, :, h].rearrange("b k v -> k b v"), st_s[:, :, :]).then_inc(state_out, 16)
                elif kind == "stp":
                    h = step[1]
                    after(sp, "dve", "U", h)
                    sp.dma_start(st_prompt[0, 0, h], st_in[:, 0, :]).then_inc(final_out, 16)
                elif kind == "ldr":
                    for who, s in (("dve", ("Us", HA - 1, 1)), ("act", ("o", HA - 1)), ("pe", ("Us", HA - 1, 1))):
                        after(sp, who, *s)
                    sp.dma_start(x1[:, 0:NP, :], dram["x_prompt"][0].rearrange("(t p) d -> p t d", p=P)).then_inc(rest_in, 16)
                    sp.dma_start(x1[:, NP, :], dram["x_sample"].rearrange("b l d -> (b l) d")).then_inc(rest_in, 16)
                elif kind == "keep":
                    t = step[1]
                    after(sp, "dve", "r", "A", t)
                    sp.dma_start(kept[:, t, :], x1[:, t, :]).then_inc(kept_out, 16)
                elif kind == "ldk":
                    after(sp, "pe", "cx", SB - 1)
                    sp.wait_ge(kept_out, 16 * NT)
                    sp.dma_start(xB[:, :, :], kept).then_inc(rest_in, 16)
                elif kind == "och":
                    after(sp, "dve", "lcn")
                    after(sp, "dve", "kqs")
                    after(sp, "dve", "r", "A", NT - 1)
                    sp.dma_start(post[:, :], dram["b_norm_post"].to_broadcast([P, D])).then_inc(post_in, 16)
                    sp.dma_start(ckv_prompt[0].rearrange("(t p) n -> p t n", p=P), ckvn[:, 0:NP, :]).then_inc(latent_out, 16)
                    sp.dma_start(ckv_sample.rearrange("b l n -> (b l) n"), ckvn[:, NP, :]).then_inc(latent_out, 16)
                    sp.dma_start(krope_prompt[0].rearrange("(t p) n -> p t n", p=P), krn[:, 0:NP, :]).then_inc(latent_out, 16)
                    sp.dma_start(krope_sample.rearrange("b l n -> (b l) n"), krn[:, NP, :]).then_inc(latent_out, 16)
                elif kind == "ldc":
                    b = step[1]
                    if b < 2:
                        after(sp, "pe", "wt", 2)
                    else:
                        after(sp, "pool", "cs", b - 2)
                        after(sp, "pe", "cr", b - 2)
                    sp.dma_start(craw[b % 2][:, :, :], dram["cache_ckv"][b].rearrange("(s p) n -> p s n", p=P)).then_inc(cache_in[b % 2], 16)
                    sp.dma_start(kraw[b % 2][:, :, :], dram["cache_krope"][b].rearrange("(s p) n -> p s n", p=P)).then_inc(cache_in[b % 2], 16)
                elif kind == "oy":
                    t = step[1]
                    after(sp, "dve", "r", "B", t)
                    sp.dma_start(y_prompt[0, t * P:(t + 1) * P, :] if t < NP else y_sample.rearrange("b l d -> (b l) d"),
                                 xB[:, t, :]).then_inc(y_out, 16)
            sp.wait_ge(y_out, 16 * NT)
            sp.wait_ge(latent_out, 16 * 4)
            sp.wait_ge(state_out, 16 * HA)
            sp.wait_ge(final_out, 16 * HA)

        @block.gpsimd
        def _(pool):
            own = [0]

            def link(ins):
                own[0] += 1
                ins.then_inc(pool_own, 1)
                pool.wait_ge(pool_own, own[0])

            def rms(name, width, count, factor=1.0):
                s, r = S1(name), S1(name, stat2)
                link(pool.tensor_scalar(r, s, 1.0 / width, EPS, MUL, ADD))
                if factor == 1.0:
                    return pool.tensor_tensor(r, r, minus_half[:, 0:count], ALU.pow)
                link(pool.tensor_tensor(r, r, minus_half[:, 0:count], ALU.pow))
                return pool.tensor_scalar(r, r, factor, None, MUL)

            pool.memset(q_own[:, :, :], 0.0).then_inc(own_set, 1)
            pool.memset(glrT[:, :], 1.0).then_inc(ones_set, 1)
            link(pool.memset(minus_half[:, :], -0.5))
            pool.wait_ge(gains_in, 16 * len(gain))
            for step in STEPS:
                if "pool" not in parts(step):
                    continue
                kind = step[0]
                if kind == "piece":
                    _, name, j = step
                    n = PIECE_NO[name, j]
                    pool.wait_ge(stage_in[n % NSTAGE], STAGE_COUNT[n])
                    for i, (w, k0, k1, c0, cols, g) in enumerate(SLABS[name][j]):
                        if g:
                            last = pool.tensor_tensor(spot(n, i), spot(n, i), over(gain[g][:, k0:k1], cols), MUL)
                elif kind == "xn":
                    after(pool, "act", *step)
                    last = rms(("x", step[1]), D, 1)
                elif kind in ("o", "os"):
                    after(pool, "act", *step)
                    h = step[1]
                    a, _b = STAT["o", h]
                    a, m = (a, NP) if kind == "o" else (a + NP, 1)
                    s, r = stat[:, a:a + m], stat2[:, a:a + m]
                    link(pool.tensor_scalar(r, s, 1.0 / DV, EPS, MUL, ADD))
                    link(pool.tensor_tensor(r, r, minus_half[:, 0:m], ALU.pow))
                    last = pool.tensor_scalar(r, r, 0.5, None, MUL)
                elif kind == "r":
                    _, ph, t = step
                    after(pool, "act", "yt", ph, t)
                    s, r = S1(("y", ph, t)), S1(("yr", ph, t), stat2)
                    link(pool.tensor_tensor(s[:, 0:2], s[:, 0:2], s[:, 2:4], ADD))
                    link(pool.tensor_tensor(r, s[:, 0:1], s[:, 1:2], ADD))
                    link(pool.tensor_scalar(r, r, 1.0 / D, EPS, MUL, ADD))
                    last = pool.tensor_tensor(r, r, minus_half[:, 0:1], ALU.pow)
                elif kind == "cs":
                    b = step[1]
                    pool.wait_ge(cache_in[b % 2], 32 * (b // 2 + 1))
                    after(pool, "pe", *(("sv", b - 1) if b else ("gb", 0, 1)))
                    link(pool.tensor_copy(cn[0][:, :, :], craw[b % 2][:, :, :]))
                    last = pool.tensor_tensor(cn[1][:, :, :], craw[b % 2][:, :, :], raw(cn[0][:, :, :]), SUB)
                elif kind == "rx":
                    after(pool, "act", "rs", step[1])
                    last = rms(("x1", step[1]), D, 1)
                elif kind == "lcn":
                    after(pool, "act", "lc", NT - 1)
                    last = rms(("lat",), KL, NT)
                elif kind == "qs":
                    after(pool, "act", "kqs")
                    s, r = S1(("qa",)), S1(("qa",), stat2)
                    link(pool.tensor_tensor(r, s, S1(("qb",)), ADD))
                    link(pool.tensor_scalar(r, r, 1.0 / QL, EPS, MUL, ADD))
                    last = pool.tensor_tensor(r, r, minus_half[:, 0:NT], ALU.pow)
                last.then_inc(done["pool"], 1)
                pool.wait_ge(done["pool"], AT["pool"][step])

        @block.scalar
        def _(act):
            def copy(out, in_):
                return act.activation(out, in_, ACT.Copy)

            act.wait_ge(consts_in, 16)
            for step in STEPS:
                if "act" not in parts(step):
                    continue
                kind = step[0]
                who = parts(step)[parts(step).index("act") - 1] if parts(step)[0] != "act" else None
                if who and who != "sp":
                    after(act, who, *step)
                bank, row = banks(step) if step in BANK_NO else (None, None)
                if kind == "const":
                    act.wait_ge(const_r_in, 16)
                    last = copy(const_r[:, :], const_raw[:, :])
                elif kind == "piece":
                    _, name, j = step
                    n = PIECE_NO[name, j]
                    if who == "sp":
                        act.wait_ge(stage_in[n % NSTAGE], STAGE_COUNT[n])
                    if name == ("wo", "B", 0):
                        after(act, "pe", "cr", SB - 1)
                        after(act, "pool", "cs", SB - 1)
                    elif name == ("wo", "B", 1):
                        after(act, "pe", "cx", SB - 1)
                    elif name == "uv":
                        after(act, "pe", "O", HB - 1)
                    if BEFORE[name]:
                        after(act, "pe", *USERS[BEFORE[name]])
                    m = used(name, j)
                    last = copy(weights(name)[0][:, j * PIECE:j * PIECE + m], stage[n % NSTAGE][:, 0:m])
                elif kind == "xn":
                    t = step[1]
                    act.wait_ge(x_in[t], 16)
                    last = act.activation(junk[:, :], rows[:, t, :], ACT.Square, accum_out=S1(("x", t)))
                elif kind in ("xT", "oT"):
                    t = step[-1]
                    last = copy(hat[0][:, :, t * P:(t + 1) * P], row.rearrange("p (k n) -> p k n", n=P))
                elif kind == "glr":
                    act.wait_ge(ones_set, 1)
                    last = copy(glrT[0:RANK, :].rearrange("p (a n) -> p a n", a=2), bank[0:RANK, :, 0:HALF])
                elif kind == "z":
                    v = z_abs[:, step[1], :]
                    act.activation(v, bank[:, 0, :], ACT.Abs).then_inc(act_own, 1)
                    act.wait_ge(act_own, step[1] + 1)
                    last = act.activation(v, v, ACT.Exp, scale=-1.0)
                elif kind == "ln":
                    last = act.activation(z_abs[:, :, :], z_abs[:, :, :], ACT.Ln, bias=1.0)
                elif kind == "c":
                    t = step[1]
                    v = bank[:, :, 0:2 * (P + 2)].rearrange("p a (h n) -> p a h n", n=P + 2)
                    copy(cumT[:, :, t * P:(t + 1) * P].rearrange("p (a h) n -> p a h n", a=2), v[:, :, :, 0:P])
                    last = copy(decay[:, :, t:t + 1].rearrange("p (a h) n -> p a h n", a=2), v[:, :, :, P:P + 1])
                elif kind == "e":
                    h = step[1]
                    if h:
                        after(act, "dve", "k", h - 1)
                        after(act, "dve", "Us", h - 1, 1)
                    act.activation(Ep[:, :], cumT[:, h, :], ACT.Exp)
                    act.activation(Em[:, :], cumT[:, h, :], ACT.Exp, scale=-1.0)
                    last = act.activation(eB[:, :], decay[:, h, :], ACT.Exp)
                elif kind == "q":
                    last = copy(qT[0][:, :], tmp[:, :])
                elif kind == "k":
                    last = copy(kT[0][:, :], kt[:, :])
                elif kind == "sc":
                    last = copy(scT[0][:, :], tmp[:, :])
                elif kind == "v":
                    last = copy(vv[0][:, 0:NP, :], row.rearrange("p (t n) -> p t n", n=DV))
                elif kind == "vt":
                    t = step[1]
                    if t == NP:
                        copy(v_s[:, :], bank[:, 0, 0:DV])
                    last = copy(vv[0][:, t, :], bank[:, 0, 0:DV])
                elif kind == "gl":
                    t = step[1]
                    after(act, "dve", *(("Slo", HA - 1) if t < NP else ("gl", 0)))
                    act.wait_ge(final_out, 16 * HA)
                    last = act.activation(th[:, (t % NP) * DV:(t % NP + 1) * DV], bank[:, 0, 0:DV], ACT.Tanh, scale=0.5)
                elif kind == "vs":
                    copy(v_s[:, :], bank[:, 0, 0:DV])
                    last = copy(vv[0][:, NP, :], bank[:, 0, 0:DV])
                elif kind == "kT":
                    last = copy(kn[0][:, :, :], row[:, 0:TOK].rearrange("p (t n) -> p t n", n=DK))
                elif kind == "gt":
                    h = step[1]
                    if h:
                        after(act, "dve", "Slo", h - 1)
                        act.wait_ge(final_out, 16 * h)
                    last = act.activation(th, row, ACT.Tanh, scale=0.5)
                elif kind == "gts":
                    after(act, "dve", "gt", step[1])
                    last = act.activation(th[:, 0:DV], bank[:, 0, 0:DV], ACT.Tanh, scale=0.5)
                elif kind == "U":
                    last = copy(st[0][:, 1:, :], st_in[:, 1:, :])
                elif kind == "o":
                    for t in range(NP):
                        last = act.activation(junk[:, t * DV:(t + 1) * DV], row[:, t * DV:(t + 1) * DV], ACT.Square, accum_out=S1(("o", step[1]), t=t))
                elif kind == "os":
                    last = act.activation(junk[:, 0:DV], row[:, 0:DV], ACT.Square, accum_out=S1(("o", step[1]), t=NP))
                elif kind in ("y", "ys"):
                    _, ph, s = step
                    for i, t in enumerate(range(NP) if kind == "y" else [NP]):
                        last = act.activation(junk[:, i * 256:(i + 1) * 256], row[:, i * 256:(i + 1) * 256], ACT.Square, accum_out=S1(("y", ph, t), t=s))
                elif kind == "yt":
                    _, ph, t = step
                    last = act.activation(junk[:, 0:256], bank[:, 0, 0:256], ACT.Square, accum_out=S1(("y", ph, t), t=3))
                elif kind == "rs":
                    t = step[1]
                    after(act, "dve", "r", "A", t)
                    last = act.activation(junk[:, :], x1[:, t, :], ACT.Square, accum_out=S1(("x1", t)))
                elif kind == "lgh":
                    after(act, "dve", "lg", step[1])
                    last = copy(lg[0][:, step[1], :], z_min[:, step[1], :])
                elif kind == "lc":
                    last = act.activation(junk[:, 0:KL], bank[:, 0, 0:KL], ACT.Square, accum_out=S1(("lat",), t=step[1]))
                elif kind == "cn":
                    after(act, "dve", "lcn")
                    last = copy(cn_s[0][:, :], ckvn[:, NP, :])
                elif kind == "cT":
                    t = step[1]
                    c = slice(t * P, (t + 1) * P)
                    copy(cT[0][:, :, c], bank[:, 0, 0:KL].rearrange("p (k n) -> p k n", n=P))
                    copy(krS[0:ROPE, c], bank[0:ROPE, 1, 0:P])
                    last = copy(krS[ROPE:P, c], bank[0:ROPE, 1, 0:P])
                elif kind in ("qa", "qas", "kq", "kqs"):
                    a = ROPE if kind[0] == "k" else 0
                    m = QL - 256 if kind[0] == "k" else 256
                    for i, t in enumerate([NP] if kind[-1] == "s" else range(NP)):
                        last = act.activation(junk[:, i * 256:i * 256 + m], row[:, i * 256 + a:i * 256 + a + m], ACT.Square,
                                              accum_out=S1(("qb" if kind[0] == "k" else "qa",), t=t))
                elif kind == "qT":
                    t = step[1]
                    last = copy(qlT[0][:, :, t * P:(t + 1) * P], bank[:, 0, 0:QL].rearrange("p (k n) -> p k n", n=P))
                elif kind == "gb":
                    _, s, j = step
                    after(act, "dve", *(("gb", s, 0) if j else ("gb", s + 1, 1) if s < 3 else ("kqs",)))
                    last = act.activation(thb[:, :].rearrange("p (a n) -> p a n", a=2), bank[:, :, 0:HALF], ACT.Tanh, scale=0.5)
                elif kind == "qrT":
                    t = step[1]
                    if t == 0:
                        act.wait_ge(kept_out, 16 * NT)
                    last = copy(rotary_to(t, slice(0, ROPE)), rotary_from(row, t))
                elif kind == "qn":
                    last = copy(qN[0][:, :], bank[:, 0, :])
                elif kind == "qns":
                    last = copy(qN_s[0][:, :], bank[:, 0, 0:2 * P])
                elif kind == "wt":
                    copy(wT[0][:, :], bank[:, 0, :])
                    last = copy(wT[1][:, :], bank[:, 1, :])
                elif kind == "kh":
                    last = copy(kN[0][:, :], bank[:, 0, :])
                elif kind == "vh":
                    last = copy(vN[0][:, :, :], row.rearrange("p (t n) -> p t n", n=2 * VB))
                elif kind == "qabs":
                    for i in range(2):
                        last = copy(by_stream(qab[0][:, :, :, :], 2 * step[1] + i),
                                    bank[:, 0, i * KL:(i + 1) * KL].rearrange("p (k b n) -> p k b n", k=KC, n=SL))
                elif kind == "S":
                    _, h, u = step
                    for j, (i, c0) in enumerate(zip(UNITS[u], (0, UNITS[u][0] + 1))):
                        last = act.activation(prob[u][:, c0:c0 + i + 1, :], bank[:, j, 0:(i + 1) * P].rearrange("p (s n) -> p s n", n=P),
                                              ACT.Exp, scale=SCALE, bias=S1(("S", h, u), stat2, j), accum_out=S1(("S", h, u), t=j))
                elif kind == "T":
                    last = copy(pT[step[2]][0][:, :], row[:, 0:TOK])
                elif kind == "ct":
                    last = copy(sT[0][:, :, :], bank[:, :, :])
                elif kind == "cr":
                    copy(skS[0:ROPE, :], bank[0:ROPE, 0, :])
                    last = copy(skS[ROPE:P, :], bank[0:ROPE, 0, :])
                elif kind == "ss":
                    b = step[1]
                    last = act.activation(sprob[:, :, :], row[:, 0:TOK].rearrange("p (s n) -> p s n", n=P), ACT.Exp,
                                          scale=SCALE, bias=S1(("ss", b), stat2), accum_out=S1(("ss", b)))
                elif kind == "st":
                    last = copy(spT[0][:, :], row[:, 0:TOK])
                elif kind == "cx":
                    last = copy(qab[0][:, :, step[1], :], bank[:, 0, 0:KL].rearrange("p (k n) -> p k n", n=P))
                elif kind == "Oh":
                    after(act, "dve", "O", step[1])
                    last = copy(qS[:, step[1], :], gateT[:, step[1], 0:SEQ])
                elif kind == "soh":
                    after(act, "dve", "so")
                    last = copy(oS_s[:, :, :], gateT[:, :, SEQ:TOK])
                last.then_inc(done["act"], 1)
                act.wait_ge(done["act"], AT["act"][step])

        @block.vector
        def _(dve):
            own = [0]

            def link(ins):
                own[0] += 1
                ins.then_inc(dve_own, 1)
                dve.wait_ge(dve_own, own[0])

            def tt(out, a, b, op):
                return dve.tensor_tensor(out, a, b, op)

            def low(lo, full, hi):
                return dve.tensor_tensor(lo, full, raw(hi), SUB)

            def rotate(out, src, tables, scratch):
                cos, sin = tables
                m = src.shape[1]
                t1, t2 = (scratch[:, i * m * RH:(i + 1) * m * RH].rearrange("p (m n) -> p m n", n=RH) for i in range(2))
                a, b = src[:, :, 0:RH], src[:, :, RH:ROPE]
                tt(t1, a, cos, MUL)
                link(tt(t2, b, sin, MUL))
                link(tt(out[:, :, 0:RH], t1, t2, SUB))
                tt(t1, b, cos, MUL)
                link(tt(t2, a, sin, MUL))
                return tt(out[:, :, RH:ROPE], t1, t2, ADD)

            dve.wait_ge(consts_in, 16)
            for step in STEPS:
                if "dve" not in parts(step):
                    continue
                kind = step[0]
                if parts(step)[0] != "dve":
                    after(dve, parts(step)[parts(step).index("dve") - 1], *step)
                bank, row = banks(step) if step in BANK_NO else (None, None)
                if kind == "piece":
                    _, name, j = step
                    m = used(name, j)
                    hi, lo = weights(name)
                    c = slice(j * PIECE, j * PIECE + m)
                    last = low(lo[:, c], stage[PIECE_NO[name, j] % NSTAGE][:, 0:m], hi[:, c])
                elif kind == "xn":
                    t = step[1]
                    last = dve.tensor_scalar(rows[:, t, :], rows[:, t, :], S1(("x", t), stat2), None, MUL)
                elif kind in ("xT", "oT"):
                    t = step[-1]
                    c = slice(t * P, (t + 1) * P)
                    last = low(hat[1][:, :, c], row.rearrange("p (k n) -> p k n", n=P), hat[0][:, :, c])
                elif kind == "z":
                    last = dve.tensor_scalar(z_min[:, step[1], :], bank[:, 0, :], 0.0, None, ALU.min)
                elif kind == "lg":
                    after(dve, "act", "ln")
                    t = step[1]
                    last = tt(z_min[:, t, :], z_min[:, t, :], z_abs[:, t, :], SUB)
                elif kind == "lgh":
                    t = step[1]
                    last = low(lg[1][:, t, :], z_min[:, t, :], lg[0][:, t, :])
                elif kind == "q":
                    h = step[1]
                    after(dve, "act", "e", h)
                    if h == 0:
                        after(dve, "act", "const")
                        dve.wait_ge(own_set, 1)
                    after(dve, "pe", "qp", h)
                    v = banks(("qp", h))[0][:, :, 0:HALF]
                    link(dve.scalar_tensor_tensor(tmp[:, :].rearrange("p (a n) -> p a n", a=2), v, DK ** -0.5,
                                                  Ep[:, :].rearrange("p (a n) -> p a n", a=2), MUL, MUL))
                    for b in range(SB):
                        last = dve.tensor_copy(q_own[:, b, b * SL:(b + 1) * SL], tmp[:, SEQ + b * SL:SEQ + (b + 1) * SL])
                elif kind == "k":
                    last = tt(kt[:, :].rearrange("p (a n) -> p a n", a=2), bank[:, :, 0:HALF], Em[:, :].rearrange("p (a n) -> p a n", a=2), MUL)
                elif kind == "qlo":
                    after(dve, "act", "q", step[1])
                    last = low(qT[1][:, :], tmp[:, :], qT[0][:, :])
                elif kind == "klo":
                    after(dve, "act", "k", step[1])
                    last = low(kT[1][:, :], kt[:, :], kT[0][:, :])
                elif kind == "sc":
                    tt(tmp[:, 0:SEQ].rearrange("p (t n) -> p t n", n=P), bank[:, 0, :].rearrange("p (t n) -> p t n", n=P),
                       times(cst("mask_p"), NP), MUL)
                    last = tt(tmp[:, SEQ:TOK], bank[:, 1, 0:P], cst("mask_s"), MUL)
                elif kind == "sclo":
                    after(dve, "act", "sc", step[1])
                    last = low(scT[1][:, :], tmp[:, :], scT[0][:, :])
                elif kind == "v":
                    last = low(vv[1][:, 0:NP, :], row.rearrange("p (t n) -> p t n", n=DV), vv[0][:, 0:NP, :])
                elif kind == "vt":
                    last = low(vv[1][:, step[1], :], bank[:, 0, 0:DV], vv[0][:, step[1], :])
                elif kind == "gl":
                    t = step[1]
                    v = th[:, (t % NP) * DV:(t % NP + 1) * DV]
                    link(dve.scalar_tensor_tensor(v, v, 1.0, bank[:, 0, 0:DV], ADD, MUL))
                    o = rows[:, t, (HA - 1) * DV:HA * DV]
                    last = tt(o, o, v, MUL)
                elif kind == "vs":
                    last = low(vv[1][:, NP, :], v_s[:, :], vv[0][:, NP, :])
                elif kind == "kT":
                    low(kn[1][:, :, :], row[:, 0:TOK].rearrange("p (t n) -> p t n", n=DK), kn[0][:, :, :])
                    last = tt(k_own[:, :, :], times(bank[:, 1, 0:P], SB), over(cst("member"), DK), MUL)
                elif kind == "gt":
                    h = step[1]
                    last = dve.scalar_tensor_tensor(rows[:, 0:NP, h * DV:(h + 1) * DV], th.rearrange("p (t n) -> p t n", n=DV), 1.0,
                                                    row.rearrange("p (t n) -> p t n", n=DV), ADD, MUL)
                elif kind == "gts":
                    h = step[1]
                    last = dve.scalar_tensor_tensor(rows[:, NP, h * DV:(h + 1) * DV], th[:, 0:DV], 1.0, bank[:, 0, 0:DV], ADD, MUL)
                elif kind == "U":
                    if step[1]:
                        dve.wait_ge(final_out, 16 * step[1])
                    for t in range(NP):
                        e_end = Ep[:, t * P + P - 1:t * P + P]
                        u = row[:, t * DV:(t + 1) * DV]
                        nxt = (t + 1) % NP
                        if t:
                            link(tt(st_in[:, 0, :], u, st_in[:, t, :], ADD))
                            u = st_in[:, 0, :]
                        if t < NP - 1:
                            link(dve.tensor_scalar(st_in[:, nxt, :], u, e_end, eB[:, t + 1:t + 2], MUL, MUL))
                        else:
                            last = dve.tensor_scalar(st_in[:, 0, :], u, e_end, None, MUL)
                elif kind == "Slo":
                    after(dve, "act", "U", step[1])
                    last = low(st[1][:, 1:, :], st_in[:, 1:, :], st[0][:, 1:, :])
                elif kind == "Us":
                    _, h, j = step
                    dve.wait_ge(state_in, 16 * (h + 1))
                    v = st_s[:, 4 * j:4 * j + 4, :]
                    link(tt(v, row.rearrange("p (b n) -> p b n", n=DV), v, ADD))
                    for b in range(4 * j, 4 * j + 4):
                        e = Ep[:, SEQ + b * SL + SL - 1:SEQ + (b + 1) * SL]
                        last = dve.tensor_scalar(st_s[:, b, :], st_s[:, b, :], e, None, MUL)
                elif kind in ("o", "os"):
                    h = step[1]
                    for i, t in enumerate(range(NP) if kind == "o" else [NP]):
                        v = rows[:, t, h * DV:(h + 1) * DV]
                        o = row[:, i * DV:(i + 1) * DV]
                        last = (dve.scalar_tensor_tensor(v, o, S1(("o", h), stat2, t), v, MUL, MUL) if h + 1 < HA
                                else dve.tensor_scalar(v, o, S1(("o", h), stat2, t), None, MUL))
                elif kind in ("y", "ys"):
                    _, ph, s = step
                    t = slice(0, NP) if kind == "y" else slice(NP, NT)
                    m = NP if kind == "y" else 1
                    y = rows if ph == "A" else y_rows
                    dve.wait_ge(post_in, 32 if ph == "A" else 48)
                    last = tt(y[:, t, s * 256:(s + 1) * 256], row[:, 0:m * 256].rearrange("p (t n) -> p t n", n=256),
                              times(post[:, s * 256:(s + 1) * 256], m), MUL)
                elif kind == "r":
                    _, ph, t = step
                    dve.wait_ge(rest_in, 32 if ph == "A" else 48)
                    r = S1(("yr", ph, t), stat2)
                    y, x = (rows, x1) if ph == "A" else (y_rows, xB)
                    yb, _row = banks(("yt", ph, t))
                    link(dve.scalar_tensor_tensor(y[:, t, 768:D], yb[:, 0, 0:256], r, post[:, 768:D], MUL, MUL))
                    dve.scalar_tensor_tensor(x[:, t, 0:768], y[:, t, 0:768], r, x[:, t, 0:768], MUL, ADD)
                    last = tt(x[:, t, 768:D], y[:, t, 768:D], x[:, t, 768:D], ADD)
                elif kind == "rx":
                    t = step[1]
                    last = dve.tensor_scalar(rows[:, t, :], x1[:, t, :], S1(("x1", t), stat2), None, MUL)
                elif kind == "lc":
                    if step[1] == 0:
                        dve.wait_ge(state_out, 16 * HA)
                        dve.wait_ge(final_out, 16 * HA)
                    last = dve.tensor_copy(ckvn[:, step[1], :], bank[:, 0, 0:KL])
                elif kind == "lcn":
                    for t in range(NT):
                        last = dve.scalar_tensor_tensor(ckvn[:, t, :], ckvn[:, t, :], S1(("lat",), stat2, t), lat_gain[:, :], MUL, MUL)
                elif kind == "cn":
                    last = low(cn_s[1][:, :], ckvn[:, NP, :], cn_s[0][:, :])
                elif kind == "cT":
                    t = step[1]
                    c = slice(t * P, (t + 1) * P)
                    low(cT[1][:, :, c], bank[:, 0, 0:KL].rearrange("p (k n) -> p k n", n=P), cT[0][:, :, c])
                    last = low(krL[:, c], bank[0:ROPE, 1, 0:P], krS[0:ROPE, c])
                elif kind in ("qa", "qas", "kq", "kqs"):
                    t = slice(NP, NT) if kind[-1] == "s" else slice(0, NP)
                    n = t.stop - t.start
                    v = row[:, 0:n * 256].rearrange("p (t n) -> p t n", n=256)
                    if kind[0] == "q":
                        last = dve.tensor_copy(qln[:, t, 0:256], v)
                    else:
                        link(rotate(krn[:, t, :], v[:, :, 0:ROPE],
                                    [cst(c).rearrange("p (t n) -> p t n", n=RH)[:, t, :] for c in ("cos", "sin")], thb))
                        last = dve.tensor_copy(qln[:, t, 256:QL], v[:, :, ROPE:ROPE + QL - 256])
                elif kind == "qs":
                    for t in range(NT):
                        last = dve.tensor_scalar(qln[:, t, :], qln[:, t, :], S1(("qa",), stat2, t), None, MUL)
                elif kind == "qT":
                    t = step[1]
                    c = slice(t * P, (t + 1) * P)
                    last = low(qlT[1][:, :, c], bank[:, 0, 0:QL].rearrange("p (k n) -> p k n", n=P), qlT[0][:, :, c])
                elif kind == "gb":
                    _, s, j = step
                    last = dve.scalar_tensor_tensor(gateT[:, 2 * s + j, :].rearrange("p (a n) -> p a n", a=2),
                                                    thb[:, :].rearrange("p (a n) -> p a n", a=2),
                                                    1.0, bank[:, :, 0:HALF], ADD, MUL)
                elif kind == "qr":
                    t = step[1]
                    if t > 1:
                        after(dve, "pe", "qrT", t - 2)
                    elif t == 0:
                        dve.wait_ge(latent_out, 16 * 4)
                        after(dve, "pe", "cT", NT - 1)
                    v = bank[:, 0, :].rearrange("p (h n) -> p h n", n=ROPE)
                    tables = [times(cst(n)[:, t * RH:(t + 1) * RH], HB) for n in ("cos", "sin")]
                    last = rotate(qrn[t % 2][:, :].rearrange("p (h n) -> p h n", n=ROPE), v, tables, rtmp)
                elif kind == "qrT":
                    t = step[1]
                    last = low(rotary_to(t, slice(ROPE, P)), rotary_from(row, t), rotary_to(t, slice(0, ROPE)))
                elif kind == "qn":
                    last = low(qN[1][:, :], bank[:, 0, :], qN[0][:, :])
                elif kind == "qns":
                    last = low(qN_s[1][:, :], bank[:, 0, 0:2 * P], qN_s[0][:, :])
                elif kind == "kh":
                    last = low(kN[1][:, :], bank[:, 0, :], kN[0][:, :])
                elif kind == "vh":
                    last = low(vN[1][:, :, :], row.rearrange("p (t n) -> p t n", n=2 * VB), vN[0][:, :, :])
                elif kind == "qabs":
                    for i in range(2):
                        hi, lo = (by_stream(x[:, :, :, :], 2 * step[1] + i) for x in qab)
                        last = low(lo, bank[:, 0, i * KL:(i + 1) * KL].rearrange("p (k b n) -> p k b n", k=KC, n=SL), hi)
                elif kind == "S":
                    _, h, u = step
                    for j, i in enumerate(UNITS[u]):
                        ins = dve.reduce_max(S1(("S", h, u), t=j), bank[:, j, 0:(i + 1) * P], AX.X)
                    link(ins)
                    last = dve.tensor_scalar(S1(("S", h, u), stat2), S1(("S", h, u)), -SCALE, None, MUL)
                elif kind == "T":
                    last = low(pT[step[2]][1][:, :], row[:, 0:TOK], pT[step[2]][0][:, :])
                elif kind == "N":
                    _, h, u = step
                    after(dve, "act", "S", h, u)
                    r = S1(("S", h, u), stat2)
                    link(dve.reciprocal(r, S1(("S", h, u))))
                    for j, (i, c0) in enumerate(zip(UNITS[u], (0, UNITS[u][0] + 1))):
                        v = prob[u][:, c0:c0 + i + 1, :]
                        last = dve.tensor_scalar(v, v, r[:, j:j + 1], 0.5, MUL, MUL)
                elif kind == "O":
                    v = gateT[:, step[1], 0:SEQ]
                    last = tt(v, bank[:, 0, :], v, MUL)
                elif kind == "Oh":
                    h = step[1]
                    last = low(oT_lo[:, h, 0:SEQ], gateT[:, h, 0:SEQ], qS[:, h, :])
                elif kind == "ct":
                    last = low(sT[1][:, :, :], bank[:, :, :], sT[0][:, :, :])
                elif kind == "cr":
                    last = low(skL[:, :], bank[0:ROPE, 0, :], skS[0:ROPE, :])
                elif kind == "ss":
                    b = step[1]
                    link(dve.reduce_max(S1(("ss", b)), row[:, 0:TOK], AX.X))
                    last = dve.tensor_scalar(S1(("ss", b), stat2), S1(("ss", b)), -SCALE, None, MUL)
                elif kind == "st":
                    last = low(spT[1][:, :], row[:, 0:TOK], spT[0][:, :])
                elif kind == "sv":
                    b = step[1]
                    after(dve, "act", "ss", b)
                    r = S1(("ss", b), stat2)
                    link(dve.reciprocal(r, S1(("ss", b))))
                    last = dve.tensor_scalar(ctxn[:, :], bank[:, 0, 0:KL], r, 0.5, MUL, MUL)
                elif kind == "cx":
                    last = low(qab[1][:, :, step[1], :], bank[:, 0, 0:KL].rearrange("p (k n) -> p k n", n=P), qab[0][:, :, step[1], :])
                elif kind == "so":
                    v = gateT[:, :, SEQ:TOK]
                    last = tt(v, row.rearrange("p (h n) -> p h n", n=P), v, MUL)
                elif kind == "soh":
                    last = low(oT_lo[:, :, SEQ:TOK], gateT[:, :, SEQ:TOK], oS_s[:, :, :])
                last.then_inc(done["dve"], 1)
                dve.wait_ge(done["dve"], AT["dve"][step])

        @block.tensor
        def _(pe):
            def mm3(out, a, b, first, last):
                pe.matmul(out, a[0], b[0], start=first, stop=False)
                pe.matmul(out, a[0], b[1], start=False, stop=False)
                return pe.matmul(out, a[1], b[0], start=False, stop=last)

            def cut(pair_, *idx):
                return tuple(x[idx] for x in pair_)

            A_ = slice(None)

            def natural(row, name, tiles, cols, kts, src):
                w = [x[:, :].rearrange("p (j m) -> p j m", m=PIECE)[:, :, 0:4 * cols].rearrange("p j (k n) -> p j k n", n=cols) for x in weights(name)]
                for i, t in enumerate(tiles):
                    for k in range(kts):
                        if not src and (t, k) in ((0, HB - 1), (NP, 0)):
                            after(pe, "dve", *(("Oh", HB - 1) if t < NP else ("soh",)))
                        last = mm3(row[:, i * 256:i * 256 + cols], cut(src, A_, k, slice(t * P, (t + 1) * P)) if src else outT(k, t),
                                   cut(w, A_, k // 4, k % 4), k == 0, k == kts - 1)
                return last

            def outT(k, t):
                return qS[:, k, t * P:(t + 1) * P] if t < NP else oS_s[:, k, :], oT_lo[:, k, t * P:(t + 1) * P]

            def ready(name):
                after(pe, "dve", "piece", name, len(SLABS[name]) - 1)

            for step in STEPS:
                if "pe" not in parts(step):
                    continue
                kind = step[0]
                bank, row = before_bank(pe, step)
                if kind in ("xT", "oT"):
                    t = step[-1]
                    if kind == "oT":
                        after(pe, "dve", "gl", t)
                    else:
                        after(pe, "dve", *(("xn", t) if step[1] == "A" else ("rx", t)))
                    for k in range(KD):
                        last = pe.transpose(row[:, k * P:(k + 1) * P], rows[:, t, k * P:(k + 1) * P], ident)
                elif kind == "glr":
                    ready("glr")
                    after(pe, "dve", "xT", "A", NT - 1)
                    w = [x[:, 0:KD * RANK].rearrange("p (k n) -> p k n", n=RANK) for x in weights("glr")]
                    for a in range(2):
                        for k in range(KD):
                            last = mm3(bank[0:RANK, a, 0:HALF], cut(w, A_, k), cut(hat, A_, k, slice(a * HALF, (a + 1) * HALF)), k == 0, k == KD - 1)
                elif kind == "z":
                    t = step[1]
                    after(pe, "act", "glr")
                    pe.wait_ge(gate_in, 32)
                    last = pe.matmul(bank[:, 0, :], glrT[:, t * P:(t + 1) * P], gate_w[:, :], start=True, stop=True)
                elif kind == "c":
                    t = step[1]
                    after(pe, "dve", "lgh", t)
                    after(pe, "act", "const")
                    m = cst_r("cum_p" if t < NP else "cum_s")
                    for h in range(HA):
                        o = bank[:, h // 2, (h % 2) * (P + 2):(h % 2 + 1) * (P + 2)]
                        pe.matmul(o, lg[0][:, t, h * DK:(h + 1) * DK], m, start=True, stop=False)
                        last = pe.matmul(o, lg[1][:, t, h * DK:(h + 1) * DK], m, start=False, stop=True)
                elif kind in ("qp", "k"):
                    h = step[1]
                    after(pe, "dve", "piece", ("qk", h), 0 if kind == "qp" else 1)
                    off = 0 if kind == "qp" else PIECE
                    w = [x[:, off:off + KD * DK].rearrange("p (k n) -> p k n", n=DK) for x in weights(("qk", h))]
                    for a in range(2):
                        for k in range(KD):
                            last = mm3(bank[:, a, 0:HALF], cut(w, A_, k), cut(hat, A_, k, slice(a * HALF, (a + 1) * HALF)), k == 0, k == KD - 1)
                elif kind in ("vt", "gl"):
                    t = step[1]
                    name = ("v", 0) if kind == "vt" else ("g", HA - 1)
                    ready(name)
                    if kind == "vt":
                        after(pe, "dve", "xT", "A", t)
                    last = natural(row, name, [t], DV, KD, hat)
                elif kind in ("v", "vs", "gt", "gts"):
                    name = ("v" if kind[0] == "v" else "g", step[1])
                    ready(name)
                    last = natural(row, name, [NP] if kind[-1] == "s" else range(NP), DV, KD, hat)
                elif kind == "kT":
                    after(pe, "dve", "k", step[1])
                    for t in range(NT):
                        last = pe.transpose(row[:, t * P:(t + 1) * P], kt[:, t * P:(t + 1) * P], ident)
                elif kind == "sc":
                    h = step[1]
                    after(pe, "dve", "klo", h)
                    for t in range(NT):
                        c = slice(t * P, (t + 1) * P)
                        last = mm3(row[:, c], cut(kT, A_, c), cut(qT, A_, c), True, True)
                elif kind == "U":
                    after(pe, "dve", *(("v", step[1]) if step[1] else ("vt", NT - 1)))
                    after(pe, "dve", "kT", step[1])
                    for t in range(NP):
                        last = mm3(row[:, t * DV:(t + 1) * DV], cut(kn, A_, t), cut(vv, A_, t), True, True)
                elif kind == "Us":
                    _, h, j = step
                    after(pe, "act", *(("vs", h) if h else ("vt", NT - 1)))
                    for b in range(4):
                        last = pe.matmul(row[:, b * DV:(b + 1) * DV], k_own[:, 4 * j + b, :], v_s[:, :], start=True, stop=True)
                elif kind == "o":
                    h = step[1]
                    after(pe, "dve", "sclo", h)
                    after(pe, "dve", "Slo", h)
                    for t in range(NP):
                        c = slice(t * P, (t + 1) * P)
                        o = row[:, t * DV:(t + 1) * DV]
                        last = mm3(o, cut(scT, A_, c), cut(vv, A_, t), True, t == 0)
                        if t:
                            last = mm3(o, cut(qT, A_, c), cut(st, A_, t), False, True)
                elif kind == "os":
                    h = step[1]
                    pe.wait_ge(state_in, 16 * (h + 1))
                    for b in range(SB):
                        pe.matmul(row[:, 0:DV], q_own[:, b, :], st_s[:, b, :], start=b == 0, stop=False)
                    after(pe, "dve", "sclo", h)
                    after(pe, "dve", *(("vs", h) if h else ("vt", NT - 1)))
                    last = mm3(row[:, 0:DV], cut(scT, A_, slice(SEQ, TOK)), cut(vv, A_, NP), False, True)
                elif kind in ("y", "ys"):
                    _, ph, s = step
                    ready(("wo", ph, s))
                    after(pe, "dve", *(("oT", NP - 1 if kind == "y" else NP) if ph == "A" else ("Oh", HB - 2)))
                    last = natural(row, ("wo", ph, s), range(NP) if kind == "y" else [NP], 256, KD, hat if ph == "A" else None)
                elif kind == "yt":
                    _, ph, t = step
                    ready(("wo", ph, 3))
                    last = natural(row, ("wo", ph, 3), [t], 256, KD, hat if ph == "A" else None)
                elif kind == "lc":
                    ready("kvc")
                    after(pe, "dve", "xT", "B", step[1])
                    last = natural(row, "kvc", [step[1]], KL, KD, hat)
                elif kind == "cT":
                    t = step[1]
                    after(pe, "dve", "kqs")
                    for c in range(KC):
                        pe.transpose(bank[:, 0, c * P:(c + 1) * P], ckvn[:, t, c * P:(c + 1) * P], ident)
                    last = pe.transpose(bank[0:ROPE, 1, 0:P], krn[:, t, :], ident)
                elif kind in ("qa", "qas"):
                    ready("ql0")
                    last = natural(row, "ql0", range(NP) if kind == "qa" else [NP], 256, KD, hat)
                elif kind in ("kq", "kqs"):
                    ready("kq")
                    last = natural(row, "kq", [NP] if kind == "kqs" else range(NP), ROPE + QL - 256, KD, hat)
                elif kind == "qT":
                    t = step[1]
                    after(pe, "dve", "qs")
                    for k in range(KQ):
                        last = pe.transpose(bank[:, 0, k * P:(k + 1) * P], qln[:, t, k * P:(k + 1) * P], ident)
                elif kind == "gb":
                    _, s, j = step
                    ready(("gb", s))
                    w = [x[:, :].rearrange("p (k n) -> p k n", n=256) for x in weights(("gb", s))]
                    for a in range(2):
                        for k in range(KD):
                            last = mm3(bank[:, a, 0:HALF], cut(w, A_, k, slice(j * P, (j + 1) * P)), cut(hat, A_, k, slice(a * HALF, (a + 1) * HALF)), k == 0, k == KD - 1)
                elif kind == "qr":
                    t = step[1]
                    ready("uqr")
                    after(pe, "dve", "qT", NT - 1)
                    for g in range(2):
                        w = [x[:, g * PIECE:g * PIECE + KQ * 256].rearrange("p (k n) -> p k n", n=256) for x in weights("uqr")]
                        for k in range(KQ):
                            last = mm3(bank[:, 0, g * 256:(g + 1) * 256], cut(qlT, A_, k, slice(t * P, (t + 1) * P)), cut(w, A_, k), k == 0, k == KQ - 1)
                elif kind == "qrT":
                    t = step[1]
                    after(pe, "dve", "qr", t)
                    for h in range(HB):
                        last = pe.transpose(row[0:ROPE, h * P:(h + 1) * P], qrn[t % 2][:, h * ROPE:(h + 1) * ROPE], ident)
                elif kind == "qn":
                    h = step[1]
                    ready(("hd", h))
                    w = [x[:, 0:KQ * NOPE].rearrange("p (k n) -> p k n", n=NOPE) for x in weights(("hd", h))]
                    for k in range(KQ):
                        last = mm3(bank[:, 0, :], cut(w, A_, k), cut(qlT, A_, k, slice(0, SEQ)), k == 0, k == KQ - 1)
                elif kind == "qns":
                    ready(("pre", step[1]))
                    for i in range(2):
                        w = [x[:, i * PIECE:i * PIECE + KQ * NOPE].rearrange("p (k n) -> p k n", n=NOPE) for x in weights(("pre", step[1]))]
                        for k in range(KQ):
                            last = mm3(bank[:, 0, i * P:(i + 1) * P], cut(w, A_, k), cut(qlT, A_, k, slice(SEQ, TOK)), k == 0, k == KQ - 1)
                elif kind == "wt":
                    for j, x in enumerate(weights(("pre", step[1]))):
                        for i in range(2):
                            for c in range(KC):
                                at = i * PIECE + KQ * NOPE + c * NOPE
                                last = pe.transpose(bank[:, j, (i * KC + c) * P:(i * KC + c + 1) * P], raw(x[:, at:at + NOPE]), ident)
                elif kind == "kh":
                    h = step[1]
                    w = [x[:, KQ * NOPE:(KQ + KC) * NOPE].rearrange("p (k n) -> p k n", n=P) for x in weights(("hd", h))]
                    for c in range(KC):
                        last = mm3(bank[:, 0, :], cut(w, A_, c), cut(cT, A_, c, slice(0, SEQ)), c == 0, c == KC - 1)
                elif kind == "vh":
                    w = [cut(weights(("hd", 2 * step[1] + c)), A_, slice((KQ + KC) * NOPE, (KQ + KC) * NOPE + 2 * VB)) for c in range(KC)]
                    ready(("hd", 2 * step[1] + 1))
                    for t in range(NP):
                        for c in range(KC):
                            last = mm3(row[:, t * 2 * VB:(t + 1) * 2 * VB], cut(cT, A_, c, slice(t * P, (t + 1) * P)), w[c], c == 0, c == KC - 1)
                elif kind == "qabs":
                    after(pe, "act", "wt", step[1])
                    after(pe, "dve", "qns", step[1])
                    for i in range(2):
                        for c in range(KC):
                            j = (i * KC + c) * P
                            last = mm3(bank[:, 0, j:j + P], cut(wT, A_, slice(j, j + P)), cut(qN_s, A_, slice(i * P, (i + 1) * P)), True, True)
                elif kind == "S":
                    _, h, u = step
                    after(pe, "dve", "qn", h)
                    after(pe, "dve", "kh", h)
                    after(pe, "dve", "qrT", NT - 1)
                    for j, i in enumerate(UNITS[u]):
                        q, keys = slice(i * P, (i + 1) * P), slice(0, (i + 1) * P)
                        o = bank[:, j, keys]
                        mm3(o, cut(qN, A_, q), cut(kN, A_, keys), True, False)
                        pe.matmul(o, qS[:, h, q], krS[:, keys], start=False, stop=False)
                        pe.matmul(o, qS[0:ROPE, h, q], krL[:, keys], start=False, stop=False)
                        last = pe.matmul(bank[:, j, q], cst_r("early", 1), cst_r("late", 1), start=False, stop=True)
                elif kind == "T":
                    _, h, u = step
                    after(pe, "dve", "N", h, 1)
                    for n, (s, i) in enumerate((s, i) for s in KEY_UNITS[u] for i in range(s, NP)):
                        v = [x for x in range(2) if i in UNITS[x]][0]
                        at = s + (0 if UNITS[v][0] == i else UNITS[v][0] + 1)
                        last = pe.transpose(row[:, n * P:(n + 1) * P], prob[v][:, at, :], ident)
                elif kind == "O":
                    h = step[1]
                    after(pe, "dve", "T", h, 1)
                    after(pe, "dve", "vh", h // 2)
                    for s, u, at in ((s, u, n * (NP - KEY_UNITS[u][0]) * P) for u in range(2) for n, s in enumerate(KEY_UNITS[u])):
                        last = mm3(bank[:, 0, s * P:SEQ], cut(vN, A_, s, slice((h % 2) * VB, (h % 2 + 1) * VB)),
                                   cut(pT[u], A_, slice(at, at + (NP - s) * P)), s == 0, (u, s) == (1, KEY_UNITS[1][-1]))
                elif kind == "ct":
                    b = step[1]
                    pe.wait_ge(cache_in[b % 2], 32 * (b // 2 + 1))
                    for c in range(KC):
                        for s in range(PAST // P):
                            last = pe.transpose(bank[:, c, s * P:(s + 1) * P], craw[b % 2][:, s, c * P:(c + 1) * P], ident)
                elif kind == "cr":
                    b = step[1]
                    for s in range(PAST // P):
                        last = pe.transpose(bank[0:ROPE, 0, s * P:(s + 1) * P], kraw[b % 2][:, s, :], ident)
                elif kind == "ss":
                    b = step[1]
                    after(pe, "dve", "cr", b)
                    after(pe, "dve", "qabs", HB // 2 - 1)
                    for o, keys, kr, kl in ((bank[:, 0, :], sT, skS[:, :], skL[:, :]),
                                            (bank[:, 1, 0:P], cut(cT, A_, A_, slice(SEQ, TOK)), krS[:, SEQ:TOK], krL[:, SEQ:TOK])):
                        for c in range(KC):
                            mm3(o, cut(qab, A_, c, b), cut(keys, A_, c), c == 0, False)
                        q = qS_s[:, b, :, :].rearrange("p h n -> p (h n)")
                        pe.matmul(o, q, kr, start=False, stop=False)
                        last = pe.matmul(o, q[0:ROPE, :], kl, start=False, stop=keys is sT)
                    a, _b = CONST_R["others"]
                    at = a + P - b * SL
                    last = pe.matmul(bank[:, 1, 0:P], cst_r("ones", 1), const_r[0:1, at:at + P], start=False, stop=True)
                elif kind == "st":
                    b = step[1]
                    after(pe, "act", "ss", b)
                    for s in range(NT):
                        last = pe.transpose(row[:, s * P:(s + 1) * P], sprob[:, s, :], ident)
                elif kind == "sv":
                    b = step[1]
                    after(pe, "dve", "st", b)
                    after(pe, "pool", "cs", b)
                    after(pe, "dve", "cn")
                    for s in range(NT):
                        last = mm3(bank[:, 0, 0:KL], cut(spT, A_, slice(s * P, (s + 1) * P)), cut(cn, A_, s) if s < NT - 1 else cut(cn_s, A_, A_), s == 0, s == NT - 1)
                elif kind == "cx":
                    after(pe, "dve", "sv", step[1])
                    for c in range(KC):
                        last = pe.transpose(bank[:, 0, c * P:(c + 1) * P], ctxn[:, c * P:(c + 1) * P], ident)
                elif kind == "so":
                    ready("uv")
                    after(pe, "dve", "cx", SB - 1)
                    w = [x[:, :].rearrange("p (k n) -> p k n", n=HB * VB) for x in weights("uv")]
                    for h in range(HB):
                        for c in range(KC):
                            ctx_h = [x[:, c, :, h * SL:(h + 1) * SL] for x in qab]
                            last = mm3(row[:, h * P:(h + 1) * P].rearrange("p (b n) -> p b n", n=SL), cut(w, A_, c, slice(h * VB, (h + 1) * VB)), ctx_h, c == 0, c == KC - 1)
                last.then_inc(done["pe"], 1)


_INS = ["x_prompt", "x_sample", "state_gla", "cache_ckv", "cache_krope", "a_norm_pre", "a_w_in", "a_w_gate2", "a_b_gate",
        "a_head_norm", "a_w_out", "a_norm_post", "kv_norm", "kv_w_down", "kv_latent_norm", "kv_w_uk", "kv_w_uv",
        "b_norm_pre", "b_w_in", "b_q_norm", "b_w_uq", "b_w_out", "b_norm_post"]
_GAINS = ["a_norm_pre", "a_head_norm", "kv_norm", "b_norm_pre", "b_q_norm"]
_OUTS = [(1, SEQ, D), (SB, SL, D), (1, 1, HA, DK, DV), (1, SB, HA, DK, DV), (1, SEQ, KL), (1, SEQ, ROPE), (SB, SL, KL), (SB, SL, ROPE)]


def constants():
    import numpy as np
    i = np.arange(P)
    before = (i[:, None] <= i[None, :]).astype(np.float32)
    same = (i[:, None] // SL == i[None, :] // SL).astype(np.float32)
    half = (i < P // 2).astype(np.float32)[:, None]
    tau = np.float32(1.0 / 16.0)
    cum_p = np.zeros((P, P + 2), np.float32)
    cum_p[:, :P] = (before - half) * tau
    cum_p[:, P:P + 1] = half * tau
    cum_s = np.zeros((P, P + 2), np.float32)
    cum_s[:, :P] = before * same * tau
    pos = np.concatenate([np.arange(SEQ), PAST + np.arange(P) % SL]).astype(np.float32)
    inv = np.power(np.float32(10000.0), -np.arange(RH, dtype=np.float32) / np.float32(RH)).astype(np.float32)
    ang = (pos[:, None] * inv[None, :]).reshape(NT, P, RH).transpose(1, 0, 2).reshape(P, NT * RH)
    row = np.ones((P, 1), np.float32)
    others = np.full(2 * P, NEG, np.float32)
    others[P:P + SL] = 0.0
    const = [np.eye(P), before, before * same, (i[:, None] // SL == np.arange(SB)[None, :]), np.cos(ang), np.sin(ang)]
    const_r = [cum_p, cum_s, row * (1 - half.T * 0 - (i >= P // 2)[None, :]), row * np.where(i >= P // 2, NEG, 0.0)[None, :], row * np.ones((1, P)), row * others[None, :]]
    return [np.ascontiguousarray(np.concatenate(x, axis=1).astype(np.float32)) for x in (const, const_r)]


def kernel(**inputs):
    import numpy as _np
    import concourse.bacc as _bacc
    from concourse import mybir as _mybir
    from concourse.bass_utils import run_bass_kernel_spmd as _run

    nc = _bacc.Bacc("TRN2", target_bir_lowering=False, num_devices=1)
    arrays, dram = {}, {}
    data = {name: _np.ascontiguousarray(inputs[name]) for name in _INS}
    data["const"], data["const_r"] = constants()
    for name in _GAINS:
        data[name] = _np.ascontiguousarray(data[name].reshape(-1, P).T)
    for name, a in data.items():
        arrays[f"in_{name}_dram"] = a
        dram[name] = nc.dram_tensor(f"in_{name}_dram", a.shape, _mybir.dt.from_np(a.dtype), kind="ExternalInput").ap()
    outs = [nc.dram_tensor(f"out_{i}_dram", shape, _mybir.dt.float32, kind="ExternalOutput").ap() for i, shape in enumerate(_OUTS)]
    program(nc, dram, outs)
    r = _run(nc, [arrays], core_ids=[0])
    return tuple(r.results[0][f"out_{i}_dram"] for i in range(len(_OUTS)))
```
